# Optimizing a Trainium2 kernel written in Bass

```python
import math
import jax, jax.numpy as jnp
from jax import lax
import numpy as np

D_MODEL = 1024
BATCH = 1
SEQ = 256
DEPTH = 1

CHUNK = 64
LEFT_CHUNKS = 8
BAND = LEFT_CHUNKS + 1
ATTN_HEADS = 8
HEAD_DIM = 64
ATTN_WIDTH = ATTN_HEADS * HEAD_DIM
REL_MAX = 256
REL_SIZE = (CHUNK - 1) + REL_MAX + 1
SSM_WIDTH = D_MODEL // 2
SSM_GROUP = 16
SSM_GROUPS = SSM_WIDTH // SSM_GROUP
SSM_STATE = 64
DT_MIN = 0.001
DT_MAX = 0.1
N_BRANCHES = 2
IN_WIDTH = 3 * ATTN_WIDTH + SSM_WIDTH + N_BRANCHES * D_MODEL
N_EXPERTS = 32
TOP_K = 4
D_EXPERT = D_MODEL
SWIGLU_LIMIT = 7.0
SWIGLU_ALPHA = 1.702
EXPERT_BLOCK = 256
LN_EPS = 1e-5
DEEPNORM_ALPHA = (2 * DEPTH) ** 0.25
DEEPNORM_BETA = (8 * DEPTH) ** -0.25
NEG_INF = -1e30

kernel_name = "streaming_hybrid_relattn_s5_moe"

def layer_norm(x, g, b):
    xf = x.astype(jnp.float32)
    mu = jnp.mean(xf, axis=-1, keepdims=True)
    var = jnp.mean(jnp.square(xf - mu), axis=-1, keepdims=True)
    y = (xf - mu) * lax.rsqrt(var + LN_EPS) * g.astype(jnp.float32) + b.astype(jnp.float32)
    return y.astype(x.dtype)

def chunked_rel_attention(q, k, v, rel_bias):
    bsz, s, _ = q.shape
    nc = s // CHUNK
    shp = (bsz, nc, CHUNK, ATTN_HEADS, HEAD_DIM)
    q = q.reshape(shp) * (HEAD_DIM ** -0.5)
    k = k.reshape(shp)
    v = v.reshape(shp)
    pad = ((0, 0), (LEFT_CHUNKS, 0), (0, 0), (0, 0), (0, 0))
    k_pad = jnp.pad(k, pad)
    v_pad = jnp.pad(v, pad)
    k_band = jnp.concatenate([k_pad[:, j:j + nc] for j in range(BAND)], axis=2)
    v_band = jnp.concatenate([v_pad[:, j:j + nc] for j in range(BAND)], axis=2)
    qc = jnp.arange(CHUNK)[:, None]
    kk = jnp.arange(BAND * CHUNK)[None, :]
    dist = qc - (kk - LEFT_CHUNKS * CHUNK)
    idx = jnp.clip(dist, -(CHUNK - 1), REL_MAX) + (CHUNK - 1)
    bias = rel_bias.astype(jnp.float32)[:, idx]
    key_chunk = jnp.arange(nc)[:, None] - LEFT_CHUNKS + jnp.arange(BAND * CHUNK)[None, :] // CHUNK
    valid = key_chunk >= 0
    scores = jnp.einsum('bnqhd,bnkhd->bnhqk', q, k_band,
                        preferred_element_type=jnp.float32) + bias[None, None]
    scores = jnp.where(valid[None, :, None, None, :], scores, NEG_INF)
    p = jax.nn.softmax(scores, axis=-1).astype(v.dtype)
    o = jnp.einsum('bnhqk,bnkhd->bnqhd', p, v_band)
    return o.reshape(bsz, s, ATTN_WIDTH)

def s5_ssm(u, lam_re, lam_im, log_dt, b_re, b_im, c_re, c_im, d_skip):
    bsz, s, _ = u.shape
    f32 = jnp.float32
    uf = u.astype(f32).reshape(bsz, s, SSM_GROUPS, SSM_GROUP)
    lam = lax.complex(lam_re.astype(f32), lam_im.astype(f32))
    dt = jnp.exp(log_dt.astype(f32))[:, None]
    lam_bar = jnp.exp(lam * dt)
    b_mat = lax.complex(b_re.astype(f32), b_im.astype(f32))
    b_bar = ((lam_bar - 1.0) / lam)[..., None] * b_mat
    c_mat = lax.complex(c_re.astype(f32), c_im.astype(f32))
    bu = jnp.einsum('bsgc,gpc->bsgp', uf.astype(jnp.complex64), b_bar)
    a = jnp.broadcast_to(lam_bar, bu.shape)

    def combine(e1, e2):
        a1, x1 = e1
        a2, x2 = e2
        return a1 * a2, a2 * x1 + x2

    _, states = lax.associative_scan(combine, (a, bu), axis=1)
    y = jnp.einsum('bsgp,gcp->bsgc', states, c_mat).real
    y = y + d_skip.astype(f32).reshape(SSM_GROUPS, SSM_GROUP) * uf
    return y.reshape(bsz, s, SSM_WIDTH).astype(u.dtype)

def moe_ffn(h, router_w, router_b, w_gate_up, b_gate_up, w_down, b_down):
    bsz, s, d = h.shape
    t = bsz * s
    hf = h.reshape(t, d)
    logits = (hf @ router_w + router_b).astype(jnp.float32)
    top_vals, top_idx = lax.top_k(logits, TOP_K)
    gates = jax.nn.softmax(top_vals, axis=-1)
    n_assign = t * TOP_K
    flat_e = top_idx.reshape(-1)
    flat_tok = jnp.repeat(jnp.arange(t, dtype=jnp.int32), TOP_K)
    flat_g = gates.reshape(-1)
    order = jnp.argsort(flat_e)
    sorted_e = flat_e[order]
    counts = jnp.bincount(flat_e, length=N_EXPERTS)
    starts = jnp.cumsum(counts) - counts
    padded = ((counts + EXPERT_BLOCK - 1) // EXPERT_BLOCK) * EXPERT_BLOCK
    pends = jnp.cumsum(padded)
    pstarts = pends - padded
    rank = jnp.arange(n_assign) - starts[sorted_e]
    dest = pstarts[sorted_e] + rank
    n_rows = ((n_assign + N_EXPERTS * EXPERT_BLOCK + EXPERT_BLOCK - 1) // EXPERT_BLOCK) * EXPERT_BLOCK
    n_blocks = n_rows // EXPERT_BLOCK
    tok_pad = jnp.full((n_rows,), t, jnp.int32).at[dest].set(flat_tok[order])
    gate_pad = jnp.zeros((n_rows,), jnp.float32).at[dest].set(flat_g[order])
    blk_start = jnp.arange(n_blocks) * EXPERT_BLOCK
    blk_expert = jnp.minimum(jnp.searchsorted(pends, blk_start, side='right'), N_EXPERTS - 1)
    x_tok = jnp.concatenate([hf, jnp.zeros((1, d), hf.dtype)], axis=0)
    xb = x_tok[tok_pad].reshape(n_blocks, EXPERT_BLOCK, d)

    def expert_block(args):
        xblk, e = args
        gu = xblk @ w_gate_up[e] + b_gate_up[e]
        x_glu, x_lin = jnp.split(gu, 2, axis=-1)
        x_glu = jnp.minimum(x_glu, SWIGLU_LIMIT)
        x_lin = jnp.clip(x_lin, -SWIGLU_LIMIT, SWIGLU_LIMIT)
        act = x_glu * jax.nn.sigmoid(SWIGLU_ALPHA * x_glu) * (x_lin + 1.0)
        return act @ w_down[e] + b_down[e]

    yb = lax.map(expert_block, (xb, blk_expert)).reshape(n_rows, d)
    y = jnp.zeros((t + 1, d), yb.dtype).at[tok_pad].add(yb * gate_pad[:, None].astype(yb.dtype))
    return y[:t].reshape(bsz, s, d)

def setup_inputs(seed: int = 0) -> dict:
    key = jax.random.key(seed)
    ks = jax.random.split(key, 32)
    f32 = jnp.float32

    def nrm(k, shape, scale):
        return jax.random.normal(k, shape, f32) * scale

    L, D, E = DEPTH, D_MODEL, N_EXPERTS
    G, P, Hg = SSM_GROUPS, SSM_STATE, SSM_GROUP
    lam_im0 = jnp.pi * jnp.arange(P, dtype=f32)
    return {
        'x': nrm(ks[0], (BATCH, SEQ, D), 1.0),
        'ln_in_g': 1.0 + nrm(ks[1], (D,), 0.02),
        'ln_in_b': nrm(ks[2], (D,), 0.02),
        'w_in': nrm(ks[3], (L, D, IN_WIDTH), D ** -0.5),
        'b_gate': nrm(ks[4], (L, N_BRANCHES * D), 0.02),
        'rel_bias': nrm(ks[5], (L, ATTN_HEADS, REL_SIZE), 0.2),
        'lam_re': -0.5 + nrm(ks[6], (L, G, P), 0.01),
        'lam_im': lam_im0 + nrm(ks[7], (L, G, P), 0.01),
        'log_dt': jax.random.uniform(ks[8], (L, G), f32, math.log(DT_MIN), math.log(DT_MAX)),
        'ssm_b_re': nrm(ks[9], (L, G, P, Hg), (2 * Hg) ** -0.5),
        'ssm_b_im': nrm(ks[10], (L, G, P, Hg), (2 * Hg) ** -0.5),
        'ssm_c_re': nrm(ks[11], (L, G, Hg, P), (2 * P) ** -0.5),
        'ssm_c_im': nrm(ks[12], (L, G, Hg, P), (2 * P) ** -0.5),
        'ssm_d': nrm(ks[13], (L, SSM_WIDTH), 1.0),
        'w_glu': nrm(ks[14], (L, SSM_WIDTH, 2 * SSM_WIDTH), SSM_WIDTH ** -0.5),
        'w_up_attn': nrm(ks[15], (L, ATTN_WIDTH, D), ATTN_WIDTH ** -0.5),
        'w_up_ssm': nrm(ks[16], (L, SSM_WIDTH, D), SSM_WIDTH ** -0.5),
        'w_o': nrm(ks[17], (L, D, D), DEEPNORM_BETA * D ** -0.5),
        'ln1_g': 1.0 + nrm(ks[18], (L, D), 0.02),
        'ln1_b': nrm(ks[19], (L, D), 0.02),
        'router_w': nrm(ks[20], (L, D, E), D ** -0.5),
        'router_b': nrm(ks[21], (L, E), 0.01),
        'w_gate_up': nrm(ks[22], (L, E, D, 2 * D_EXPERT), D ** -0.5),
        'b_gate_up': nrm(ks[23], (L, E, 2 * D_EXPERT), 0.01),
        'w_down': nrm(ks[24], (L, E, D_EXPERT, D), DEEPNORM_BETA * D_EXPERT ** -0.5),
        'b_down': nrm(ks[25], (L, E, D), 0.01),
        'ln2_g': 1.0 + nrm(ks[26], (L, D), 0.02),
        'ln2_b': nrm(ks[27], (L, D), 0.02),
    }

def reference(x, ln_in_g, ln_in_b, w_in, b_gate, rel_bias, lam_re, lam_im, log_dt,
              ssm_b_re, ssm_b_im, ssm_c_re, ssm_c_im, ssm_d, w_glu, w_up_attn, w_up_ssm,
              w_o, ln1_g, ln1_b, router_w, router_b, w_gate_up, b_gate_up, w_down, b_down,
              ln2_g, ln2_b):
    splits = [ATTN_WIDTH, 2 * ATTN_WIDTH, 3 * ATTN_WIDTH, 3 * ATTN_WIDTH + SSM_WIDTH]
    h = layer_norm(x, ln_in_g, ln_in_b)
    for l in range(DEPTH):
        proj = h @ w_in[l]
        q, k, v, u, gate_logits = jnp.split(proj, splits, axis=-1)
        gates = jax.nn.sigmoid(gate_logits + b_gate[l])
        g_attn, g_ssm = jnp.split(gates, 2, axis=-1)
        y_attn = chunked_rel_attention(q, k, v, rel_bias[l]) @ w_up_attn[l]
        y_s = s5_ssm(u, lam_re[l], lam_im[l], log_dt[l], ssm_b_re[l], ssm_b_im[l],
                     ssm_c_re[l], ssm_c_im[l], ssm_d[l])
        glu_a, glu_b = jnp.split(jax.nn.gelu(y_s) @ w_glu[l], 2, axis=-1)
        y_ssm = (glu_a * jax.nn.sigmoid(glu_b)) @ w_up_ssm[l]
        mix = (g_attn * y_attn + g_ssm * y_ssm) @ w_o[l]
        h = layer_norm(DEEPNORM_ALPHA * h + mix, ln1_g[l], ln1_b[l])
        ffn = moe_ffn(h, router_w[l], router_b[l], w_gate_up[l], b_gate_up[l],
                      w_down[l], b_down[l])
        h = layer_norm(DEEPNORM_ALPHA * h + ffn, ln2_g[l], ln2_b[l])
    return h


_drawn_inputs = setup_inputs


def setup_inputs(seed=0):
    import zlib

    import numpy as np

    out = dict(_drawn_inputs(seed))
    spreads = {}
    factors = {'b_gate': 25.525,
     'rel_bias': 3.51,
     'lam_re': 64.0,
     'lam_im': 29.536,
     'log_dt': 27.536,
     'ssm_b_re': 31.96,
     'ssm_b_im': 31.768,
     'ssm_c_re': 44.416,
     'ssm_c_im': 34.52,
     'router_b': 5.092,
     'b_gate_up': 8.0,
     'b_down': 8.0,
     'ln2_g': 7.835,
     'ln2_b': 8.728}
    for name, (base, spread) in spreads.items():
        noise = np.random.default_rng([zlib.crc32(name.encode()), seed]).standard_normal(out[name].shape)
        drawn = base * np.exp(spread * noise) if base else spread * noise
        out[name] = __import__('jax').numpy.asarray(drawn.astype(out[name].dtype))
    for name, factor in factors.items():
        out[name] = (out[name] * factor).astype(out[name].dtype)
    return out
```

```python
from contextlib import ExitStack

import numpy as np

import concourse.bass as bass
from concourse import mybir

F32 = mybir.dt.float32
I32 = mybir.dt.int32
U32 = mybir.dt.uint32
ALU = mybir.AluOpType
ACT = mybir.ActivationFunctionType
AX_X = mybir.AxisListType.X

P = 128
T = 256
TT = T // P
D = 1024
KD = D // P
AW = 512
KA = AW // P
HEADS, HD = 8, 64
CHUNK = 64
REL = 320
GS = 16
NST = 64
ST = 16
E = 32
TOPK = 4
CAP = 64
ROUNDS = T // CAP
PAIRS = E // 2
LIMIT = 7.0
SWALPHA = 1.702
EPS = 1e-5
ALPHA = 2.0 ** 0.25
MAGIC = 12582912.0
TWO_PI = 6.2831845
INV_2PI = float(1.0 / (2.0 * np.pi))
GELU_A, GELU_C = 0.044715, 0.7978845608028654
FAR = 1000.0
K_ORDER = [2, 3, 4, 5, 6, 7, 1, 0]
J_ORDER = [1, 0, 2, 3]

C_G, C_B, C_GATE, C_D, C_RE, C_IM, C_DT, C_END = 0, 8, 16, 32, 36, 52, 68, 84
O_ID, O_UP, O_SLOT, O_TIME, O_MASK, O_END = 0, 128, 256, 384, 640, 648


def trunk_and_moe(nc, x, w_in, w_glu, w_ua, w_us, w_o, w_gu, w_dn, rel_bias, router_w, router_b,
                  cols_d, bc_d, consts_d, lnrows_d, bgu_d, bdn_d, out):
    with ExitStack() as ctx:
        def sb(name, shape, dt=F32):
            return ctx.enter_context(nc.sbuf_tensor(name, shape, dt))

        def sem(name):
            return ctx.enter_context(nc.semaphore(name))

        gu_ring = sb("gu_ring", [P, 2, KD, 2 * D])
        dn_ring = sb("dn_ring", [P, KD, D])
        stream = [gu_ring[:, 0, 2 * s:2 * s + 2, :].rearrange("p a n -> p (a n)") for s in range(4)]
        g1 = gu_ring[:, 1, :, :].rearrange("p k n -> p (k n)")
        cosT = g1[:, 0:4096].rearrange("p (b i t) -> p b i t", b=4, i=4)
        sinT = g1[:, 4096:8192].rearrange("p (b i t) -> p b i t", b=4, i=4)
        BT = g1[:, 8192:12288].rearrange("p (r b m s) -> p r b m s", r=2, b=4, m=8)
        gatesT = g1[:, 12288:16384].rearrange("p (n t) -> p n t", n=16)
        bc_raw = g1[:, 12288:13312]
        bt_raw = bc_raw[:, 0:512].rearrange("p (r b s) -> p r b s", r=2, b=4)
        ct_raw = bc_raw[:, 512:1024].rearrange("p (r i c) -> p r i c", r=2, i=ST)
        lamw = g1[:, 13312:13312 + 24 * ST].rearrange("p (n i) -> p n i", i=ST)
        ctw = g1[:, 14336:14336 + 1024].rearrange("p (r i c) -> p r i c", r=4, i=ST)
        dn = dn_ring[:, :, :].rearrange("p k n -> p (k n)")
        QZ = dn[:, 0:2048].rearrange("p (h t) -> p h t", h=HEADS)
        KT = dn[:, 2048:3072].rearrange("p (j t) -> p j t", j=KA)
        PT0 = dn[:, 0:2048].rearrange("p (h t) -> p h t", h=HEADS)
        PT1 = dn[:, 2048:3072].rearrange("p (h t) -> p h t", h=HEADS)
        V = dn[:, 3072:4096].rearrange("p (a n) -> p a n", a=TT)
        relb = dn[:, 4096:6144].rearrange("p (h j) -> p h j", h=HEADS)
        CT = dn[:, 6144:7168].rearrange("p (r i c) -> p r i c", r=2, i=ST)
        uT = dn[:, 7168:8192].rearrange("p (b t) -> p b t", b=4)
        h = sb("h", [P, TT, D])
        hT_mem = sb("hT_mem", [P, 2048])
        hT = hT_mem[:, :].rearrange("p (k t) -> p k t", k=KD)
        mixT = hT
        XT = hT_mem[:, 0:1024].rearrange("p (k c) -> p k c", k=KD)
        wide = sb("wide", [P, 2048])
        s_re = wide[:, 0:1024].rearrange("p (i t) -> p i t", i=4)
        s_im = wide[:, 1024:2048].rearrange("p (i t) -> p i t", i=4)
        ssmT = wide[:, 0:1024].rearrange("p (b t) -> p b t", b=4)
        gel = wide[:, 1024:2048].rearrange("p (b t) -> p b t", b=4)
        tmpg = [gel[:, 0, :], gel[:, 1, :]]
        h1T = wide[:, :].rearrange("p (k t) -> p k t", k=KD)
        xg, xl, sig = wide[:, 0:512], wide[:, 512:1024], wide[:, 1024:1536]
        sel4 = [wide[:, 1536:1792].rearrange("p (q c) -> p q c", q=4), wide[:, 1792:2048].rearrange("p (q c) -> p q c", q=4)]
        mid = sb("mid", [P, 3072])
        z_re = mid[:, 0:1024].rearrange("p (i t) -> p i t", i=4)
        z_im = mid[:, 1024:2048].rearrange("p (i t) -> p i t", i=4)
        tmp = mid[:, 2048:3072].rearrange("p (i t) -> p i t", i=4)
        S1 = mid[:, 0:2048].rearrange("p (h k) -> p h k", h=HEADS)
        S0 = mid[:, 2048:3072].rearrange("p (h k) -> p h k", h=HEADS)
        rows = mid[:, 0:2048].rearrange("p (r d) -> p r d", r=2)
        actT = mid[:, 0:512].rearrange("p (k c) -> p k c", k=4)
        ysb = mid[:, 512:1024]
        Pm = mid[:, 1024:1280].rearrange("p (a s) -> p a s", a=TT)
        PG = mid[:, 1280:1536].rearrange("p (a s) -> p a s", a=TT)
        bgu = mid[:, 1536:2048]
        bdn = mid[:, 2048:3072]
        attnT_m = sb("attnT", [P, 1024])
        attnT = attnT_m[:, :].rearrange("p (j t) -> p j t", j=KA)
        GTz = attnT_m[:, :].rearrange("p (a f t) -> p a f t", a=2, f=2)
        consts = sb("consts", [P, O_END])
        ident = consts[:, O_ID:O_ID + 128]
        upper = consts[:, O_UP:O_UP + 128]
        slots = consts[:, O_SLOT:O_SLOT + 128]
        times = consts[:, O_TIME:O_TIME + 256]
        gmask = consts[:, O_MASK:O_MASK + 8]
        cols = sb("cols", [P, C_END])
        posx = sb("posx", [P, TT, ROUNDS * E + 2])
        gx = sb("gx", [P, TT, ROUNDS * E])
        decay = sb("decay", [P, ST])
        turn = sb("turn", [P, ST])
        stat = sb("stat", [P, TT, 2, 6])
        mv = sb("mv", [P, TT, 2])
        rstd = sb("rstd", [P, TT])
        half_power = sb("half_power", [P, 1])
        negmax = sb("negmax", [P, 2, HEADS])
        psums = sb("psums", [P, 2, HEADS])
        logits = sb("logits", [P, TT, E])
        top = sb("top", [P, TT, 8])
        topi = sb("topi", [P, TT, 8], U32)
        topf = sb("topf", [P, TT, 8])
        ex = sb("ex", [P, TT, 8])
        mask = sb("mask", [P, TT, E])
        Gd = sb("Gd", [P, TT, E])
        rwb = sb("rwb", [P, E])
        cmax = sb("cmax", [P, 1])
        cint = sb("cint", [P, 1], I32)
        rw = attnT_m[:, 0:256].rearrange("p (k e) -> p k e", k=KD)
        oneh = attnT_m[:, 256:512].rearrange("p (a k e) -> p a k e", a=TT, k=TOPK)
        oneg = attnT_m[:, 512:768].rearrange("p (a k e) -> p a k e", a=TT, k=TOPK)
        GdT = attnT_m[0:32, 768:1024]
        ones = sb("ones", [P, P])

        ps = [ctx.enter_context(nc.psum_tensor(f"ps{i}", [P, 512], F32)) for i in range(8)]
        psA, psB, psY, psM = ps[4], ps[5], ps[6], ps[7]

        x_in = [sem(f"x_in{i}") for i in range(TT)]
        const_in, cols_in, bc_in, relb_in, rb_in = (sem(n) for n in ("const_in", "cols_in", "bc_in", "relb_in", "rb_in"))
        rw_in, lnin_in, ln1_in, bgu_in, bdn_in, ln2_in = (sem(n) for n in ("rw_in", "lnin_in", "ln1_in", "bgu_in", "bdn_in", "ln2_in"))
        w_loaded = [sem(f"w_loaded{s}") for s in range(4)]
        gu_loaded = [[sem(f"gu_loaded{a}_{k}") for k in range(KD)] for a in range(2)]
        dn_loaded = [sem(f"dn_loaded{j}") for j in range(4)]
        vec_chain, act_chain, pool_chain = sem("vec_chain"), sem("act_chain"), sem("pool_chain")
        xhat_ready, hT_psum, hT_act, hT_vec = sem("xhat_ready"), sem("hT_psum"), sem("hT_act"), sem("hT_vec")
        dt_ready, lam_ready, decay_ready, turn_ready, sin_ready, coef_ready = (
            sem(n) for n in ("dt_ready", "lam_ready", "decay_ready", "turn_ready", "sin_ready", "coef_ready"))
        ang_ready, table_ready = sem("ang_ready"), sem("table_ready")
        qz_zero, bt_ready, ct_ready, h_ready = sem("qz_zero"), sem("bt_ready"), sem("ct_ready"), sem("h_ready")
        proj_done, proj_act, proj_vec = sem("proj_done"), sem("proj_act"), sem("proj_vec")
        bu_psum, bu_used, s_ready, y_psum, y_used = (sem(n) for n in ("bu_psum", "bu_used", "s_ready", "y_psum", "y_used"))
        gelu_arg, gelu_sig, gelu_ready = sem("gelu_arg"), sem("gelu_sig"), sem("gelu_ready")
        score_psum, score_used, max_ready, exp_done, p_norm = (sem(n) for n in ("score_psum", "score_used", "max_ready", "exp_done", "p_norm"))
        pt_psum, pt_act, pt_vec, pv_psum, attn_ready = (sem(n) for n in ("pt_psum", "pt_act", "pt_vec", "pv_psum", "attn_ready"))
        mix_ready, wo_done, h1_ready, h1T_psum, h1T_act, h1T_vec = (sem(n) for n in ("mix_ready", "wo_done", "h1_ready", "h1T_psum", "h1T_act", "h1T_vec"))
        ln1_done = sem("ln1_done")
        logit_psum, top_ready, topexp, mask_ready, pos_psum, gd_ready, gdT_psum, gdT_ready = (
            sem(n) for n in ("logit_psum", "top_ready", "topexp", "mask_ready", "pos_psum", "gd_ready", "gdT_psum", "gdT_ready"))
        gdT_used, var_ready, rstd_ready = sem("gdT_used"), sem("var_ready"), sem("rstd_ready")
        slots_ready, count_ready, pad_ready = sem("slots_ready"), sem("count_ready"), sem("pad_ready")
        gtz_zero = sem("gtz_zero")
        p_ready, gather_psum, xt_ready = sem("p_ready"), sem("gather_psum"), sem("xt_ready")
        sel_ready, gu_done, gu_used, dn_used = sem("sel_ready"), sem("gu_done"), sem("gu_used"), sem("dn_used")
        pg_ready, gt_psum, gt_ready = sem("pg_ready"), sem("gt_psum"), sem("gt_ready")
        xg_ready, ab_free, lin_ready, sig_ready, act_ready = (sem(n) for n in ("xg_ready", "ab_free", "lin_ready", "sig_ready", "act_ready"))
        at_psum, at_ready, y_ready = sem("at_psum"), sem("at_ready"), sem("y_ready")
        moe_done, out_ready, out_done = sem("moe_done"), sem("out_ready"), sem("out_done")

        G_U, G_Q, G_K, G_V, G_GATE, G_GLU, G_US, G_UA, G_END = 0, 4, 8, 12, 16, 32, 40, 48, 56
        after_block = [4, 8, 12, 16, 20, 24, 28, 32, 40, 48, 56]
        B_WO = 11

        def w_in_block(c0):
            return w_in[:, c0:c0 + 512].rearrange("(k p) n -> p k n", p=P)

        blocks = [w_in_block(c) for c in (1536, 0, 512, 1024, 2048, 2560, 3072, 3584)]
        blocks += [w.rearrange("(k p) n -> p k n", p=P) for w in (w_glu, w_us, w_ua)]
        blocks += [w_o[:, c:c + 512].rearrange("(k p) n -> p k n", p=P) for c in (0, 512)]

        def bank_of(g):
            return ps[g % 2][:, 0:T]

        def read_by_act(g):
            return g < G_GLU or (g < G_US and g % 2 == 0)

        def group_read(g):
            mine = [i for i in range(g + 1) if read_by_act(i) == read_by_act(g)]
            return (proj_act if read_by_act(g) else proj_vec), len(mine)

        def gu_src(e, k):
            return w_gu[e, k * P:(k + 1) * P, :]

        def dn_src(e, j):
            return w_dn[e, 2 * j * P:2 * (j + 1) * P, :].rearrange("(k p) n -> p k n", p=P)

        block = ctx.enter_context(nc.Block())

        @block.sync
        def _(sp):
            def load_block(i):
                if i >= 4:
                    sp.wait_ge(proj_done, after_block[i - 4])
                src = blocks[i]
                nk = src.shape[1]
                dst = stream[i % 4].rearrange("p (k n) -> p k n", k=nk)
                for a in range(2):
                    ks = slice(a * nk // 2, (a + 1) * nk // 2)
                    sp.dma_start(dst[:, ks, :], src[:, ks, :]).then_inc(w_loaded[i % 4], 16)

            for tt in range(TT):
                sp.dma_start(h[:, tt, :], x[tt * P:(tt + 1) * P, :]).then_inc(x_in[tt], 16)
            for i in range(len(blocks)):
                load_block(i)

            def load_gu(e, a, k):
                sp.dma_start(gu_ring[:, a, k, :], gu_src(e, k)).then_inc(gu_loaded[a][k], 16)

            def load_dn(e, j):
                sp.dma_start(dn_ring[:, 2 * j:2 * j + 2, :], dn_src(e, j)).then_inc(dn_loaded[j], 16)

            sp.wait_ge(pv_psum, 2)
            sp.wait_ge(proj_done, G_US)
            for j in J_ORDER:
                load_dn(0, j)
            for k in K_ORDER[0:2] + [4, 5, 0, 1]:
                load_gu(1, 1, k)
            sp.wait_ge(proj_done, G_UA)
            load_gu(0, 0, 2)
            load_gu(0, 0, 3)
            sp.wait_ge(proj_done, G_END)
            load_gu(0, 0, 4)
            load_gu(0, 0, 5)
            sp.wait_ge(mix_ready, KD)
            load_gu(1, 1, 6)
            load_gu(1, 1, 7)
            sp.wait_ge(wo_done, 2)
            load_gu(0, 0, 6)
            load_gu(0, 0, 7)
            sp.wait_ge(wo_done, 4)
            load_gu(0, 0, 1)
            load_gu(0, 0, 0)
            for i, j in enumerate(J_ORDER):
                sp.wait_ge(dn_used, i + 1)
                load_dn(1, j)

            def pair_loads(it, pair):
                for a in range(2):
                    n, e = it * 2 + a, pair * 2 + a
                    for i, k in enumerate(K_ORDER):
                        if i % 2 == 0:
                            sp.wait_ge(gu_used, n * KD + (i + 2 - 2 * KD))
                        sp.dma_start(gu_ring[:, a, k, :],
                                     w_gu[bass.ds(e, 1), k * P:(k + 1) * P, :].rearrange("o p n -> (o p) n")).then_inc(gu_loaded[a][k], 16)
                    for i, j in enumerate(J_ORDER):
                        if i % 2 == 0:
                            sp.wait_ge(dn_used, n * 4 + (i + 2 - 4))
                        sp.dma_start(dn_ring[:, 2 * j:2 * j + 2, :],
                                     w_dn[bass.ds(e, 1), 2 * j * P:2 * (j + 1) * P, :].rearrange("o (k p) n -> p (o k) n", p=P)).then_inc(dn_loaded[j], 16)

            with sp.Fori(1, PAIRS) as it:
                pair_loads(it, it)
            sp.wait_ge(count_ready, 1)
            fullest = sp.value_load(cint[0:1, 0:1], min_val=0, max_val=T)
            with sp.If(fullest > CAP):
                with sp.Fori(1, ROUNDS) as rnd:
                    with sp.Fori(0, PAIRS) as pair:
                        pair_loads(rnd * PAIRS + pair, pair)
            with sp.Else():
                sp.nop()
            sp.wait_ge(moe_done, 1)
            for r in range(2):
                sp.dma_start(gu_ring[:, 0, 0, r * D:(r + 1) * D],
                             lnrows_d[4 + r:5 + r, :].to_broadcast([P, D])).then_inc(ln2_in, 16)
            for tt in range(TT):
                sp.wait_ge(out_ready, tt + 1)
                sp.dma_start(out[tt * P:(tt + 1) * P, :], h[:, tt, :]).then_inc(out_done, 16)
            sp.wait_ge(out_done, 16 * TT)

        @block.scalar
        def _(act):
            chain = [0]

            def link(ins):
                chain[0] += 1
                ins.then_inc(act_chain, 1)
                act.wait_ge(act_chain, chain[0])

            act.dma_start(cols[:, :], cols_d).then_inc(cols_in, 16)
            act.dma_start(consts[:, :], consts_d).then_inc(const_in, 16)
            act.dma_start(bc_raw, bc_d).then_inc(bc_in, 16)
            act.dma_start(rwb[:, :], router_b.to_broadcast([P, E])).then_inc(rb_in, 16)
            for a in range(2):
                act.dma_start(relb[CHUNK * a:CHUNK * a + CHUNK, :, :],
                              bass.AP(tensor=rel_bias.tensor, offset=0, ap=[[1, CHUNK], [REL, HEADS], [1, 256]])).then_inc(relb_in, 16)

            act.wait_ge(cols_in, 16)
            act.activation(lamw[:, 0, :], cols[:, C_DT:C_DT + ST], ACT.Exp).then_inc(dt_ready, 1)
            act.wait_ge(lam_ready, 1)
            act.activation(decay[:, :], lamw[:, 1, :], ACT.Exp).then_inc(decay_ready, 1)
            act.wait_ge(turn_ready, 1)
            act.activation(lamw[:, 5, :], turn[:, :], ACT.Sin, scale=TWO_PI).then_inc(sin_ready, 1)
            act.activation(lamw[:, 6, :], turn[:, :], ACT.Sin, scale=TWO_PI / 2).then_inc(sin_ready, 1)

            def tables(b):
                act.wait_ge(ang_ready, b + 1)
                link(act.activation(cosT[:, b], sinT[:, b], ACT.Sin, scale=TWO_PI / 2))
                link(act.activation(sinT[:, b], sinT[:, b], ACT.Sin, scale=TWO_PI))
                link(act.activation(cosT[:, b], cosT[:, b], ACT.Square))
                act.activation(cosT[:, b], cosT[:, b], ACT.Copy, scale=-2.0, bias=1.0).then_inc(table_ready, 1)

            for k in (0, 1, 4, 5):
                act.wait_ge(hT_psum, k // 2 + 1)
                act.activation(hT[:, k, :], ps[4 + k // 2][:, (k % 2) * T:(k % 2) * T + T], ACT.Identity,
                               bias=cols[:, C_B + k:C_B + k + 1], scale=cols[:, C_G + k:C_G + k + 1]).then_inc(hT_act, 1)
            tables(0)

            def evac(g):
                act.wait_ge(proj_done, g + 1)
                src = bank_of(g)
                if g < G_Q:
                    ins = act.activation(uT[:, g - G_U, :], src, ACT.Copy)
                elif g < G_K:
                    j = g - G_Q
                    if j == 0:
                        act.wait_ge(qz_zero, 1)
                    act.activation(QZ[0:64, 2 * j, :], src[0:64, :], ACT.Copy, scale=HD ** -0.5)
                    ins = act.activation(QZ[64:128, 2 * j + 1, :], src[64:128, :], ACT.Copy, scale=HD ** -0.5)
                elif g < G_V:
                    ins = act.activation(KT[:, g - G_K, :], src, ACT.Copy)
                elif g < G_GATE:
                    a, c = divmod(g - G_V, 2)
                    ins = act.activation(V[:, a, c * 256:(c + 1) * 256], src, ACT.Copy)
                else:
                    n = g - G_GATE
                    if n == 0:
                        act.wait_ge(ct_ready, 1)
                        act.wait_ge(bt_ready, 2)
                    ins = act.activation(gatesT[:, n, :], src, ACT.Sigmoid, bias=cols[:, C_GATE + n:C_GATE + n + 1])
                ins.then_inc(proj_act, 1)

            for g in range(G_U, G_Q):
                evac(g)
            tables(1)
            for g in range(G_Q, G_V):
                evac(g)
            tables(2)
            for g in range(G_V, G_GATE + 4):
                evac(g)
            tables(3)
            for g in range(G_GATE + 4, G_GATE + 12):
                evac(g)
            act.wait_ge(gelu_arg, 1)
            act.activation(gel, gel, ACT.Sigmoid, scale=2.0 * GELU_C).then_inc(gelu_sig, 1)
            for g in range(G_GATE + 12, G_GLU):
                evac(g)

            act.wait_ge(max_ready, 1)
            for a, Sx in ((0, S0), (1, S1)):
                for hd in range(HEADS):
                    act.activation(Sx[:, hd, :], Sx[:, hd, :], ACT.Exp, bias=negmax[:, a, hd:hd + 1],
                                   accum_out=psums[:, a, hd:hd + 1]).then_inc(exp_done, 1)
            for i in range(4):
                g = G_GLU + 2 * i
                act.wait_ge(proj_done, g + 1)
                if i >= 1:
                    act.wait_ge(proj_vec, i)
                act.activation(tmpg[i % 2], bank_of(g), ACT.Sigmoid).then_inc(proj_act, 1)
            for i in (1, 3, 5):
                act.wait_ge(pt_psum, i + 1)
                dst = (PT0[:, 2 * i:2 * i + 2, :] if i < 4 else PT1[:, 4 * (i - 4):4 * (i - 4) + 4, :])
                act.activation(dst.rearrange("p h t -> p (h t)"), ps[2 + i][:, :], ACT.Copy).then_inc(pt_act, 1)
            for i in (1, 3):
                act.wait_ge(h1T_psum, i + 1)
                act.activation(h1T[:, 2 * i:2 * i + 2, :].rearrange("p k t -> p (k t)"), ps[i][:, :], ACT.Copy).then_inc(h1T_act, 1)
            for a in range(TT):
                act.wait_ge(top_ready, a + 1)
                act.activation(ex[:, a, 0:TOPK], top[:, a, 0:TOPK], ACT.Exp, bias=topf[:, a, 7:8],
                               accum_out=ex[:, a, 4:5]).then_inc(topexp, 1)
            act.wait_ge(gdT_psum, 2)
            act.activation(GdT, ps[5][0:32, 256:512], ACT.Copy).then_inc(gdT_ready, 1)
            for i, bank in ((0, psM), (1, psY)):
                act.wait_ge(gather_psum, i + 1)
                act.activation(XT[:, 4 * i:4 * i + 4, :].rearrange("p k c -> p (k c)"), bank[:, :], ACT.Copy).then_inc(xt_ready, 1)

            def pair_work(it):
                for a in range(2):
                    n = it * 2 + a
                    act.wait_ge(xg_ready, n + 1)
                    act.activation(sig, xg, ACT.Sigmoid, scale=SWALPHA).then_inc(sig_ready, 1)
                    if a == 1:
                        act.wait_ge(gather_psum, it * 2 + 3)
                        act.activation(XT[:, 0:4, :].rearrange("p k c -> p (k c)"), psM[:, :], ACT.Copy).then_inc(xt_ready, 1)
                    act.wait_ge(gt_psum, n + 2)
                    act.activation(GTz[0:64, a, 0, :], psY[0:64, 0:256], ACT.Copy).then_inc(gt_ready, 1)
                    act.activation(GTz[64:128, a, 1, :], psY[64:128, 0:256], ACT.Copy).then_inc(gt_ready, 1)
                    act.wait_ge(at_psum, n + 1)
                    act.activation(actT[:, :, :].rearrange("p k c -> p (k c)"), psY[:, :], ACT.Copy).then_inc(at_ready, 1)
                    if a == 1:
                        act.wait_ge(gather_psum, it * 2 + 4)
                        act.activation(XT[:, 4:8, :].rearrange("p k c -> p (k c)"), psA[:, :], ACT.Copy).then_inc(xt_ready, 1)

            with act.Fori(0, PAIRS) as it:
                pair_work(it)
            act.wait_ge(count_ready, 1)
            fullest = act.value_load(cint[0:1, 0:1], min_val=0, max_val=T)
            with act.If(fullest > CAP):
                with act.Fori(1, ROUNDS) as rnd:
                    with act.Fori(0, PAIRS) as pair:
                        pair_work(rnd * PAIRS + pair)
            with act.Else():
                act.nop()

        @block.gpsimd
        def _(pool):
            chain = [0]

            def link(ins):
                chain[0] += 1
                ins.then_inc(pool_chain, 1)
                pool.wait_ge(pool_chain, chain[0])

            norms = [0]

            def inverse_deviation(tt):
                norms[0] += 1
                pool.wait_ge(var_ready, norms[0])
                pool.tensor_tensor(rstd[:, tt:tt + 1], mv[:, tt, 1:2], half_power[:, :], ALU.pow).then_inc(rstd_ready, 1)

            pool.memset(QZ, 0.0).then_inc(qz_zero, 1)
            pool.memset(ones[:, :], 1.0).then_inc(pad_ready, 1)
            link(pool.memset(CT, 0.0))
            link(pool.memset(half_power[:, :], -0.5))
            for tt in range(TT):
                inverse_deviation(tt)
            pool.wait_ge(const_in, 16)
            pool.wait_ge(bc_in, 16)
            for r in range(2):
                for b in range(4):
                    ins = pool.tensor_tensor(BT[:, r, b], bt_raw[:, r, b].unsqueeze(1).to_broadcast([P, 8, NST]),
                                             gmask.unsqueeze(2).to_broadcast([P, 8, NST]), ALU.mult)
                ins.then_inc(bt_ready, 1)
            pool.wait_ge(coef_ready, 1)
            cr = lamw[:, 12, :].unsqueeze(2).to_broadcast([P, ST, GS])
            ci = lamw[:, 13, :].unsqueeze(2).to_broadcast([P, ST, GS])
            for n, (c, co) in enumerate(((0, cr), (1, ci), (0, ci), (1, cr))):
                link(pool.tensor_tensor(ctw[:, n], ct_raw[:, c], co, ALU.mult))
            link(pool.tensor_tensor(ctw[:, 0], ctw[:, 0], ctw[:, 1], ALU.subtract))
            link(pool.tensor_tensor(ctw[:, 2], ctw[:, 2], ctw[:, 3], ALU.add))
            for hf in range(2):
                q, c = slice(64 * hf, 64 * hf + 64), slice(GS * hf, GS * hf + GS)
                link(pool.tensor_copy(CT[q, 0, :, c], ctw[q, 0]))
                ins = pool.tensor_scalar(CT[q, 1, :, c], ctw[q, 2], -1.0, None, ALU.mult)
                if hf == 0:
                    link(ins)
            ins.then_inc(ct_ready, 1)

            pool.wait_ge(pt_psum, 6)
            for r in range(2):
                pool.dma_start(rows[:, r, :], lnrows_d[r:r + 1, :].to_broadcast([P, D])).then_inc(lnin_in, 16)
            pool.dma_start(bdn[0:E, :], bdn_d).then_inc(bdn_in, 16)
            pool.wait_ge(lnin_in, 32)
            link(pool.tensor_tensor(h[:, :, :], h[:, :, :], rows[:, 0, :].unsqueeze(1).to_broadcast([P, TT, D]), ALU.mult))
            pool.tensor_tensor(h[:, :, :], h[:, :, :], rows[:, 1, :].unsqueeze(1).to_broadcast([P, TT, D]), ALU.add).then_inc(h_ready, 1)
            pool.wait_ge(h_ready, 1)
            for r in range(2):
                pool.dma_start(rows[:, r, :], lnrows_d[2 + r:3 + r, :].to_broadcast([P, D])).then_inc(ln1_in, 16)
            pool.wait_ge(proj_done, G_END)
            pool.dma_start(rw, router_w.rearrange("(k p) e -> p k e", p=P)).then_inc(rw_in, 16)
            for tt in range(TT):
                inverse_deviation(tt)
            pool.wait_ge(ln1_done, TT)
            pool.dma_start(bgu, bgu_d).then_inc(bgu_in, 16)
            pool.wait_ge(gdT_used, 4)
            pool.memset(GTz, 0.0).then_inc(gtz_zero, 1)

            def pair_work(it, pair):
                for a in range(2):
                    n, e = it * 2 + a, pair * 2 + a
                    pool.wait_ge(gu_done, n + 1)
                    picked = ident.rearrange("p (q e) -> p q e", q=4)[:, :, bass.ds(e, 1)].to_broadcast([P, 4, CAP])
                    pool.tensor_tensor(sel4[a], picked, ones[:, 0:CAP].unsqueeze(1).to_broadcast([P, 4, CAP]), ALU.mult).then_inc(sel_ready, 1)

            with pool.Fori(0, PAIRS) as it:
                pair_work(it, it)
            pool.wait_ge(count_ready, 1)
            fullest = pool.value_load(cint[0:1, 0:1], min_val=0, max_val=T)
            with pool.If(fullest > CAP):
                with pool.Fori(1, ROUNDS) as rnd:
                    with pool.Fori(0, PAIRS) as pair:
                        pair_work(rnd * PAIRS + pair, pair)
            with pool.Else():
                pool.nop()
            for tt in range(TT):
                inverse_deviation(tt)

        @block.vector
        def _(dve):
            chain = [0]

            def link(ins):
                chain[0] += 1
                ins.then_inc(vec_chain, 1)
                dve.wait_ge(vec_chain, chain[0])

            norms = [0]

            def norm_rows(tt, signal):
                for i in range(2):
                    ins = dve.bn_stats(stat[:, tt, i, :], h[:, tt, i * 512:(i + 1) * 512])
                    chain[0] += 1
                    ins.then_inc(vec_chain, 1)
                dve.wait_ge(vec_chain, chain[0])
                norms[0] += 1
                link(dve.bn_aggr(mv[:, tt, :], stat[:, tt, :, :].rearrange("p a b -> p (a b)")))
                dve.tensor_scalar(mv[:, tt, 1:2], mv[:, tt, 1:2], EPS, None, ALU.add).then_inc(var_ready, 1)
                dve.wait_ge(rstd_ready, norms[0])
                ins = dve.tensor_scalar(h[:, tt, :], h[:, tt, :], mv[:, tt, 0:1], rstd[:, tt:tt + 1], ALU.subtract, ALU.mult)
                if signal is None:
                    link(ins)
                else:
                    ins.then_inc(signal, 1)

            for tt in range(TT):
                dve.wait_ge(x_in[tt], 16)
                norm_rows(tt, xhat_ready)

            L = lambda i: lamw[:, i, :]
            lre, lim = cols[:, C_RE:C_RE + ST], cols[:, C_IM:C_IM + ST]
            dve.wait_ge(cols_in, 16)
            dve.wait_ge(dt_ready, 1)
            dve.tensor_tensor(L(1), lre, L(0), ALU.mult).then_inc(lam_ready, 1)
            link(dve.tensor_tensor(L(2), lim, L(0), ALU.mult))
            link(dve.tensor_scalar(L(3), L(2), INV_2PI, None, ALU.mult))
            link(dve.tensor_scalar(L(4), L(3), MAGIC, -MAGIC, ALU.add, ALU.add))
            dve.tensor_tensor(turn[:, :], L(3), L(4), ALU.subtract).then_inc(turn_ready, 1)
            dve.wait_ge(turn_ready, 1)

            for k in (2, 3, 6, 7):
                dve.wait_ge(hT_psum, k // 2 + 1)
                dve.tensor_scalar(hT[:, k, :], ps[4 + k // 2][:, (k % 2) * T:(k % 2) * T + T], cols[:, C_G + k:C_G + k + 1],
                                  cols[:, C_B + k:C_B + k + 1], ALU.mult, ALU.add).then_inc(hT_vec, 1)

            def phases(b):
                ang = sinT[:, b]
                if b == 0:
                    dve.wait_ge(const_in, 16)
                link(dve.tensor_tensor(ang, times.unsqueeze(1).to_broadcast([P, 4, T]),
                                       turn[:, 4 * b:4 * b + 4].unsqueeze(2).to_broadcast([P, 4, T]), ALU.mult))
                link(dve.tensor_scalar(tmp, ang, MAGIC, -MAGIC, ALU.add, ALU.add))
                dve.tensor_tensor(ang, ang, tmp, ALU.subtract).then_inc(ang_ready, 1)
                dve.wait_ge(ang_ready, b + 1)

            phases(0)
            phases(1)
            dve.wait_ge(sin_ready, 2)
            dve.wait_ge(decay_ready, 1)
            link(dve.tensor_tensor(L(7), L(6), L(6), ALU.mult))
            link(dve.tensor_scalar(L(7), L(7), -2.0, 1.0, ALU.mult, ALU.add))
            link(dve.tensor_tensor(L(8), decay[:, :], L(7), ALU.mult))
            link(dve.tensor_scalar(L(8), L(8), 1.0, None, ALU.subtract))
            link(dve.tensor_tensor(L(9), decay[:, :], L(5), ALU.mult))
            link(dve.tensor_tensor(L(10), lre, lre, ALU.mult))
            link(dve.tensor_tensor(L(11), lim, lim, ALU.mult))
            link(dve.tensor_tensor(L(10), L(10), L(11), ALU.add))
            link(dve.reciprocal(L(10), L(10)))
            for o, (a1, b1, a2, b2, op) in ((12, (8, lre, 9, lim, ALU.add)), (13, (9, lre, 8, lim, ALU.subtract))):
                link(dve.tensor_tensor(L(14), L(a1), b1, ALU.mult))
                link(dve.tensor_tensor(L(15), L(a2), b2, ALU.mult))
                link(dve.tensor_tensor(L(14), L(14), L(15), op))
                ins = dve.tensor_tensor(L(o), L(14), L(10), ALU.mult)
                if o == 12:
                    link(ins)
            ins.then_inc(coef_ready, 1)

            def ssm_block(b):
                dve.wait_ge(table_ready, b + 1)
                dve.wait_ge(bu_psum, b + 1)
                cs, sn = cosT[:, b], sinT[:, b]
                for j in range(2):
                    re = ps[2 + j][:, :].rearrange("p (i t) -> p i t", i=2)
                    im = ps[4 + j][:, :].rearrange("p (i t) -> p i t", i=2)
                    v = slice(2 * j, 2 * j + 2)
                    chain[0] += 4
                    dve.tensor_tensor(z_re[:, v], re, cs[:, v], ALU.mult).then_inc(vec_chain, 1)
                    dve.tensor_tensor(tmp[:, v], im, sn[:, v], ALU.mult).then_inc(vec_chain, 1)
                    dve.tensor_tensor(z_im[:, v], im, cs[:, v], ALU.mult).then_inc(vec_chain, 1)
                    dve.wait_ge(vec_chain, chain[0] - 1)
                    dve.tensor_tensor(z_re[:, v], z_re[:, v], tmp[:, v], ALU.add).then_inc(vec_chain, 1)
                    dve.wait_ge(vec_chain, chain[0])
                    dve.tensor_tensor(tmp[:, v], re, sn[:, v], ALU.mult).then_inc(bu_used, 1)
                    dve.wait_ge(bu_used, 2 * b + j + 1)
                    link(dve.tensor_tensor(z_im[:, v], z_im[:, v], tmp[:, v], ALU.subtract))
                for zz in (z_re, z_im):
                    for i in range(4):
                        n = 4 * b + i
                        dve.tensor_tensor_scan(zz[:, i], decay[:, n:n + 1].to_broadcast([P, T]), zz[:, i], 0.0,
                                               ALU.mult, ALU.add).then_inc(vec_chain, 1)
                        chain[0] += 1
                dve.wait_ge(vec_chain, chain[0])
                if b >= 1:
                    dve.wait_ge(y_psum, b)
                chain[0] += 2
                dve.tensor_tensor(s_re, z_re, cs, ALU.mult).then_inc(vec_chain, 1)
                dve.tensor_tensor(tmp, z_im, sn, ALU.mult).then_inc(vec_chain, 1)
                dve.wait_ge(vec_chain, chain[0])
                link(dve.tensor_tensor(s_re, s_re, tmp, ALU.subtract))
                chain[0] += 2
                dve.tensor_tensor(s_im, z_re, sn, ALU.mult).then_inc(vec_chain, 1)
                dve.tensor_tensor(tmp, z_im, cs, ALU.mult).then_inc(vec_chain, 1)
                dve.wait_ge(vec_chain, chain[0])
                dve.tensor_tensor(s_im, s_im, tmp, ALU.add).then_inc(s_ready, 1)
                dve.wait_ge(s_ready, b + 1)

            def y_block(b):
                dve.wait_ge(y_psum, b + 1)
                dve.scalar_tensor_tensor(out=uT[:, b, :], in0=uT[:, b, :], scalar=cols[:, C_D + b:C_D + b + 1],
                                         in1=ps[6 + b // 2][:, (b % 2) * 256:(b % 2) * 256 + 256], op0=ALU.mult, op1=ALU.add).then_inc(y_used, 1)

            ssm_block(0)
            phases(2)
            ssm_block(1)
            y_block(0)
            phases(3)
            ssm_block(2)
            y_block(1)
            ssm_block(3)
            y_block(2)
            y_block(3)
            dve.wait_ge(y_used, 4)
            link(dve.tensor_tensor(gel, uT, uT, ALU.mult))
            link(dve.tensor_scalar(gel, gel, GELU_A, 1.0, ALU.mult, ALU.add))
            dve.tensor_tensor(gel, gel, uT, ALU.mult).then_inc(gelu_arg, 1)

            dve.wait_ge(relb_in, 32)
            link(dve.memset(S1[0:64, :, 192:256], -1e30))
            link(dve.memset(S0[0:64, :, 64:128], -1e30))
            for a, Sx in ((1, S1), (0, S0)):
                for c in range(2):
                    nk = CHUNK * (2 * a + c + 1)
                    q = slice(64 * c, 64 * c + 64)
                    rev = slice(nk - 1, None, -1)
                    for half in range(2 * (a + 1)):
                        dve.wait_ge(score_psum, 4 * (1 - a) + half + 1 if a else 4 + half + 1)
                        hs = 2 if a else 4
                        hh = slice(hs * half, hs * half + hs)
                        src = ps[2 + half] if a else ps[6 + half]
                        src = src[q, :].rearrange("p (h k) -> p h k", h=hs)[:, :, 0:nk]
                        dve.tensor_tensor(Sx[q, hh, 0:nk], src, relb[q, hh, rev], ALU.add).then_inc(score_used, 1)
            dve.wait_ge(score_used, 12)
            for a, Sx in ((0, S0), (1, S1)):
                link(dve.tensor_reduce(negmax[:, a, :], Sx, AX_X, ALU.max))
            dve.tensor_scalar(negmax[:, :, :], negmax[:, :, :], -1.0, None, ALU.mult).then_inc(max_ready, 1)
            dve.wait_ge(gelu_sig, 1)
            dve.tensor_tensor(uT, uT, gel, ALU.mult).then_inc(gelu_ready, 1)
            dve.wait_ge(exp_done, 2 * HEADS)
            link(dve.reciprocal(psums[:, :, :], psums[:, :, :]))
            for a, Sx in ((0, S0), (1, S1)):
                dve.tensor_tensor(Sx, Sx, psums[:, a, :].unsqueeze(2).to_broadcast([P, HEADS, P * (a + 1)]), ALU.mult).then_inc(p_norm, 1)

            for i in range(4):
                g = G_GLU + 2 * i + 1
                dve.wait_ge(proj_done, g + 1)
                dve.wait_ge(proj_act, G_GLU + i + 1)
                dve.tensor_tensor(ssmT[:, i, :], bank_of(g), tmpg[i % 2], ALU.mult).then_inc(proj_vec, 1)
            for i in (0, 2, 4):
                dve.wait_ge(pt_psum, i + 1)
                dst = (PT0[:, 2 * i:2 * i + 2, :] if i < 4 else PT1[:, 4 * (i - 4):4 * (i - 4) + 4, :])
                dve.tensor_copy(dst.rearrange("p h t -> p (h t)"), ps[2 + i][:, :]).then_inc(pt_vec, 1)
            dve.wait_ge(proj_act, G_GLU + 4)
            for n in range(8):
                dve.wait_ge(proj_done, G_US + n + 1)
                dve.tensor_tensor(mixT[:, n, :], bank_of(G_US + n), gatesT[:, 8 + n, :], ALU.mult).then_inc(proj_vec, 1)
            for i in range(2):
                dve.wait_ge(pv_psum, i + 1)
                dve.tensor_copy(attnT[:, 2 * i:2 * i + 2, :].rearrange("p j t -> p (j t)"), ps[2 + i][:, :]).then_inc(attn_ready, 1)
            for n in range(8):
                dve.wait_ge(proj_done, G_UA + n + 1)
                if n >= 2:
                    dve.wait_ge(mix_ready, n - 1)
                dve.tensor_tensor(gel[:, n % 2, :], bank_of(G_UA + n), gatesT[:, n, :], ALU.mult).then_inc(proj_vec, 1)
                dve.wait_ge(proj_vec, 4 + 8 + n + 1)
                dve.tensor_tensor(mixT[:, n, :], mixT[:, n, :], gel[:, n % 2, :], ALU.add).then_inc(mix_ready, 1)

            dve.wait_ge(h_ready, 1)
            dve.wait_ge(wo_done, 4)
            for tt in range(TT):
                for hf in range(2):
                    v = slice(hf * 512, hf * 512 + 512)
                    chain[0] += 1
                    dve.scalar_tensor_tensor(out=h[:, tt, v], in0=h[:, tt, v], scalar=ALPHA, in1=ps[4 + 2 * tt + hf][:, :],
                                             op0=ALU.mult, op1=ALU.add).then_inc(vec_chain, 1)
                dve.wait_ge(vec_chain, chain[0])
                norm_rows(tt, None)
                dve.wait_ge(ln1_in, 32)
                link(dve.tensor_tensor(h[:, tt, :], h[:, tt, :], rows[:, 0, :], ALU.mult))
                dve.tensor_tensor(h[:, tt, :], h[:, tt, :], rows[:, 1, :], ALU.add).then_inc(ln1_done, 1)
            for i in (0, 2):
                dve.wait_ge(h1T_psum, i + 1)
                dve.tensor_copy(h1T[:, 2 * i:2 * i + 2, :].rearrange("p k t -> p (k t)"), ps[i][:, :]).then_inc(h1T_vec, 1)

            dve.wait_ge(rb_in, 16)
            for a in range(TT):
                dve.wait_ge(logit_psum, a + 1)
                link(dve.tensor_tensor(logits[:, a, :], ps[4 + a][:, 0:E], rwb[:, :], ALU.add))
                link(dve.max(top[:, a, :], logits[:, a, :]))
                link(dve.max_index(topi[:, a, :], top[:, a, :], logits[:, a, :]))
                link(dve.tensor_copy(topf[:, a, 0:7], topi[:, a, 0:7]))
                dve.tensor_scalar(topf[:, a, 7:8], top[:, a, 0:1], -1.0, None, ALU.mult).then_inc(top_ready, 1)
            dve.wait_ge(top_ready, TT)
            iota_e = times[:, 0:E].unsqueeze(1).to_broadcast([P, TOPK, E])
            for a in range(TT):
                link(dve.tensor_tensor(oneh[:, a], iota_e, topf[:, a, 0:TOPK].unsqueeze(2).to_broadcast([P, TOPK, E]), ALU.is_equal))
                dve.tensor_reduce(mask[:, a, :], oneh[:, a].rearrange("p k e -> p e k"), AX_X, ALU.add).then_inc(mask_ready, 1)
            dve.wait_ge(topexp, TT)
            for a in range(TT):
                link(dve.reciprocal(ex[:, a, 5:6], ex[:, a, 4:5]))
                link(dve.tensor_scalar(ex[:, a, 0:TOPK], ex[:, a, 0:TOPK], ex[:, a, 5:6], None, ALU.mult))
                link(dve.tensor_tensor(oneg[:, a], oneh[:, a], ex[:, a, 0:TOPK].unsqueeze(2).to_broadcast([P, TOPK, E]), ALU.mult))
                dve.tensor_reduce(Gd[:, a, :], oneg[:, a].rearrange("p k e -> p e k"), AX_X, ALU.add).then_inc(gd_ready, 1)
            dve.wait_ge(mask_ready, TT)
            dve.wait_ge(pos_psum, 1)
            for a in range(TT):
                link(dve.scalar_tensor_tensor(out=logits[:, a, :], in0=mask[:, a, :], scalar=FAR,
                                              in1=ps[6][:, a * E:(a + 1) * E], op0=ALU.mult, op1=ALU.add))
            for r in range(ROUNDS):
                ins = dve.tensor_scalar(posx[:, :, r * E:(r + 1) * E], logits[:, :, :], -FAR - CAP * r, None, ALU.add)
                link(ins) if r == 0 else ins.then_inc(slots_ready, 1)
            dve.wait_ge(gd_ready, TT)
            for r in range(ROUNDS):
                dve.tensor_copy(gx[:, :, r * E:(r + 1) * E], Gd[:, :, :]).then_inc(slots_ready, 1)
            dve.memset(posx[:, :, ROUNDS * E:], -FAR).then_inc(slots_ready, 1)
            dve.wait_ge(ln1_done, TT)
            dve.wait_ge(h1T_psum, 4)

            def next_rows(it_next):
                for tt in range(TT):
                    for a in range(2):
                        where = posx[:, tt, bass.ds(it_next * 2 + a, 1)]
                        dve.tensor_scalar(Pm[:, tt, CAP * a:CAP * a + CAP], slots[:, 0:CAP], where, None, ALU.is_equal).then_inc(p_ready, 1)

            for tt in range(TT):
                for a in range(2):
                    dve.tensor_scalar(Pm[:, tt, CAP * a:CAP * a + CAP], slots[:, 0:CAP], posx[:, tt, a:a + 1], None, ALU.is_equal).then_inc(p_ready, 1)
            link(dve.tensor_reduce(cmax[:, :], ps[6][:, 2 * E:3 * E], AX_X, ALU.max))
            dve.tensor_copy(cint[:, :], cmax[:, :]).then_inc(count_ready, 1)
            dve.wait_ge(slots_ready, 2 * ROUNDS)
            dve.wait_ge(count_ready, 1)
            dve.memset(cmax[:, :], 0.0).then_inc(ab_free, 1)

            def pair_work(it):
                for a in range(2):
                    n = it * 2 + a
                    dve.wait_ge(gt_psum, n + 1)
                    for tt in range(TT):
                        dve.tensor_scalar(PG[:, tt, :], slots, posx[:, tt, bass.ds(n, 1)], gx[:, tt, bass.ds(n, 1)],
                                          ALU.is_equal, ALU.mult).then_inc(pg_ready, 1)
                    if a == 0:
                        dve.wait_ge(gather_psum, it * 2 + 2)
                        next_rows(it + 1)
                    dve.wait_ge(gu_done, n + 3)
                    dve.tensor_scalar(xg, psA[:, :], LIMIT, None, ALU.min).then_inc(xg_ready, 1)
                    dve.tensor_scalar(xl, psB[:, :], LIMIT, -LIMIT, ALU.min, ALU.max).then_inc(ab_free, 1)
                    dve.wait_ge(xg_ready, n + 1)
                    dve.wait_ge(ab_free, n + 2)
                    dve.scalar_tensor_tensor(out=xl, in0=xl, scalar=1.0, in1=xg, op0=ALU.add, op1=ALU.mult).then_inc(lin_ready, 1)
                    dve.wait_ge(lin_ready, n + 1)
                    dve.wait_ge(sig_ready, n + 1)
                    dve.tensor_tensor(xl, xl, sig, ALU.mult).then_inc(act_ready, 1)
                    dve.wait_ge(dn_used, n * 4 + 4)
                    dve.tensor_copy(ysb, psY[:, :]).then_inc(y_ready, 1)

            with dve.Fori(0, PAIRS) as it:
                pair_work(it)
            fullest = dve.value_load(cint[0:1, 0:1], min_val=0, max_val=T)
            with dve.If(fullest > CAP):
                with dve.Fori(1, ROUNDS) as rnd:
                    with dve.Fori(0, PAIRS) as pair:
                        pair_work(rnd * PAIRS + pair)
            with dve.Else():
                dve.nop()

            dve.wait_ge(moe_done, 1)
            for tt in range(TT):
                for hf in range(2):
                    v = slice(hf * 512, hf * 512 + 512)
                    chain[0] += 1
                    dve.scalar_tensor_tensor(out=h[:, tt, v], in0=h[:, tt, v], scalar=ALPHA, in1=ps[2 * tt + hf][:, :],
                                             op0=ALU.mult, op1=ALU.add).then_inc(vec_chain, 1)
                dve.wait_ge(vec_chain, chain[0])
                norm_rows(tt, None)
                dve.wait_ge(ln2_in, 32)
                link(dve.tensor_tensor(h[:, tt, :], h[:, tt, :], gu_ring[:, 0, 0, 0:D], ALU.mult))
                dve.tensor_tensor(h[:, tt, :], h[:, tt, :], gu_ring[:, 0, 0, D:2 * D], ALU.add).then_inc(out_ready, 1)

        @block.tensor
        def _(pe):
            pe.wait_ge(const_in, 16)
            for tt in range(TT):
                pe.wait_ge(xhat_ready, tt + 1)
                for k in range(KD):
                    c = (k % 2) * 256 + tt * P
                    ins = pe.transpose(ps[4 + k // 2][:, c:c + P], h[:, tt, k * P:(k + 1) * P], ident)
                    if tt == TT - 1 and k % 2:
                        ins.then_inc(hT_psum, 1)
            pe.wait_ge(hT_act, KD // 2)
            pe.wait_ge(hT_vec, KD // 2)

            def project(g, blk, nk, lhs, rhs):
                if g in (0, G_Q, G_K, G_V, G_GATE, G_GATE + 4, G_GATE + 8, G_GATE + 12, G_GLU, G_US, G_UA):
                    pe.wait_ge(w_loaded[blk % 4], 32 * (blk // 4 + 1))
                if g >= 2:
                    pe.wait_ge(*group_read(g - 2))
                for k in range(nk):
                    ins = pe.matmul(bank_of(g), lhs(k), rhs(k), start=(k == 0), stop=(k == nk - 1))
                ins.then_inc(proj_done, 1)

            def from_h(g0, blk):
                wv = stream[blk % 4].rearrange("p (k n) -> p k n", k=KD)
                for j in range(4):
                    if g0 == G_V:
                        a, c = divmod(j, 2)
                        project(g0 + j, blk, KD, lambda k: hT[:, k, a * P:(a + 1) * P], lambda k: wv[:, k, c * 256:(c + 1) * 256])
                    else:
                        project(g0 + j, blk, KD, lambda k: wv[:, k, j * P:(j + 1) * P], lambda k: hT[:, k, :])

            def inputs_of_states(b):
                if b == 0:
                    pe.wait_ge(bt_ready, 2)
                    pe.wait_ge(proj_act, 4)
                else:
                    pe.wait_ge(bu_used, 2 * b)
                for r in range(2):
                    for i in range(4):
                        ins = pe.matmul(ps[2 + 2 * r + i // 2][:, (i % 2) * 256:(i % 2) * 256 + 256],
                                        BT[:, r, b, 2 * i:2 * i + 2, :].rearrange("p m s -> p (m s)"), uT[:, b, :], start=True, stop=True)
                ins.then_inc(bu_psum, 1)

            def outputs_of_states(b):
                pe.wait_ge(s_ready, b + 1)
                if b % 2:
                    pe.wait_ge(y_used, b)
                if b == 0:
                    pe.wait_ge(ct_ready, 1)
                for r, s in ((0, s_re), (1, s_im)):
                    for i in range(4):
                        ins = pe.matmul(ps[6 + b // 2][32 * i:32 * i + 32, (b % 2) * 256:(b % 2) * 256 + 256],
                                        CT[:, r, 4 * b + i, :], s[:, i, :], start=(r == 0), stop=(r == 1), skip_group_check=True)
                ins.then_inc(y_psum, 1)

            from_h(G_U, 0)
            inputs_of_states(0)
            from_h(G_Q, 1)
            inputs_of_states(1)
            from_h(G_K, 2)
            outputs_of_states(0)
            from_h(G_V, 3)
            inputs_of_states(2)
            from_h(G_GATE, 4)
            outputs_of_states(1)
            inputs_of_states(3)
            from_h(G_GATE + 4, 5)
            outputs_of_states(2)
            from_h(G_GATE + 8, 6)
            outputs_of_states(3)

            pe.wait_ge(bu_used, 8)
            for half in range(4):
                for hd in range(2 * half, 2 * half + 2):
                    ins = pe.matmul(ps[2 + half][:, (hd % 2) * 256:(hd % 2) * 256 + 256], QZ[:, hd, P:2 * P], KT[:, hd // 2, :], start=True, stop=True)
                ins.then_inc(score_psum, 1)
            pe.wait_ge(y_used, 4)
            for half in range(2):
                for hd in range(4 * half, 4 * half + 4):
                    ins = pe.matmul(ps[6 + half][:, (hd % 4) * P:(hd % 4) * P + P], QZ[:, hd, 0:P], KT[:, hd // 2, 0:P], start=True, stop=True)
                ins.then_inc(score_psum, 1)
            from_h(G_GATE + 12, 7)

            wg = stream[8 % 4].rearrange("p (k n) -> p k n", k=KA)
            pe.wait_ge(gelu_ready, 1)
            for i in range(4):
                for g, c in ((G_GLU + 2 * i, AW + i * P), (G_GLU + 2 * i + 1, i * P)):
                    project(g, 8, KA, lambda k: wg[:, k, c:c + P], lambda k: uT[:, k, :])

            pe.wait_ge(p_norm, 2)
            for i in range(4):
                for hd in (2 * i, 2 * i + 1):
                    c = (hd % 2) * 256
                    pe.transpose(ps[2 + i][:, c:c + P], S0[:, hd, :], ident)
                    ins = pe.transpose(ps[2 + i][:, c + P:c + 2 * P], S1[:, hd, 0:P], ident)
                ins.then_inc(pt_psum, 1)
            for i in range(2):
                for hd in range(4 * i, 4 * i + 4):
                    ins = pe.transpose(ps[6 + i][:, (hd % 4) * P:(hd % 4) * P + P], S1[:, hd, P:2 * P], ident)
                ins.then_inc(pt_psum, 1)
            wu = stream[9 % 4].rearrange("p (k n) -> p k n", k=KA)
            pe.wait_ge(proj_vec, 4)
            for n in range(8):
                project(G_US + n, 9, KA, lambda k: wu[:, k, n * P:(n + 1) * P], lambda k: ssmT[:, k, :])
            pe.wait_ge(pt_act, 3)
            pe.wait_ge(pt_vec, 3)
            for j in range(4):
                for hd in (2 * j, 2 * j + 1):
                    q = slice(64 * (hd % 2), 64 * (hd % 2) + 64)
                    o = ps[2 + j // 2][q, (j % 2) * 256:(j % 2) * 256 + 256]
                    pe.matmul(o, V[:, 0, hd * HD:(hd + 1) * HD], PT0[:, hd, :], start=True, stop=False, skip_group_check=True)
                    ins = pe.matmul(o[:, P:2 * P], V[:, 1, hd * HD:(hd + 1) * HD], PT1[:, hd, :], start=False, stop=True, skip_group_check=True)
                if j % 2:
                    ins.then_inc(pv_psum, 1)
            pe.wait_ge(attn_ready, 2)
            wa = stream[10 % 4].rearrange("p (k n) -> p k n", k=KA)
            for n in range(8):
                project(G_UA + n, 10, KA, lambda k: wa[:, k, n * P:(n + 1) * P], lambda k: attnT[:, k, :])
            pe.wait_ge(mix_ready, KD)
            for hf in range(2):
                blk = B_WO + hf
                pe.wait_ge(w_loaded[blk % 4], 32 * (blk // 4 + 1))
                wo = stream[blk % 4].rearrange("p (k n) -> p k n", k=KD)
                for tt in range(TT):
                    for k in range(KD):
                        ins = pe.matmul(ps[4 + 2 * tt + hf][:, :], mixT[:, k, tt * P:(tt + 1) * P], wo[:, k, :], start=(k == 0), stop=(k == KD - 1))
                    ins.then_inc(wo_done, 1)
            for tt in range(TT):
                pe.wait_ge(ln1_done, tt + 1)
                for k in range(KD):
                    c = (k % 2) * 256 + tt * P
                    ins = pe.transpose(ps[k // 2][:, c:c + P], h[:, tt, k * P:(k + 1) * P], ident)
                    if tt == TT - 1 and k % 2:
                        ins.then_inc(h1T_psum, 1)
            pe.wait_ge(h1T_act, 2)
            pe.wait_ge(h1T_vec, 2)
            pe.wait_ge(rw_in, 16)
            for a in range(TT):
                for k in range(KD):
                    ins = pe.matmul(ps[4 + a][:, 0:E], h1T[:, k, a * P:(a + 1) * P], rw[:, k, :], start=(k == 0), stop=(k == KD - 1))
                ins.then_inc(logit_psum, 1)
            pe.wait_ge(mask_ready, TT)
            pe.wait_ge(pad_ready, 1)
            pe.matmul(ps[6][:, 0:E], upper, mask[:, 0, :], start=True, stop=True)
            pe.matmul(ps[6][:, E:2 * E], ones[:, :], mask[:, 0, :], start=True, stop=False)
            pe.matmul(ps[6][:, E:2 * E], upper, mask[:, 1, :], start=False, stop=True)
            pe.matmul(ps[6][:, 2 * E:3 * E], ones[:, :], mask[:, 0, :], start=True, stop=False)
            pe.matmul(ps[6][:, 2 * E:3 * E], ones[:, :], mask[:, 1, :], start=False, stop=True).then_inc(pos_psum, 1)
            def gather(i, bank):
                for k in range(4 * i, 4 * i + 4):
                    for tt in range(TT):
                        ins = pe.matmul(bank[:, (k % 4) * P:(k % 4) * P + P], h[:, tt, k * P:(k + 1) * P], Pm[:, tt, :],
                                        start=(tt == 0), stop=(tt == TT - 1), skip_group_check=True)
                ins.then_inc(gather_psum, 1)

            pe.wait_ge(p_ready, 4)
            gather(0, psM)
            pe.wait_ge(gd_ready, TT)
            for tt in range(TT):
                pe.transpose(ps[5][0:E, 256 + tt * P:256 + (tt + 1) * P], Gd[:, tt, :], ident).then_inc(gdT_psum, 1)
            pe.wait_ge(count_ready, 1)
            gather(1, psY)
            pe.wait_ge(gdT_ready, 1)
            pe.wait_ge(bdn_in, 16)
            for tt in range(TT):
                for hf in range(2):
                    pe.matmul(ps[2 * tt + hf][:, :], GdT[:, tt * P:(tt + 1) * P], bdn[0:E, hf * 512:(hf + 1) * 512],
                              start=True, stop=False, skip_group_check=True).then_inc(gdT_used, 1)
            pe.sem_inc(gu_done, 2)
            pe.sem_inc(gt_psum, 1)
            pe.wait_ge(bgu_in, 16)
            pe.wait_ge(gtz_zero, 1)

            def combine(a, n):
                pe.wait_ge(y_ready, n + 1)
                pe.wait_ge(gt_ready, n * 2 + 2)
                for hf in range(2):
                    for tt in range(TT):
                        pe.matmul(ps[2 * tt + hf][:, :], GTz[:, a, hf, tt * P:(tt + 1) * P], ysb, start=False, stop=False, skip_group_check=True)

            def pair_work(it):
                for a in range(2):
                    n = it * 2 + a
                    if a == 0:
                        pe.wait_ge(xt_ready, it * 2 + 2)
                    pe.wait_ge(ab_free, n + 1)
                    for i, k in enumerate(K_ORDER):
                        pe.wait_ge(gu_loaded[a][k], it * 16 + 16)
                        for q in range(4):
                            bank, hf = (psA, psB)[q // 2], q % 2
                            ins = pe.matmul(bank[64 * hf:64 * hf + 64, :], XT[:, k, CAP * a:CAP * a + CAP], gu_ring[:, a, k, q * 512:(q + 1) * 512],
                                            start=(i == 0), stop=False, skip_group_check=True)
                        ins.then_inc(gu_used, 1)
                    pe.wait_ge(sel_ready, n + 1)
                    for q in range(4):
                        bank, hf = (psA, psB)[q // 2], q % 2
                        ins = pe.matmul(bank[64 * hf:64 * hf + 64, :], sel4[a][:, q, :], bgu, start=False, stop=True, skip_group_check=True)
                    ins.then_inc(gu_done, 1)
                    if a == 1:
                        combine(0, n - 1)
                    pe.wait_ge(pg_ready, n * 2 + 2)
                    for tt in range(TT):
                        ins = pe.transpose(psY[:, tt * P:(tt + 1) * P], PG[:, tt, :], ident)
                    ins.then_inc(gt_psum, 1)
                    if a == 0:
                        pe.wait_ge(p_ready, it * 4 + 8)
                        pe.wait_ge(xt_ready, it * 2 + 2)
                        gather(0, psM)
                    pe.wait_ge(act_ready, n + 1)
                    pe.wait_ge(gt_ready, n * 2 + 2)
                    for j in range(4):
                        ins = pe.transpose(psY[:, j * P:(j + 1) * P], xl[:, j * P:(j + 1) * P], ident)
                    ins.then_inc(at_psum, 1)
                    if a == 1:
                        gather(1, psA)
                    pe.wait_ge(at_ready, n + 1)
                    for i, j in enumerate(J_ORDER):
                        pe.wait_ge(dn_loaded[j], n * 16 + 16)
                        for k in (2 * j, 2 * j + 1):
                            for hf in range(2):
                                ins = pe.matmul(psY[64 * hf:64 * hf + 64, :], actT[:, k % 4, CAP * (k // 4):CAP * (k // 4) + CAP],
                                                dn_ring[:, k, hf * 512:(hf + 1) * 512], start=(i == 0 and k % 2 == 0), stop=(i == 3 and k % 2 == 1), skip_group_check=True)
                        ins.then_inc(dn_used, 1)
                    if a == 1:
                        combine(1, n)

            with pe.Fori(0, PAIRS) as it:
                pair_work(it)
            fullest = pe.value_load(cint[0:1, 0:1], min_val=0, max_val=T)
            with pe.If(fullest > CAP):
                with pe.Fori(1, ROUNDS) as rnd:
                    with pe.Fori(0, PAIRS) as pair:
                        pair_work(rnd * PAIRS + pair)
            with pe.Else():
                pe.nop()
            pe.matmul(psB[0:32, 0:32], ident[:, 0:32], ident[:, 0:32], start=True, stop=True, skip_group_check=True).then_inc(moe_done, 1)


def _consts():
    c = np.zeros((P, O_END), np.float32)
    c[:, O_ID:O_ID + 128] = np.eye(P)
    c[:, O_UP:O_UP + 128] = np.triu(np.ones((P, P)), 1)
    c[:, O_SLOT:O_SLOT + 128] = np.tile(np.arange(CAP), 2)[None]
    c[:, O_TIME:O_TIME + 256] = np.arange(T)[None]
    c[np.arange(P), O_MASK + np.arange(P) // GS] = 1
    return c


def kernel(**inputs):
    import concourse.bacc as bacc
    from concourse.bass_utils import run_bass_kernel_spmd

    a = {k: np.asarray(v) for k, v in inputs.items()}

    def by_partition(v):
        return v.reshape(-1, P).T

    def by_state(v):
        return v.reshape(ST, 2 * NST).T

    cols = np.concatenate([
        by_partition(a["ln_in_g"]), by_partition(a["ln_in_b"]), by_partition(a["b_gate"][0]), by_partition(a["ssm_d"][0]),
        by_state(a["lam_re"][0]), by_state(a["lam_im"][0]), by_state(np.repeat(a["log_dt"][0][:, None], NST, axis=1))], axis=1)
    b_l = [a[n][0].reshape(4, 8, NST, GS).transpose(1, 3, 0, 2).reshape(P, -1) for n in ("ssm_b_re", "ssm_b_im")]
    c_l = [a[n][0].reshape(ST, 2, GS, NST).transpose(1, 3, 0, 2).reshape(P, -1) for n in ("ssm_c_re", "ssm_c_im")]
    arrays = {
        "x": a["x"][0], "w_in": a["w_in"][0], "w_glu": a["w_glu"][0], "w_ua": a["w_up_attn"][0], "w_us": a["w_up_ssm"][0],
        "w_o": a["w_o"][0], "w_gu": a["w_gate_up"][0], "w_dn": a["w_down"][0], "rel_bias": a["rel_bias"][0],
        "router_w": a["router_w"][0], "router_b": a["router_b"],
        "cols": cols, "bc": np.concatenate(b_l + c_l, axis=1), "consts": _consts(),
        "lnrows": np.stack([a["ln_in_g"], a["ln_in_b"], a["ln1_g"][0], a["ln1_b"][0], a["ln2_g"][0], a["ln2_b"][0]]),
        "bgu": a["b_gate_up"][0].reshape(E, 4, 512).transpose(1, 0, 2).reshape(P, 512), "bdn": a["b_down"][0],
    }
    nc = bacc.Bacc("TRN2", target_bir_lowering=False, num_devices=1)
    ins, aps = {}, []
    for name, v in arrays.items():
        v = np.ascontiguousarray(v)
        ins[f"in_{name}_dram"] = v
        aps.append(nc.dram_tensor(f"in_{name}_dram", v.shape, mybir.dt.from_np(v.dtype), kind="ExternalInput").ap())
    aps.append(nc.dram_tensor("out_0_dram", (T, D), F32, kind="ExternalOutput").ap())
    trunk_and_moe(nc, *aps)
    r = run_bass_kernel_spmd(nc, [ins], core_ids=[0])
    return r.results[0]["out_0_dram"].reshape(1, T, D)
```

```python
from contextlib import ExitStack

import numpy as np

import concourse.bass as bass
from concourse import mybir

F32 = mybir.dt.float32
I32 = mybir.dt.int32
U32 = mybir.dt.uint32
ALU = mybir.AluOpType
ACT = mybir.ActivationFunctionType
AX_X = mybir.AxisListType.X

P = 128
T = 256
TT = T // P
D = 1024
KD = D // P
AW = 512
KA = AW // P
HEADS, HD = 8, 64
CHUNK = 64
REL = 320
GS = 16
NST = 64
ST = 16
E = 32
TOPK = 4
CAP = 64
ROUNDS = T // CAP
PAIRS = E // 2
LIMIT = 7.0
SWALPHA = 1.702
EPS = 1e-5
ALPHA = 2.0 ** 0.25
MAGIC = 12582912.0
TWO_PI = 6.2831845
INV_2PI = float(1.0 / (2.0 * np.pi))
GELU_A, GELU_C = 0.044715, 0.7978845608028654
FAR = 1000.0
K_ORDER = [2, 3, 4, 5, 6, 7, 1, 0]
J_ORDER = [1, 0, 2, 3]

C_G, C_B, C_GATE, C_D, C_RE, C_IM, C_DT, C_END = 0, 8, 16, 32, 36, 52, 68, 84
O_ID, O_UP, O_SLOT, O_TIME, O_MASK, O_ALPHA, O_END = 0, 128, 256, 384, 640, 648, 776


def trunk_and_moe(nc, x, w_in, w_glu, w_ua, w_us, w_o, w_gu, w_dn, rel_bias, router_w, router_b,
                  cols_d, bc_d, consts_d, lnrows_d, bgu_d, bdn_d, out):
    with ExitStack() as ctx:
        def sb(name, shape, dt=F32):
            return ctx.enter_context(nc.sbuf_tensor(name, shape, dt))

        def sem(name):
            return ctx.enter_context(nc.semaphore(name))

        gu_ring = sb("gu_ring", [P, 2, KD, 2 * D])
        dn_ring = sb("dn_ring", [P, KD, D])
        stream = [gu_ring[:, 0, 2 * s:2 * s + 2, :].rearrange("p a n -> p (a n)") for s in range(4)]
        g1 = gu_ring[:, 1, :, :].rearrange("p k n -> p (k n)")
        cosT = g1[:, 0:4096].rearrange("p (b i t) -> p b i t", b=4, i=4)
        sinT = g1[:, 4096:8192].rearrange("p (b i t) -> p b i t", b=4, i=4)
        BT = g1[:, 8192:12288].rearrange("p (r b m s) -> p r b m s", r=2, b=4, m=8)
        gatesT = g1[:, 12288:16384].rearrange("p (n t) -> p n t", n=16)
        bc_raw = g1[:, 12288:13312]
        bt_raw = bc_raw[:, 0:512].rearrange("p (r b s) -> p r b s", r=2, b=4)
        ct_raw = bc_raw[:, 512:1024].rearrange("p (r i c) -> p r i c", r=2, i=ST)
        lamw = g1[:, 13312:13312 + 24 * ST].rearrange("p (n i) -> p n i", i=ST)
        ctw = g1[:, 14336:14336 + 1024].rearrange("p (r i c) -> p r i c", r=4, i=ST)
        dn = dn_ring[:, :, :].rearrange("p k n -> p (k n)")
        QZ = dn[:, 0:2048].rearrange("p (h t) -> p h t", h=HEADS)
        KT = dn[:, 2048:3072].rearrange("p (j t) -> p j t", j=KA)
        PT0 = dn[:, 0:2048].rearrange("p (h t) -> p h t", h=HEADS)
        PT1 = dn[:, 2048:3072].rearrange("p (h t) -> p h t", h=HEADS)
        V = dn[:, 3072:4096].rearrange("p (a n) -> p a n", a=TT)
        relb = dn[:, 4096:6144].rearrange("p (h j) -> p h j", h=HEADS)
        CT = dn[:, 6144:7168].rearrange("p (r i c) -> p r i c", r=2, i=ST)
        uT = dn[:, 7168:8192].rearrange("p (b t) -> p b t", b=4)
        h = sb("h", [P, TT, D])
        hT_mem = sb("hT_mem", [P, 2048])
        hT = hT_mem[:, :].rearrange("p (k t) -> p k t", k=KD)
        mixT = hT
        XT = hT_mem[:, 0:1024].rearrange("p (k c) -> p k c", k=KD)
        wide = sb("wide", [P, 2048])
        s_re = wide[:, 0:1024].rearrange("p (i t) -> p i t", i=4)
        s_im = wide[:, 1024:2048].rearrange("p (i t) -> p i t", i=4)
        ssmT = wide[:, 0:1024].rearrange("p (b t) -> p b t", b=4)
        gel = wide[:, 1024:2048].rearrange("p (b t) -> p b t", b=4)
        tmpg = [gel[:, i, :] for i in range(4)]
        h1T = wide[:, :].rearrange("p (k t) -> p k t", k=KD)
        xg, xl, sig = wide[:, 0:512], wide[:, 512:1024], wide[:, 1024:1536]
        Gd = wide[:, 0:TT * P].rearrange("p (a e) -> p a e", a=TT)
        sel4 = [wide[:, 1536:1792].rearrange("p (q c) -> p q c", q=4), wide[:, 1792:2048].rearrange("p (q c) -> p q c", q=4)]
        mid = sb("mid", [P, 3072])
        z_re = mid[:, 0:1024].rearrange("p (i t) -> p i t", i=4)
        z_im = mid[:, 1024:2048].rearrange("p (i t) -> p i t", i=4)
        tmp = mid[:, 2048:3072].rearrange("p (i t) -> p i t", i=4)
        S1 = mid[:, 0:2048].rearrange("p (h k) -> p h k", h=HEADS)
        S0 = mid[:, 2048:3072].rearrange("p (h k) -> p h k", h=HEADS)
        rows = mid[:, 0:2048].rearrange("p (r d) -> p r d", r=2)
        actT = mid[:, 0:512].rearrange("p (k c) -> p k c", k=4)
        ysb = mid[:, 512:1024]
        Pm = mid[:, 1024:1280].rearrange("p (a s) -> p a s", a=TT)
        PG = mid[:, 1280:1536].rearrange("p (a s) -> p a s", a=TT)
        bgu = mid[:, 1536:2048]
        bdn = mid[:, 2048:3072]
        ln2_rows = [hT_mem[:, 1024:2048], mid[:, 2048:3072]]
        attnT_m = sb("attnT", [P, 1024])
        attnT = attnT_m[:, :].rearrange("p (j t) -> p j t", j=KA)
        GTz = attnT_m[:, :].rearrange("p (a f t) -> p a f t", a=2, f=2)
        consts = sb("consts", [P, O_END])
        ident = consts[:, O_ID:O_ID + 128]
        upper = consts[:, O_UP:O_UP + 128]
        slots = consts[:, O_SLOT:O_SLOT + 128]
        times = consts[:, O_TIME:O_TIME + 256]
        gmask = consts[:, O_MASK:O_MASK + 8]
        alpha_id = consts[:, O_ALPHA:O_ALPHA + 128]
        cols = sb("cols", [P, C_END])
        posx = sb("posx", [P, TT, ROUNDS * E + 2])
        gx = sb("gx", [P, TT, ROUNDS * E])
        decay = sb("decay", [P, ST])
        turn = sb("turn", [P, ST])
        stat = sb("stat", [P, TT, 2, 6])
        mv = sb("mv", [P, TT, 2])
        rstd = sb("rstd", [P, TT])
        half_power = sb("half_power", [P, 1])
        negmax = sb("negmax", [P, 2, HEADS])
        psums = sb("psums", [P, 2, HEADS])
        logits = sb("logits", [P, TT, E])
        top = sb("top", [P, TT, 8])
        topi = sb("topi", [P, TT, 8], U32)
        topf = sb("topf", [P, TT, 8])
        ex = sb("ex", [P, TT, 8])
        mask = sb("mask", [P, TT, E])
        rwb = sb("rwb", [P, E])
        cmax = sb("cmax", [P, 1])
        cint = sb("cint", [P, 1], I32)
        rw = attnT_m[:, 0:256].rearrange("p (k e) -> p k e", k=KD)
        oneh = attnT_m[:, 256:512].rearrange("p (a k e) -> p a k e", a=TT, k=TOPK)
        oneg = attnT_m[:, 512:768].rearrange("p (a k e) -> p a k e", a=TT, k=TOPK)
        GdT = attnT_m[:, 768:1024]
        ones = sb("ones", [P, P])

        ps = [ctx.enter_context(nc.psum_tensor(f"ps{i}", [P, 512], F32)) for i in range(8)]
        psA, psB, psY, psM = ps[4], ps[5], ps[6], ps[7]

        x_in = [sem(f"x_in{i}") for i in range(TT)]
        const_in, cols_in, bc_in, relb_in, rb_in = (sem(n) for n in ("const_in", "cols_in", "bc_in", "relb_in", "rb_in"))
        rw_in, lnin_in, ln1_in, bgu_in, bdn_in, ln2_in = (sem(n) for n in ("rw_in", "lnin_in", "ln1_in", "bgu_in", "bdn_in", "ln2_in"))
        w_loaded = [sem(f"w_loaded{s}") for s in range(4)]
        gu_loaded = [[sem(f"gu_loaded{a}_{k}") for k in range(KD)] for a in range(2)]
        dn_loaded = [sem(f"dn_loaded{j}") for j in range(4)]
        vec_chain, act_chain, pool_chain = sem("vec_chain"), sem("act_chain"), sem("pool_chain")
        xhat_ready, hT_psum, hT_act, hT_vec = sem("xhat_ready"), sem("hT_psum"), sem("hT_act"), sem("hT_vec")
        dt_ready, lam_ready, decay_ready, turn_ready, sin_ready, coef_ready = (
            sem(n) for n in ("dt_ready", "lam_ready", "decay_ready", "turn_ready", "sin_ready", "coef_ready"))
        ang_ready, table_ready = sem("ang_ready"), sem("table_ready")
        qz_zero, bt_ready, ct_ready, h_ready = sem("qz_zero"), sem("bt_ready"), sem("ct_ready"), sem("h_ready")
        proj_done, proj_act, proj_vec = sem("proj_done"), sem("proj_act"), sem("proj_vec")
        bu_psum, bu_used, s_ready, y_psum, y_used = (sem(n) for n in ("bu_psum", "bu_used", "s_ready", "y_psum", "y_used"))
        gelu_arg, gelu_sig, gelu_ready = sem("gelu_arg"), sem("gelu_sig"), sem("gelu_ready")
        score_psum, score_used, max_ready, exp_done, p_norm = (sem(n) for n in ("score_psum", "score_used", "max_ready", "exp_done", "p_norm"))
        pt_psum, pt_act, pt_vec, pv_psum, attn_ready = (sem(n) for n in ("pt_psum", "pt_act", "pt_vec", "pv_psum", "attn_ready"))
        mix_ready, wo_done, h1_ready, h1T_psum, h1T_act, h1T_vec = (sem(n) for n in ("mix_ready", "wo_done", "h1_ready", "h1T_psum", "h1T_act", "h1T_vec"))
        ln1_done = sem("ln1_done")
        logit_psum, top_ready, topexp, mask_ready, pos_psum, gd_ready, gdT_psum, gdT_ready = (
            sem(n) for n in ("logit_psum", "top_ready", "topexp", "mask_ready", "pos_psum", "gd_ready", "gdT_psum", "gdT_ready"))
        gd_zero, bdn_zero = sem("gd_zero"), sem("bdn_zero")
        gdT_used, var_ready, rstd_ready = sem("gdT_used"), sem("var_ready"), sem("rstd_ready")
        slots_ready, count_ready, pad_ready = sem("slots_ready"), sem("count_ready"), sem("pad_ready")
        gtz_zero = sem("gtz_zero")
        p_ready, gather_psum, xt_ready = sem("p_ready"), sem("gather_psum"), sem("xt_ready")
        sel_ready, gu_done, gu_used, dn_used = sem("sel_ready"), sem("gu_done"), sem("gu_used"), sem("dn_used")
        pg_ready, gt_psum, gt_ready = sem("pg_ready"), sem("gt_psum"), sem("gt_ready")
        xg_ready, ab_free, lin_ready, sig_ready, act_ready = (sem(n) for n in ("xg_ready", "ab_free", "lin_ready", "sig_ready", "act_ready"))
        at_psum, at_ready, y_ready = sem("at_psum"), sem("at_ready"), sem("y_ready")
        combined, out_ready, out_done = sem("combined"), sem("out_ready"), sem("out_done")

        G_U, G_Q, G_K, G_V, G_GATE, G_GLU, G_US, G_UA, G_END = 0, 4, 8, 12, 16, 32, 40, 48, 56
        after_block = [4, 8, 12, 16, 20, 24, 28, 32, 40, 48, 56]
        B_WO = 11

        def w_in_block(c0):
            return w_in[:, c0:c0 + 512].rearrange("(k p) n -> p k n", p=P)

        blocks = [w_in_block(c) for c in (1536, 0, 512, 1024, 2048, 2560, 3072, 3584)]
        blocks += [w.rearrange("(k p) n -> p k n", p=P) for w in (w_glu, w_us, w_ua)]
        blocks += [w_o[:, c:c + 512].rearrange("(k p) n -> p k n", p=P) for c in (0, 512)]

        def bank_of(g):
            return ps[g % 2][:, 0:T]

        def read_by_act(g):
            return g < G_GLU or (g < G_US and g % 2 == 0)

        def group_read(g):
            mine = [i for i in range(g + 1) if read_by_act(i) == read_by_act(g)]
            return (proj_act if read_by_act(g) else proj_vec), len(mine)

        def gu_src(e, k):
            return w_gu[e, k * P:(k + 1) * P, :]

        def dn_src(e, j):
            return w_dn[e, 2 * j * P:2 * (j + 1) * P, :].rearrange("(k p) n -> p k n", p=P)

        block = ctx.enter_context(nc.Block())

        @block.sync
        def _(sp):
            def load_block(i):
                if i >= 4:
                    sp.wait_ge(proj_done, after_block[i - 4])
                src = blocks[i]
                nk = src.shape[1]
                dst = stream[i % 4].rearrange("p (k n) -> p k n", k=nk)
                for a in range(2):
                    ks = slice(a * nk // 2, (a + 1) * nk // 2)
                    sp.dma_start(dst[:, ks, :], src[:, ks, :]).then_inc(w_loaded[i % 4], 16)

            for tt in range(TT):
                sp.dma_start(h[:, tt, :], x[tt * P:(tt + 1) * P, :]).then_inc(x_in[tt], 16)
            load_block(0)
            sp.dma_start(bc_raw, bc_d).then_inc(bc_in, 16)
            for i in range(1, 4):
                load_block(i)
            for a in range(2):
                sp.dma_start(relb[CHUNK * a:CHUNK * a + CHUNK, :, :],
                             bass.AP(tensor=rel_bias.tensor, offset=0, ap=[[1, CHUNK], [REL, HEADS], [1, 256]])).then_inc(relb_in, 16)
            for i in range(4, len(blocks)):
                load_block(i)

            def load_gu(e, a, k):
                sp.dma_start(gu_ring[:, a, k, :], gu_src(e, k)).then_inc(gu_loaded[a][k], 16)

            def load_dn(e, j):
                sp.dma_start(dn_ring[:, 2 * j:2 * j + 2, :], dn_src(e, j)).then_inc(dn_loaded[j], 16)

            sp.wait_ge(pv_psum, 2)
            sp.wait_ge(proj_done, G_US)
            for j in J_ORDER:
                load_dn(0, j)
            for k in K_ORDER[0:2] + [4, 5, 0, 1]:
                load_gu(1, 1, k)
            sp.wait_ge(proj_done, G_UA)
            load_gu(0, 0, 2)
            load_gu(0, 0, 3)
            sp.wait_ge(proj_done, G_END)
            load_gu(0, 0, 4)
            load_gu(0, 0, 5)
            sp.wait_ge(mix_ready, KD)
            load_gu(1, 1, 6)
            load_gu(1, 1, 7)
            sp.wait_ge(wo_done, 3)
            load_gu(0, 0, 6)
            load_gu(0, 0, 7)
            sp.wait_ge(wo_done, 4)
            load_gu(0, 0, 1)
            load_gu(0, 0, 0)

            def gu_loads(n, e, a):
                for i, k in enumerate(K_ORDER):
                    if i % 2 == 0:
                        sp.wait_ge(gu_used, n * KD + (i + 2 - 2 * KD))
                    sp.dma_start(gu_ring[:, a, k, :],
                                 w_gu[bass.ds(e, 1), k * P:(k + 1) * P, :].rearrange("o p n -> (o p) n")).then_inc(gu_loaded[a][k], 16)

            def dn_loads(n, e):
                for i, j in enumerate(J_ORDER):
                    if i % 2 == 0:
                        sp.wait_ge(dn_used, n * 4 + (i + 2 - 4))
                    sp.dma_start(dn_ring[:, 2 * j:2 * j + 2, :],
                                 w_dn[bass.ds(e, 1), 2 * j * P:2 * (j + 1) * P, :].rearrange("o (k p) n -> p (o k) n", p=P)).then_inc(dn_loaded[j], 16)

            swap = PAIRS - 3
            with sp.Fori(1, swap) as it:
                gu_loads(it * 2, it * 2, 0)
                dn_loads(it * 2 - 1, it * 2 - 1)
                gu_loads(it * 2 + 1, it * 2 + 1, 1)
                dn_loads(it * 2, it * 2)
            gu_loads(2 * swap, 2 * swap, 0)
            dn_loads(2 * swap - 1, 2 * swap - 1)
            dn_loads(2 * swap, 2 * swap)
            gu_loads(2 * swap + 1, 2 * swap + 1, 1)
            dn_loads(2 * swap + 1, 2 * swap + 1)
            with sp.Fori(swap + 1, PAIRS) as it:
                for a in range(2):
                    gu_loads(it * 2 + a, it * 2 + a, a)
                    dn_loads(it * 2 + a, it * 2 + a)
            sp.wait_ge(count_ready, 1)
            fullest = sp.value_load(cint[0:1, 0:1], min_val=0, max_val=T)
            with sp.If(fullest > CAP):
                with sp.Fori(1, ROUNDS) as rnd:
                    with sp.Fori(0, PAIRS) as pair:
                        for a in range(2):
                            n, e = rnd * E + pair * 2 + a, pair * 2 + a
                            gu_loads(n, e, a)
                            dn_loads(n, e)
            with sp.Else():
                sp.nop()
            for tt in range(TT):
                sp.wait_ge(out_ready, tt + 1)
                sp.dma_start(out[tt * P:(tt + 1) * P, :], h[:, tt, :]).then_inc(out_done, 16)
            sp.wait_ge(out_done, 16 * TT)

        @block.scalar
        def _(act):
            chain = [0]

            def link(ins):
                chain[0] += 1
                ins.then_inc(act_chain, 1)
                act.wait_ge(act_chain, chain[0])

            act.dma_start(cols[:, :], cols_d).then_inc(cols_in, 16)
            act.dma_start(consts[:, :], consts_d).then_inc(const_in, 16)
            act.dma_start(rwb[:, :], router_b.to_broadcast([P, E])).then_inc(rb_in, 16)

            act.wait_ge(cols_in, 16)
            act.activation(lamw[:, 0, :], cols[:, C_DT:C_DT + ST], ACT.Exp).then_inc(dt_ready, 1)
            act.wait_ge(lam_ready, 1)
            act.activation(decay[:, :], lamw[:, 1, :], ACT.Exp).then_inc(decay_ready, 1)
            act.wait_ge(turn_ready, 1)
            act.activation(lamw[:, 5, :], turn[:, :], ACT.Sin, scale=TWO_PI).then_inc(sin_ready, 1)
            act.activation(lamw[:, 6, :], turn[:, :], ACT.Sin, scale=TWO_PI / 2).then_inc(sin_ready, 1)

            def tables(b):
                act.wait_ge(ang_ready, b + 1)
                link(act.activation(cosT[:, b], sinT[:, b], ACT.Sin, scale=TWO_PI / 2))
                link(act.activation(sinT[:, b], sinT[:, b], ACT.Sin, scale=TWO_PI))
                link(act.activation(cosT[:, b], cosT[:, b], ACT.Square))
                act.activation(cosT[:, b], cosT[:, b], ACT.Copy, scale=-2.0, bias=1.0).then_inc(table_ready, 1)

            for k in (0, 1, 4, 5):
                act.wait_ge(hT_psum, k // 2 + 1)
                act.activation(hT[:, k, :], ps[4 + k // 2][:, (k % 2) * T:(k % 2) * T + T], ACT.Identity,
                               bias=cols[:, C_B + k:C_B + k + 1], scale=cols[:, C_G + k:C_G + k + 1]).then_inc(hT_act, 1)
            tables(0)

            def evac(g):
                act.wait_ge(proj_done, g + 1)
                src = bank_of(g)
                if g < G_Q:
                    ins = act.activation(uT[:, g - G_U, :], src, ACT.Copy)
                elif g < G_K:
                    j = g - G_Q
                    if j == 0:
                        act.wait_ge(qz_zero, 1)
                    act.activation(QZ[0:64, 2 * j, :], src[0:64, :], ACT.Copy, scale=HD ** -0.5)
                    ins = act.activation(QZ[64:128, 2 * j + 1, :], src[64:128, :], ACT.Copy, scale=HD ** -0.5)
                elif g < G_V:
                    ins = act.activation(KT[:, g - G_K, :], src, ACT.Copy)
                elif g < G_GATE:
                    a, c = divmod(g - G_V, 2)
                    ins = act.activation(V[:, a, c * 256:(c + 1) * 256], src, ACT.Copy)
                else:
                    n = g - G_GATE
                    if n == 0:
                        act.wait_ge(ct_ready, 1)
                        act.wait_ge(bt_ready, 2)
                    ins = act.activation(gatesT[:, n, :], src, ACT.Sigmoid, bias=cols[:, C_GATE + n:C_GATE + n + 1])
                ins.then_inc(proj_act, 1)

            for g in range(G_U, G_Q):
                evac(g)
            tables(1)
            for g in range(G_Q, G_V):
                evac(g)
            tables(2)
            for g in range(G_V, G_GATE + 4):
                evac(g)
            tables(3)
            for g in range(G_GATE + 4, G_GATE + 12):
                evac(g)
            act.wait_ge(gelu_arg, 1)
            act.activation(gel, gel, ACT.Sigmoid, scale=2.0 * GELU_C).then_inc(gelu_sig, 1)
            for g in range(G_GATE + 12, G_GLU):
                evac(g)

            act.wait_ge(max_ready, 1)
            for i in range(4):
                a, Sx = ((0, S0), (1, S1))[i // 2]
                for hd in range(4 * (i % 2), 4 * (i % 2) + 4):
                    act.activation(Sx[:, hd, :], Sx[:, hd, :], ACT.Exp, bias=negmax[:, a, hd:hd + 1],
                                   accum_out=psums[:, a, hd:hd + 1]).then_inc(exp_done, 1)
                g = G_GLU + 2 * i
                act.wait_ge(proj_done, g + 1)
                act.activation(tmpg[i], bank_of(g), ACT.Sigmoid).then_inc(proj_act, 1)
            for i in (1, 3, 5):
                act.wait_ge(pt_psum, i + 1)
                dst = (PT0[:, 2 * i:2 * i + 2, :] if i < 4 else PT1[:, 4 * (i - 4):4 * (i - 4) + 4, :])
                act.activation(dst.rearrange("p h t -> p (h t)"), ps[2 + i][:, :], ACT.Copy).then_inc(pt_act, 1)
            for tt in range(TT):
                act.wait_ge(h1T_psum, 2 * tt + 2)
                act.activation(h1T[:, 4:8, tt * P:(tt + 1) * P], ps[2 * tt + 1][:, :].rearrange("p (k t) -> p k t", k=4), ACT.Copy).then_inc(h1T_act, 1)
                act.wait_ge(top_ready, tt + 1)
                act.activation(ex[:, tt, 0:TOPK], top[:, tt, 0:TOPK], ACT.Exp, bias=topf[:, tt, 7:8],
                               accum_out=ex[:, tt, 4:5]).then_inc(topexp, 1)
            act.wait_ge(gdT_psum, 2)
            act.activation(GdT, psB[:, 256:512], ACT.Copy).then_inc(gdT_ready, 1)
            for i, bank in ((0, psM), (1, psA)):
                act.wait_ge(gather_psum, i + 1)
                act.activation(XT[:, 4 * i:4 * i + 4, :].rearrange("p k c -> p (k c)"), bank[:, :], ACT.Copy).then_inc(xt_ready, 1)

            def pair_work(it):
                for a in range(2):
                    n = it * 2 + a
                    act.wait_ge(xg_ready, n + 1)
                    act.activation(sig, xg, ACT.Sigmoid, scale=SWALPHA).then_inc(sig_ready, 1)
                    if a == 1:
                        act.wait_ge(gather_psum, it * 2 + 3)
                        act.activation(XT[:, 0:4, :].rearrange("p k c -> p (k c)"), psM[:, :], ACT.Copy).then_inc(xt_ready, 1)
                    act.wait_ge(gt_psum, n + 2)
                    act.activation(GTz[0:64, a, 0, :], psY[0:64, 0:256], ACT.Copy).then_inc(gt_ready, 1)
                    act.activation(GTz[64:128, a, 1, :], psY[64:128, 0:256], ACT.Copy).then_inc(gt_ready, 1)
                    act.wait_ge(at_psum, n + 1)
                    act.activation(actT[:, :, :].rearrange("p k c -> p (k c)"), psY[:, :], ACT.Copy).then_inc(at_ready, 1)
                    if a == 1:
                        act.wait_ge(gather_psum, it * 2 + 4)
                        act.activation(XT[:, 4:8, :].rearrange("p k c -> p (k c)"), psA[:, :], ACT.Copy).then_inc(xt_ready, 1)

            with act.Fori(0, PAIRS) as it:
                pair_work(it)
            act.wait_ge(count_ready, 1)
            fullest = act.value_load(cint[0:1, 0:1], min_val=0, max_val=T)
            with act.If(fullest > CAP):
                with act.Fori(1, ROUNDS) as rnd:
                    with act.Fori(0, PAIRS) as pair:
                        pair_work(rnd * PAIRS + pair)
            with act.Else():
                act.nop()

        @block.gpsimd
        def _(pool):
            chain = [0]

            def link(ins):
                chain[0] += 1
                ins.then_inc(pool_chain, 1)
                pool.wait_ge(pool_chain, chain[0])

            norms = [0]

            def inverse_deviation(tt):
                norms[0] += 1
                pool.wait_ge(var_ready, norms[0])
                pool.tensor_tensor(rstd[:, tt:tt + 1], mv[:, tt, 1:2], half_power[:, :], ALU.pow).then_inc(rstd_ready, 1)

            pool.memset(QZ, 0.0).then_inc(qz_zero, 1)
            pool.memset(ones[:, :], 1.0).then_inc(pad_ready, 1)
            link(pool.memset(CT, 0.0))
            link(pool.memset(half_power[:, :], -0.5))
            for tt in range(TT):
                inverse_deviation(tt)
            pool.wait_ge(const_in, 16)
            pool.wait_ge(bc_in, 16)
            for r in range(2):
                for b in range(4):
                    ins = pool.tensor_tensor(BT[:, r, b], bt_raw[:, r, b].unsqueeze(1).to_broadcast([P, 8, NST]),
                                             gmask.unsqueeze(2).to_broadcast([P, 8, NST]), ALU.mult)
                ins.then_inc(bt_ready, 1)
            pool.wait_ge(coef_ready, 1)
            cr = lamw[:, 12, :].unsqueeze(2).to_broadcast([P, ST, GS])
            ci = lamw[:, 13, :].unsqueeze(2).to_broadcast([P, ST, GS])
            for n, (c, co) in enumerate(((0, cr), (1, ci), (0, ci), (1, cr))):
                link(pool.tensor_tensor(ctw[:, n], ct_raw[:, c], co, ALU.mult))
            link(pool.tensor_tensor(ctw[:, 0], ctw[:, 0], ctw[:, 1], ALU.subtract))
            link(pool.tensor_tensor(ctw[:, 2], ctw[:, 2], ctw[:, 3], ALU.add))
            for hf in range(2):
                q, c = slice(64 * hf, 64 * hf + 64), slice(GS * hf, GS * hf + GS)
                link(pool.tensor_copy(CT[q, 0, :, c], ctw[q, 0]))
                ins = pool.tensor_scalar(CT[q, 1, :, c], ctw[q, 2], -1.0, None, ALU.mult)
                if hf == 0:
                    link(ins)
            ins.then_inc(ct_ready, 1)

            pool.wait_ge(pt_psum, 6)
            for r in range(2):
                pool.dma_start(rows[:, r, :], lnrows_d[r:r + 1, :].to_broadcast([P, D])).then_inc(lnin_in, 16)
            pool.memset(bdn[E:2 * E, :], 0.0).then_inc(bdn_zero, 1)
            pool.memset(bdn[2 * E:P, :], 0.0).then_inc(bdn_zero, 1)
            pool.dma_start(bdn[0:E, :], bdn_d).then_inc(bdn_in, 16)
            pool.wait_ge(bdn_zero, 2)
            pool.wait_ge(lnin_in, 32)
            link(pool.tensor_tensor(h[:, :, :], h[:, :, :], rows[:, 0, :].unsqueeze(1).to_broadcast([P, TT, D]), ALU.mult))
            pool.tensor_tensor(h[:, :, :], h[:, :, :], rows[:, 1, :].unsqueeze(1).to_broadcast([P, TT, D]), ALU.add).then_inc(h_ready, 1)
            pool.wait_ge(h_ready, 1)
            for r in range(2):
                pool.dma_start(rows[:, r, :], lnrows_d[2 + r:3 + r, :].to_broadcast([P, D])).then_inc(ln1_in, 16)
            pool.wait_ge(proj_done, G_END)
            pool.dma_start(rw, router_w.rearrange("(k p) e -> p k e", p=P)).then_inc(rw_in, 16)
            for tt in range(TT):
                inverse_deviation(tt)
            pool.wait_ge(ln1_done, TT)
            pool.wait_ge(logit_psum, TT)
            pool.memset(Gd, 0.0).then_inc(gd_zero, 1)
            pool.dma_start(bgu, bgu_d).then_inc(bgu_in, 16)
            pool.wait_ge(gdT_used, 4)
            pool.memset(GTz, 0.0).then_inc(gtz_zero, 1)
            for r in range(2):
                pool.dma_start(ln2_rows[r], lnrows_d[4 + r:5 + r, :].to_broadcast([P, D])).then_inc(ln2_in, 16)

            def pair_work(it, pair):
                for a in range(2):
                    n, e = it * 2 + a, pair * 2 + a
                    pool.wait_ge(gu_done, n + 1)
                    picked = ident.rearrange("p (q e) -> p q e", q=4)[:, :, bass.ds(e, 1)].to_broadcast([P, 4, CAP])
                    pool.tensor_tensor(sel4[a], picked, ones[:, 0:CAP].unsqueeze(1).to_broadcast([P, 4, CAP]), ALU.mult).then_inc(sel_ready, 1)

            with pool.Fori(0, PAIRS) as it:
                pair_work(it, it)
            pool.wait_ge(count_ready, 1)
            fullest = pool.value_load(cint[0:1, 0:1], min_val=0, max_val=T)
            with pool.If(fullest > CAP):
                with pool.Fori(1, ROUNDS) as rnd:
                    with pool.Fori(0, PAIRS) as pair:
                        pair_work(rnd * PAIRS + pair, pair)
            with pool.Else():
                pool.nop()
            for tt in range(TT):
                inverse_deviation(tt)

        @block.vector
        def _(dve):
            chain = [0]

            def link(ins):
                chain[0] += 1
                ins.then_inc(vec_chain, 1)
                dve.wait_ge(vec_chain, chain[0])

            norms = [0]

            def norm_rows(tt, signal, gain=None, shift=None, halves=None):
                halves = halves or [h[:, tt, i * 512:(i + 1) * 512] for i in range(2)]
                for i in range(2):
                    if signal is ln1_done:
                        dve.wait_ge(wo_done, 2 * tt + i + 1)
                        link(dve.scalar_tensor_tensor(out=halves[i], in0=halves[i], scalar=ALPHA, in1=ps[4 + 2 * tt + i][:, :],
                                                      op0=ALU.mult, op1=ALU.add))
                    chain[0] += 1
                    dve.bn_stats(stat[:, tt, i, :], halves[i]).then_inc(vec_chain, 1)
                dve.wait_ge(vec_chain, chain[0])
                norms[0] += 1
                link(dve.bn_aggr(mv[:, tt, :], stat[:, tt, :, :].rearrange("p a b -> p (a b)")))
                dve.tensor_scalar(mv[:, tt, 1:2], mv[:, tt, 1:2], EPS, None, ALU.add).then_inc(var_ready, 1)
                if gain is None:
                    dve.wait_ge(rstd_ready, norms[0])
                    dve.tensor_scalar(h[:, tt, :], h[:, tt, :], mv[:, tt, 0:1], rstd[:, tt:tt + 1], ALU.subtract, ALU.mult).then_inc(signal, 1)
                else:
                    for i in range(2):
                        v = slice(512 * i, 512 * i + 512)
                        chain[0] += 1
                        dve.scalar_tensor_tensor(out=h[:, tt, v], in0=halves[i], scalar=mv[:, tt, 0:1], in1=gain[:, v],
                                                 op0=ALU.subtract, op1=ALU.mult).then_inc(vec_chain, 1)
                    dve.wait_ge(vec_chain, chain[0])
                    dve.wait_ge(rstd_ready, norms[0])
                    dve.scalar_tensor_tensor(out=h[:, tt, :], in0=h[:, tt, :], scalar=rstd[:, tt:tt + 1], in1=shift, op0=ALU.mult, op1=ALU.add).then_inc(signal, 1)

            for tt in range(TT):
                dve.wait_ge(x_in[tt], 16)
                norm_rows(tt, xhat_ready)

            L = lambda i: lamw[:, i, :]
            lre, lim = cols[:, C_RE:C_RE + ST], cols[:, C_IM:C_IM + ST]
            dve.wait_ge(cols_in, 16)
            dve.wait_ge(dt_ready, 1)
            dve.tensor_tensor(L(1), lre, L(0), ALU.mult).then_inc(lam_ready, 1)
            link(dve.tensor_tensor(L(2), lim, L(0), ALU.mult))
            link(dve.tensor_scalar(L(3), L(2), INV_2PI, None, ALU.mult))
            link(dve.tensor_scalar(L(4), L(3), MAGIC, -MAGIC, ALU.add, ALU.add))
            dve.tensor_tensor(turn[:, :], L(3), L(4), ALU.subtract).then_inc(turn_ready, 1)
            dve.wait_ge(turn_ready, 1)

            for k in (2, 3, 6, 7):
                dve.wait_ge(hT_psum, k // 2 + 1)
                dve.tensor_scalar(hT[:, k, :], ps[4 + k // 2][:, (k % 2) * T:(k % 2) * T + T], cols[:, C_G + k:C_G + k + 1],
                                  cols[:, C_B + k:C_B + k + 1], ALU.mult, ALU.add).then_inc(hT_vec, 1)

            def phases(b):
                ang = sinT[:, b]
                if b == 0:
                    dve.wait_ge(const_in, 16)
                link(dve.tensor_tensor(ang, times.unsqueeze(1).to_broadcast([P, 4, T]),
                                       turn[:, 4 * b:4 * b + 4].unsqueeze(2).to_broadcast([P, 4, T]), ALU.mult))
                link(dve.tensor_scalar(tmp, ang, MAGIC, -MAGIC, ALU.add, ALU.add))
                dve.tensor_tensor(ang, ang, tmp, ALU.subtract).then_inc(ang_ready, 1)
                dve.wait_ge(ang_ready, b + 1)

            phases(0)
            phases(1)
            dve.wait_ge(sin_ready, 2)
            dve.wait_ge(decay_ready, 1)
            link(dve.tensor_tensor(L(7), L(6), L(6), ALU.mult))
            link(dve.tensor_scalar(L(7), L(7), -2.0, 1.0, ALU.mult, ALU.add))
            link(dve.tensor_tensor(L(8), decay[:, :], L(7), ALU.mult))
            link(dve.tensor_scalar(L(8), L(8), 1.0, None, ALU.subtract))
            link(dve.tensor_tensor(L(9), decay[:, :], L(5), ALU.mult))
            link(dve.tensor_tensor(L(10), lre, lre, ALU.mult))
            link(dve.tensor_tensor(L(11), lim, lim, ALU.mult))
            link(dve.tensor_tensor(L(10), L(10), L(11), ALU.add))
            link(dve.reciprocal(L(10), L(10)))
            for o, (a1, b1, a2, b2, op) in ((12, (8, lre, 9, lim, ALU.add)), (13, (9, lre, 8, lim, ALU.subtract))):
                link(dve.tensor_tensor(L(14), L(a1), b1, ALU.mult))
                link(dve.tensor_tensor(L(15), L(a2), b2, ALU.mult))
                link(dve.tensor_tensor(L(14), L(14), L(15), op))
                ins = dve.tensor_tensor(L(o), L(14), L(10), ALU.mult)
                if o == 12:
                    link(ins)
            ins.then_inc(coef_ready, 1)

            def ssm_block(b):
                dve.wait_ge(table_ready, b + 1)
                dve.wait_ge(bu_psum, b + 1)
                cs, sn = cosT[:, b], sinT[:, b]
                for j in range(2):
                    re = ps[2 + j][:, :].rearrange("p (i t) -> p i t", i=2)
                    im = ps[4 + j][:, :].rearrange("p (i t) -> p i t", i=2)
                    v = slice(2 * j, 2 * j + 2)
                    chain[0] += 4
                    dve.tensor_tensor(z_re[:, v], re, cs[:, v], ALU.mult).then_inc(vec_chain, 1)
                    dve.tensor_tensor(tmp[:, v], im, sn[:, v], ALU.mult).then_inc(vec_chain, 1)
                    dve.tensor_tensor(z_im[:, v], im, cs[:, v], ALU.mult).then_inc(vec_chain, 1)
                    dve.wait_ge(vec_chain, chain[0] - 1)
                    dve.tensor_tensor(z_re[:, v], z_re[:, v], tmp[:, v], ALU.add).then_inc(vec_chain, 1)
                    dve.wait_ge(vec_chain, chain[0])
                    dve.tensor_tensor(tmp[:, v], re, sn[:, v], ALU.mult).then_inc(bu_used, 1)
                    dve.wait_ge(bu_used, 2 * b + j + 1)
                    link(dve.tensor_tensor(z_im[:, v], z_im[:, v], tmp[:, v], ALU.subtract))
                for zz in (z_re, z_im):
                    for i in range(4):
                        n = 4 * b + i
                        dve.tensor_tensor_scan(zz[:, i], decay[:, n:n + 1].to_broadcast([P, T]), zz[:, i], 0.0,
                                               ALU.mult, ALU.add).then_inc(vec_chain, 1)
                        chain[0] += 1
                dve.wait_ge(vec_chain, chain[0])
                if b >= 1:
                    dve.wait_ge(y_psum, b)
                chain[0] += 2
                dve.tensor_tensor(s_re, z_re, cs, ALU.mult).then_inc(vec_chain, 1)
                dve.tensor_tensor(tmp, z_im, sn, ALU.mult).then_inc(vec_chain, 1)
                dve.wait_ge(vec_chain, chain[0])
                link(dve.tensor_tensor(s_re, s_re, tmp, ALU.subtract))
                chain[0] += 2
                dve.tensor_tensor(s_im, z_re, sn, ALU.mult).then_inc(vec_chain, 1)
                dve.tensor_tensor(tmp, z_im, cs, ALU.mult).then_inc(vec_chain, 1)
                dve.wait_ge(vec_chain, chain[0])
                dve.tensor_tensor(s_im, s_im, tmp, ALU.add).then_inc(s_ready, 1)
                dve.wait_ge(s_ready, b + 1)

            def y_block(b):
                dve.wait_ge(y_psum, b + 1)
                dve.scalar_tensor_tensor(out=uT[:, b, :], in0=uT[:, b, :], scalar=cols[:, C_D + b:C_D + b + 1],
                                         in1=ps[6 + b // 2][:, (b % 2) * 256:(b % 2) * 256 + 256], op0=ALU.mult, op1=ALU.add).then_inc(y_used, 1)

            ssm_block(0)
            phases(2)
            ssm_block(1)
            y_block(0)
            phases(3)
            ssm_block(2)
            y_block(1)
            ssm_block(3)
            y_block(2)
            y_block(3)
            dve.wait_ge(y_used, 4)
            link(dve.tensor_tensor(gel, uT, uT, ALU.mult))
            link(dve.tensor_scalar(gel, gel, GELU_A, 1.0, ALU.mult, ALU.add))
            dve.tensor_tensor(gel, gel, uT, ALU.mult).then_inc(gelu_arg, 1)

            dve.wait_ge(relb_in, 32)
            link(dve.memset(S1[0:64, :, 192:256], -1e30))
            link(dve.memset(S0[0:64, :, 64:128], -1e30))
            for a, Sx in ((1, S1), (0, S0)):
                for c in range(2):
                    nk = CHUNK * (2 * a + c + 1)
                    q = slice(64 * c, 64 * c + 64)
                    rev = slice(nk - 1, None, -1)
                    for half in range(2 * (a + 1)):
                        dve.wait_ge(score_psum, 4 * (1 - a) + half + 1 if a else 4 + half + 1)
                        hs = 2 if a else 4
                        hh = slice(hs * half, hs * half + hs)
                        src = ps[2 + half] if a else ps[6 + half]
                        src = src[q, :].rearrange("p (h k) -> p h k", h=hs)[:, :, 0:nk]
                        dve.tensor_tensor(Sx[q, hh, 0:nk], src, relb[q, hh, rev], ALU.add).then_inc(score_used, 1)
            dve.wait_ge(score_used, 12)
            for a, Sx in ((0, S0), (1, S1)):
                link(dve.tensor_reduce(negmax[:, a, :], Sx, AX_X, ALU.max))
            dve.tensor_scalar(negmax[:, :, :], negmax[:, :, :], -1.0, None, ALU.mult).then_inc(max_ready, 1)
            dve.wait_ge(gelu_sig, 1)
            dve.tensor_tensor(uT, uT, gel, ALU.mult).then_inc(gelu_ready, 1)
            for i in range(4):
                g = G_GLU + 2 * i + 1
                dve.wait_ge(proj_done, g + 1)
                dve.wait_ge(proj_act, G_GLU + i + 1)
                dve.tensor_tensor(ssmT[:, i, :], bank_of(g), tmpg[i], ALU.mult).then_inc(proj_vec, 1)
            dve.wait_ge(exp_done, 2 * HEADS)
            link(dve.reciprocal(psums[:, :, :], psums[:, :, :]))
            for a, Sx in ((0, S0), (1, S1)):
                dve.tensor_tensor(Sx, Sx, psums[:, a, :].unsqueeze(2).to_broadcast([P, HEADS, P * (a + 1)]), ALU.mult).then_inc(p_norm, 1)

            dve.wait_ge(proj_act, G_GLU + 4)

            def gated_ssm(n):
                dve.wait_ge(proj_done, G_US + n + 1)
                dve.tensor_tensor(mixT[:, n, :], bank_of(G_US + n), gatesT[:, 8 + n, :], ALU.mult).then_inc(proj_vec, 1)

            for n in range(4):
                gated_ssm(n)
            for i in (0, 2, 4):
                dve.wait_ge(pt_psum, i + 1)
                dst = (PT0[:, 2 * i:2 * i + 2, :] if i < 4 else PT1[:, 4 * (i - 4):4 * (i - 4) + 4, :])
                dve.tensor_copy(dst.rearrange("p h t -> p (h t)"), ps[2 + i][:, :]).then_inc(pt_vec, 1)
            gated_ssm(4)
            gated_ssm(5)
            for i in range(2):
                dve.wait_ge(pv_psum, i + 1)
                dve.tensor_copy(attnT[:, 2 * i:2 * i + 2, :].rearrange("p j t -> p (j t)"), ps[2 + i][:, :]).then_inc(attn_ready, 1)
            gated_ssm(6)
            gated_ssm(7)
            for n in range(8):
                dve.wait_ge(proj_done, G_UA + n + 1)
                if n >= 2:
                    dve.wait_ge(mix_ready, n - 1)
                dve.tensor_tensor(gel[:, n % 2, :], bank_of(G_UA + n), gatesT[:, n, :], ALU.mult).then_inc(proj_vec, 1)
                dve.wait_ge(proj_vec, 4 + 8 + n + 1)
                dve.tensor_tensor(mixT[:, n, :], mixT[:, n, :], gel[:, n % 2, :], ALU.add).then_inc(mix_ready, 1)

            dve.wait_ge(h_ready, 1)
            dve.wait_ge(ln1_in, 32)
            def new_h(tt):
                norm_rows(tt, ln1_done, rows[:, 0, :], rows[:, 1, :])
                dve.wait_ge(ln1_done, tt + 1)
                dve.wait_ge(h1T_psum, 2 * tt + 1)
                dve.tensor_copy(h1T[:, 0:4, tt * P:(tt + 1) * P], ps[2 * tt][:, :].rearrange("p (k t) -> p k t", k=4)).then_inc(h1T_vec, 1)

            iota_e = times[:, 0:E].unsqueeze(1).to_broadcast([P, TOPK, E])

            def choose(a):
                dve.wait_ge(logit_psum, a + 1)
                link(dve.tensor_tensor(logits[:, a, :], ps[4 + a][:, 0:E], rwb[:, :], ALU.add))
                link(dve.max(top[:, a, :], logits[:, a, :]))
                link(dve.max_index(topi[:, a, :], top[:, a, :], logits[:, a, :]))
                chain[0] += 1
                dve.tensor_copy(topf[:, a, 0:7], topi[:, a, 0:7]).then_inc(vec_chain, 1)
                dve.tensor_scalar(topf[:, a, 7:8], top[:, a, 0:1], -1.0, None, ALU.mult).then_inc(top_ready, 1)
                dve.wait_ge(vec_chain, chain[0])
                link(dve.tensor_tensor(oneh[:, a], iota_e, topf[:, a, 0:TOPK].unsqueeze(2).to_broadcast([P, TOPK, E]), ALU.is_equal))
                dve.tensor_reduce(mask[:, a, :], oneh[:, a].rearrange("p k e -> p e k"), AX_X, ALU.add).then_inc(mask_ready, 1)

            def gates(a):
                dve.wait_ge(topexp, a + 1)
                link(dve.reciprocal(ex[:, a, 5:6], ex[:, a, 4:5]))
                link(dve.tensor_scalar(ex[:, a, 0:TOPK], ex[:, a, 0:TOPK], ex[:, a, 5:6], None, ALU.mult))
                link(dve.tensor_tensor(oneg[:, a], oneh[:, a], ex[:, a, 0:TOPK].unsqueeze(2).to_broadcast([P, TOPK, E]), ALU.mult))

            new_h(0)
            dve.wait_ge(rb_in, 16)
            choose(0)
            gates(0)
            new_h(1)
            choose(1)
            gates(1)
            dve.wait_ge(gd_zero, 1)
            for a in range(TT):
                dve.tensor_reduce(Gd[:, a, 0:E], oneg[:, a].rearrange("p k e -> p e k"), AX_X, ALU.add).then_inc(gd_ready, 1)
            dve.wait_ge(mask_ready, TT)
            dve.wait_ge(pos_psum, 1)
            for a in range(TT):
                chain[0] += 1
                dve.scalar_tensor_tensor(out=logits[:, a, :], in0=mask[:, a, :], scalar=FAR,
                                         in1=ps[6][:, a * E:(a + 1) * E], op0=ALU.mult, op1=ALU.add).then_inc(vec_chain, 1)
            dve.wait_ge(vec_chain, chain[0])
            link(dve.tensor_scalar(posx[:, :, 0:E], logits[:, :, :], -FAR, None, ALU.add))

            def next_rows(it_next):
                for tt in range(TT):
                    for a in range(2):
                        where = posx[:, tt, bass.ds(it_next * 2 + a, 1)]
                        dve.tensor_scalar(Pm[:, tt, CAP * a:CAP * a + CAP], slots[:, 0:CAP], where, None, ALU.is_equal).then_inc(p_ready, 1)

            for tt in range(TT):
                for a in range(2):
                    dve.tensor_scalar(Pm[:, tt, CAP * a:CAP * a + CAP], slots[:, 0:CAP], posx[:, tt, a:a + 1], None, ALU.is_equal).then_inc(p_ready, 1)
            link(dve.tensor_reduce(cmax[:, :], ps[6][:, 2 * E:3 * E], AX_X, ALU.max))
            dve.tensor_copy(cint[:, :], cmax[:, :]).then_inc(count_ready, 1)
            for r in range(1, ROUNDS):
                dve.tensor_scalar(posx[:, :, r * E:(r + 1) * E], logits[:, :, :], -FAR - CAP * r, None, ALU.add).then_inc(slots_ready, 1)
            dve.wait_ge(gd_ready, TT)
            for r in range(ROUNDS):
                dve.tensor_copy(gx[:, :, r * E:(r + 1) * E], Gd[:, :, 0:E]).then_inc(slots_ready, 1)
            dve.memset(posx[:, :, ROUNDS * E:], -FAR).then_inc(slots_ready, 1)
            dve.wait_ge(slots_ready, 2 * ROUNDS)
            dve.wait_ge(count_ready, 1)
            dve.memset(cmax[:, :], 0.0).then_inc(ab_free, 1)

            def pair_work(it):
                for a in range(2):
                    n = it * 2 + a
                    dve.wait_ge(gt_psum, n + 1)
                    for tt in range(TT):
                        dve.tensor_scalar(PG[:, tt, :], slots, posx[:, tt, bass.ds(n, 1)], gx[:, tt, bass.ds(n, 1)],
                                          ALU.is_equal, ALU.mult).then_inc(pg_ready, 1)
                    if a == 0:
                        dve.wait_ge(gather_psum, it * 2 + 2)
                        next_rows(it + 1)
                    dve.wait_ge(gu_done, n + 3)
                    dve.tensor_scalar(xg, psA[:, :], LIMIT, None, ALU.min).then_inc(xg_ready, 1)
                    dve.tensor_scalar(xl, psB[:, :], LIMIT, -LIMIT, ALU.min, ALU.max).then_inc(ab_free, 1)
                    dve.wait_ge(xg_ready, n + 1)
                    dve.wait_ge(ab_free, n + 2)
                    dve.scalar_tensor_tensor(out=xl, in0=xl, scalar=1.0, in1=xg, op0=ALU.add, op1=ALU.mult).then_inc(lin_ready, 1)
                    dve.wait_ge(lin_ready, n + 1)
                    dve.wait_ge(sig_ready, n + 1)
                    dve.tensor_tensor(xl, xl, sig, ALU.mult).then_inc(act_ready, 1)
                    dve.wait_ge(dn_used, n * 4 + 4)
                    dve.tensor_copy(ysb, psY[:, :]).then_inc(y_ready, 1)

            with dve.Fori(0, PAIRS) as it:
                pair_work(it)
            fullest = dve.value_load(cint[0:1, 0:1], min_val=0, max_val=T)
            with dve.If(fullest > CAP):
                with dve.Fori(1, ROUNDS) as rnd:
                    with dve.Fori(0, PAIRS) as pair:
                        pair_work(rnd * PAIRS + pair)
                dve.wait_ge(combined, 2 * E * ROUNDS)
            with dve.Else():
                dve.nop()

            dve.wait_ge(ln2_in, 32)
            for tt in range(TT):
                dve.wait_ge(combined, 2 * E - 1 + tt)
                norm_rows(tt, out_ready, ln2_rows[0], ln2_rows[1], [ps[2 * tt + i][:, :] for i in range(2)])

        @block.tensor
        def _(pe):
            pe.wait_ge(const_in, 16)
            for tt in range(TT):
                pe.wait_ge(xhat_ready, tt + 1)
                for k in range(KD):
                    c = (k % 2) * 256 + tt * P
                    ins = pe.transpose(ps[4 + k // 2][:, c:c + P], h[:, tt, k * P:(k + 1) * P], ident)
                    if tt == TT - 1 and k % 2:
                        ins.then_inc(hT_psum, 1)
            pe.wait_ge(hT_act, KD // 2)
            pe.wait_ge(hT_vec, KD // 2)

            def project(g, blk, nk, lhs, rhs):
                if g in (0, G_Q, G_K, G_V, G_GATE, G_GATE + 4, G_GATE + 8, G_GATE + 12, G_GLU, G_US, G_UA):
                    pe.wait_ge(w_loaded[blk % 4], 32 * (blk // 4 + 1))
                if g >= 2:
                    pe.wait_ge(*group_read(g - 2))
                for k in range(nk):
                    ins = pe.matmul(bank_of(g), lhs(k), rhs(k), start=(k == 0), stop=(k == nk - 1))
                ins.then_inc(proj_done, 1)

            def from_h(g0, blk):
                wv = stream[blk % 4].rearrange("p (k n) -> p k n", k=KD)
                for j in range(4):
                    if g0 == G_V:
                        a, c = divmod(j, 2)
                        project(g0 + j, blk, KD, lambda k: hT[:, k, a * P:(a + 1) * P], lambda k: wv[:, k, c * 256:(c + 1) * 256])
                    else:
                        project(g0 + j, blk, KD, lambda k: wv[:, k, j * P:(j + 1) * P], lambda k: hT[:, k, :])

            def inputs_of_states(b):
                if b == 0:
                    pe.wait_ge(bt_ready, 2)
                    pe.wait_ge(proj_act, 4)
                else:
                    pe.wait_ge(bu_used, 2 * b)
                for r in range(2):
                    for i in range(4):
                        ins = pe.matmul(ps[2 + 2 * r + i // 2][:, (i % 2) * 256:(i % 2) * 256 + 256],
                                        BT[:, r, b, 2 * i:2 * i + 2, :].rearrange("p m s -> p (m s)"), uT[:, b, :], start=True, stop=True)
                ins.then_inc(bu_psum, 1)

            def outputs_of_states(b):
                pe.wait_ge(s_ready, b + 1)
                if b % 2:
                    pe.wait_ge(y_used, b)
                if b == 0:
                    pe.wait_ge(ct_ready, 1)
                for r, s in ((0, s_re), (1, s_im)):
                    for i in range(4):
                        ins = pe.matmul(ps[6 + b // 2][32 * i:32 * i + 32, (b % 2) * 256:(b % 2) * 256 + 256],
                                        CT[:, r, 4 * b + i, :], s[:, i, :], start=(r == 0), stop=(r == 1), skip_group_check=True)
                ins.then_inc(y_psum, 1)

            from_h(G_U, 0)
            inputs_of_states(0)
            from_h(G_Q, 1)
            inputs_of_states(1)
            from_h(G_K, 2)
            outputs_of_states(0)
            from_h(G_V, 3)
            inputs_of_states(2)
            from_h(G_GATE, 4)
            outputs_of_states(1)
            inputs_of_states(3)
            from_h(G_GATE + 4, 5)
            outputs_of_states(2)
            from_h(G_GATE + 8, 6)
            outputs_of_states(3)

            pe.wait_ge(bu_used, 8)
            for half in range(4):
                for hd in range(2 * half, 2 * half + 2):
                    ins = pe.matmul(ps[2 + half][:, (hd % 2) * 256:(hd % 2) * 256 + 256], QZ[:, hd, P:2 * P], KT[:, hd // 2, :], start=True, stop=True)
                ins.then_inc(score_psum, 1)
            pe.wait_ge(y_used, 4)
            for half in range(2):
                for hd in range(4 * half, 4 * half + 4):
                    ins = pe.matmul(ps[6 + half][:, (hd % 4) * P:(hd % 4) * P + P], QZ[:, hd, 0:P], KT[:, hd // 2, 0:P], start=True, stop=True)
                ins.then_inc(score_psum, 1)
            from_h(G_GATE + 12, 7)

            wg = stream[8 % 4].rearrange("p (k n) -> p k n", k=KA)
            pe.wait_ge(gelu_ready, 1)
            for i in range(4):
                for g, c in ((G_GLU + 2 * i, AW + i * P), (G_GLU + 2 * i + 1, i * P)):
                    project(g, 8, KA, lambda k: wg[:, k, c:c + P], lambda k: uT[:, k, :])

            wu = stream[9 % 4].rearrange("p (k n) -> p k n", k=KA)

            def up_ssm(n):
                project(G_US + n, 9, KA, lambda k: wu[:, k, n * P:(n + 1) * P], lambda k: ssmT[:, k, :])

            pe.wait_ge(proj_vec, 4)
            for n in range(4):
                up_ssm(n)
            pe.wait_ge(p_norm, 2)
            for i in range(4):
                for hd in (2 * i, 2 * i + 1):
                    c = (hd % 2) * 256
                    pe.transpose(ps[2 + i][:, c:c + P], S0[:, hd, :], ident)
                    ins = pe.transpose(ps[2 + i][:, c + P:c + 2 * P], S1[:, hd, 0:P], ident)
                ins.then_inc(pt_psum, 1)
            for i in range(2):
                for hd in range(4 * i, 4 * i + 4):
                    ins = pe.transpose(ps[6 + i][:, (hd % 4) * P:(hd % 4) * P + P], S1[:, hd, P:2 * P], ident)
                ins.then_inc(pt_psum, 1)
            up_ssm(4)
            up_ssm(5)
            pe.wait_ge(pt_act, 3)
            pe.wait_ge(pt_vec, 3)
            for j in range(4):
                for hd in (2 * j, 2 * j + 1):
                    q = slice(64 * (hd % 2), 64 * (hd % 2) + 64)
                    o = ps[2 + j // 2][q, (j % 2) * 256:(j % 2) * 256 + 256]
                    pe.matmul(o, V[:, 0, hd * HD:(hd + 1) * HD], PT0[:, hd, :], start=True, stop=False, skip_group_check=True)
                    ins = pe.matmul(o[:, P:2 * P], V[:, 1, hd * HD:(hd + 1) * HD], PT1[:, hd, :], start=False, stop=True, skip_group_check=True)
                if j % 2:
                    ins.then_inc(pv_psum, 1)
            up_ssm(6)
            up_ssm(7)
            pe.wait_ge(attn_ready, 2)
            wa = stream[10 % 4].rearrange("p (k n) -> p k n", k=KA)
            for n in range(8):
                project(G_UA + n, 10, KA, lambda k: wa[:, k, n * P:(n + 1) * P], lambda k: attnT[:, k, :])
            def out_projection(tt, hf, ks=range(KD)):
                blk = B_WO + hf
                pe.wait_ge(w_loaded[blk % 4], 32 * (blk // 4 + 1))
                wo = stream[blk % 4].rearrange("p (k n) -> p k n", k=KD)
                for k in ks:
                    ins = pe.matmul(ps[4 + 2 * tt + hf][:, :], mixT[:, k, tt * P:(tt + 1) * P], wo[:, k, :], start=(k == 0), stop=(k == KD - 1))
                if k == KD - 1:
                    ins.then_inc(wo_done, 1)

            def transpose_h1(tt):
                pe.wait_ge(ln1_done, tt + 1)
                for k in range(KD):
                    ins = pe.transpose(ps[2 * tt + k // 4][:, (k % 4) * P:(k % 4) * P + P], h[:, tt, k * P:(k + 1) * P], ident)
                    if k % 4 == 3:
                        ins.then_inc(h1T_psum, 1)

            def route(tt):
                pe.wait_ge(h1T_act, tt + 1)
                pe.wait_ge(h1T_vec, tt + 1)
                for k in range(KD):
                    ins = pe.matmul(ps[4 + tt][:, 0:E], h1T[:, k, tt * P:(tt + 1) * P], rw[:, k, :], start=(k == 0), stop=(k == KD - 1))
                ins.then_inc(logit_psum, 1)

            pe.wait_ge(mix_ready, KD)
            out_projection(0, 0)
            out_projection(0, 1)
            out_projection(1, 0)
            transpose_h1(0)
            out_projection(1, 1, range(4))
            pe.wait_ge(rw_in, 16)
            route(0)
            out_projection(1, 1, range(4, KD))
            transpose_h1(1)
            route(1)
            for tt in range(TT):
                for hf in range(2):
                    pe.matmul(ps[2 * tt + hf][:, :], alpha_id, h[:, tt, hf * 512:(hf + 1) * 512], start=True, stop=False, skip_group_check=True)
            pe.wait_ge(mask_ready, TT)
            pe.wait_ge(pad_ready, 1)
            pe.matmul(ps[6][:, 0:E], upper, mask[:, 0, :], start=True, stop=True)
            pe.matmul(ps[6][:, E:2 * E], ones[:, :], mask[:, 0, :], start=True, stop=False)
            pe.matmul(ps[6][:, E:2 * E], upper, mask[:, 1, :], start=False, stop=True)
            pe.matmul(ps[6][:, 2 * E:3 * E], ones[:, :], mask[:, 0, :], start=True, stop=False)
            pe.matmul(ps[6][:, 2 * E:3 * E], ones[:, :], mask[:, 1, :], start=False, stop=True).then_inc(pos_psum, 1)
            def gather(i, bank):
                for k in range(4 * i, 4 * i + 4):
                    for tt in range(TT):
                        ins = pe.matmul(bank[:, (k % 4) * P:(k % 4) * P + P], h[:, tt, k * P:(k + 1) * P], Pm[:, tt, :],
                                        start=(tt == 0), stop=(tt == TT - 1), skip_group_check=True)
                ins.then_inc(gather_psum, 1)

            pe.wait_ge(gd_ready, TT)
            for tt in range(TT):
                pe.transpose(psB[:, 256 + tt * P:256 + (tt + 1) * P], Gd[:, tt, :], ident).then_inc(gdT_psum, 1)
            pe.wait_ge(p_ready, 4)
            gather(0, psM)
            gather(1, psA)
            pe.wait_ge(gdT_ready, 1)
            pe.wait_ge(bdn_in, 16)
            pe.wait_ge(bdn_zero, 2)
            for tt in range(TT):
                for hf in range(2):
                    pe.matmul(ps[2 * tt + hf][:, :], GdT[:, tt * P:(tt + 1) * P], bdn[:, hf * 512:(hf + 1) * 512],
                              start=False, stop=False, skip_group_check=True).then_inc(gdT_used, 1)
            pe.sem_inc(gu_done, 2)
            pe.sem_inc(gt_psum, 1)
            pe.wait_ge(bgu_in, 16)
            pe.wait_ge(gtz_zero, 1)

            def combine(a, n):
                pe.wait_ge(y_ready, n + 1)
                pe.wait_ge(gt_ready, n * 2 + 2)
                for tt in range(TT):
                    for hf in range(2):
                        ins = pe.matmul(ps[2 * tt + hf][:, :], GTz[:, a, hf, tt * P:(tt + 1) * P], ysb, start=False, stop=False, skip_group_check=True)
                    ins.then_inc(combined, 1)

            def pair_work(it):
                for a in range(2):
                    n = it * 2 + a
                    if a == 0:
                        pe.wait_ge(xt_ready, it * 2 + 2)
                    pe.wait_ge(ab_free, n + 1)
                    for i, k in enumerate(K_ORDER):
                        pe.wait_ge(gu_loaded[a][k], it * 16 + 16)
                        for q in range(4):
                            bank, hf = (psA, psB)[q // 2], q % 2
                            ins = pe.matmul(bank[64 * hf:64 * hf + 64, :], XT[:, k, CAP * a:CAP * a + CAP], gu_ring[:, a, k, q * 512:(q + 1) * 512],
                                            start=(i == 0), stop=False, skip_group_check=True)
                        ins.then_inc(gu_used, 1)
                    pe.wait_ge(sel_ready, n + 1)
                    for q in range(4):
                        bank, hf = (psA, psB)[q // 2], q % 2
                        ins = pe.matmul(bank[64 * hf:64 * hf + 64, :], sel4[a][:, q, :], bgu, start=False, stop=True, skip_group_check=True)
                    ins.then_inc(gu_done, 1)
                    if a == 1:
                        combine(0, n - 1)
                    pe.wait_ge(pg_ready, n * 2 + 2)
                    for tt in range(TT):
                        ins = pe.transpose(psY[:, tt * P:(tt + 1) * P], PG[:, tt, :], ident)
                    ins.then_inc(gt_psum, 1)
                    if a == 0:
                        pe.wait_ge(p_ready, it * 4 + 8)
                        pe.wait_ge(xt_ready, it * 2 + 2)
                        gather(0, psM)
                    pe.wait_ge(act_ready, n + 1)
                    pe.wait_ge(gt_ready, n * 2 + 2)
                    for j in range(4):
                        ins = pe.transpose(psY[:, j * P:(j + 1) * P], xl[:, j * P:(j + 1) * P], ident)
                    ins.then_inc(at_psum, 1)
                    if a == 1:
                        gather(1, psA)
                    pe.wait_ge(at_ready, n + 1)
                    for i, j in enumerate(J_ORDER):
                        pe.wait_ge(dn_loaded[j], n * 16 + 16)
                        for k in (2 * j, 2 * j + 1):
                            for hf in range(2):
                                ins = pe.matmul(psY[64 * hf:64 * hf + 64, :], actT[:, k % 4, CAP * (k // 4):CAP * (k // 4) + CAP],
                                                dn_ring[:, k, hf * 512:(hf + 1) * 512], start=(i == 0 and k % 2 == 0), stop=(i == 3 and k % 2 == 1), skip_group_check=True)
                        ins.then_inc(dn_used, 1)
                    if a == 1:
                        combine(1, n)

            with pe.Fori(0, PAIRS) as it:
                pair_work(it)
            fullest = pe.value_load(cint[0:1, 0:1], min_val=0, max_val=T)
            with pe.If(fullest > CAP):
                with pe.Fori(1, ROUNDS) as rnd:
                    with pe.Fori(0, PAIRS) as pair:
                        pair_work(rnd * PAIRS + pair)
            with pe.Else():
                pe.nop()


def _consts():
    c = np.zeros((P, O_END), np.float32)
    c[:, O_ID:O_ID + 128] = np.eye(P)
    c[:, O_ALPHA:O_ALPHA + 128] = np.eye(P) * ALPHA
    c[:, O_UP:O_UP + 128] = np.triu(np.ones((P, P)), 1)
    c[:, O_SLOT:O_SLOT + 128] = np.tile(np.arange(CAP), 2)[None]
    c[:, O_TIME:O_TIME + 256] = np.arange(T)[None]
    c[np.arange(P), O_MASK + np.arange(P) // GS] = 1
    return c


def kernel(**inputs):
    import concourse.bacc as bacc
    from concourse.bass_utils import run_bass_kernel_spmd

    a = {k: np.asarray(v) for k, v in inputs.items()}

    def by_partition(v):
        return v.reshape(-1, P).T

    def by_state(v):
        return v.reshape(ST, 2 * NST).T

    cols = np.concatenate([
        by_partition(a["ln_in_g"]), by_partition(a["ln_in_b"]), by_partition(a["b_gate"][0]), by_partition(a["ssm_d"][0]),
        by_state(a["lam_re"][0]), by_state(a["lam_im"][0]), by_state(np.repeat(a["log_dt"][0][:, None], NST, axis=1))], axis=1)
    b_l = [a[n][0].reshape(4, 8, NST, GS).transpose(1, 3, 0, 2).reshape(P, -1) for n in ("ssm_b_re", "ssm_b_im")]
    c_l = [a[n][0].reshape(ST, 2, GS, NST).transpose(1, 3, 0, 2).reshape(P, -1) for n in ("ssm_c_re", "ssm_c_im")]
    arrays = {
        "x": a["x"][0], "w_in": a["w_in"][0], "w_glu": a["w_glu"][0], "w_ua": a["w_up_attn"][0], "w_us": a["w_up_ssm"][0],
        "w_o": a["w_o"][0], "w_gu": a["w_gate_up"][0], "w_dn": a["w_down"][0], "rel_bias": a["rel_bias"][0],
        "router_w": a["router_w"][0], "router_b": a["router_b"],
        "cols": cols, "bc": np.concatenate(b_l + c_l, axis=1), "consts": _consts(),
        "lnrows": np.stack([a["ln_in_g"], a["ln_in_b"], a["ln1_g"][0], a["ln1_b"][0], a["ln2_g"][0], a["ln2_b"][0]]),
        "bgu": a["b_gate_up"][0].reshape(E, 4, 512).transpose(1, 0, 2).reshape(P, 512), "bdn": a["b_down"][0],
    }
    nc = bacc.Bacc("TRN2", target_bir_lowering=False, num_devices=1)
    ins, aps = {}, []
    for name, v in arrays.items():
        v = np.ascontiguousarray(v)
        ins[f"in_{name}_dram"] = v
        aps.append(nc.dram_tensor(f"in_{name}_dram", v.shape, mybir.dt.from_np(v.dtype), kind="ExternalInput").ap())
    aps.append(nc.dram_tensor("out_0_dram", (T, D), F32, kind="ExternalOutput").ap())
    trunk_and_moe(nc, *aps)
    r = run_bass_kernel_spmd(nc, [ins], core_ids=[0])
    return r.results[0]["out_0_dram"].reshape(1, T, D)
```

```python
from contextlib import ExitStack

import numpy as np

import concourse.bass as bass
from concourse import mybir

F32 = mybir.dt.float32
I32 = mybir.dt.int32
U32 = mybir.dt.uint32
ALU = mybir.AluOpType
ACT = mybir.ActivationFunctionType
AX_X = mybir.AxisListType.X

P = 128
T = 256
TT = T // P
D = 1024
KD = D // P
AW = 512
KA = AW // P
HEADS, HD = 8, 64
CHUNK = 64
REL = 320
GS = 16
NST = 64
ST = 16
E = 32
TOPK = 4
CAP = 64
ROUNDS = T // CAP
PAIRS = E // 2
LIMIT = 7.0
SWALPHA = 1.702
EPS = 1e-5
ALPHA = 2.0 ** 0.25
MAGIC = 12582912.0
TWO_PI = 6.2831845
INV_2PI = float(1.0 / (2.0 * np.pi))
GELU_A, GELU_C = 0.044715, 0.7978845608028654
FAR = 1000.0
K_ORDER = [2, 3, 4, 5, 6, 7, 1, 0]
J_ORDER = [1, 0, 2, 3]

C_G, C_B, C_GATE, C_D, C_RE, C_IM, C_DT, C_G1, C_B1, C_END = 0, 8, 16, 32, 36, 52, 68, 84, 92, 100
O_ID, O_UP, O_SLOT, O_TIME, O_MASK, O_ALPHA, O_END = 0, 128, 256, 384, 640, 642, 770


def trunk_and_moe(nc, x, w_in, w_glu, w_ua, w_us, w_o, w_gu, w_dn, rel_bias, router_w, router_b,
                  cols_d, bc_d, consts_d, lnrows_d, bgu_d, bdn_d, out):
    with ExitStack() as ctx:
        def sb(name, shape, dt=F32):
            return ctx.enter_context(nc.sbuf_tensor(name, shape, dt))

        def sem(name):
            return ctx.enter_context(nc.semaphore(name))

        gu_ring = sb("gu_ring", [P, 2, KD, 2 * D])
        dn_ring = sb("dn_ring", [P, KD, D])
        stream = [gu_ring[:, 0, 2 * s:2 * s + 2, :].rearrange("p a n -> p (a n)") for s in range(4)]
        g1 = gu_ring[:, 1, :, :].rearrange("p k n -> p (k n)")
        cosT = g1[:, 0:4096].rearrange("p (b i t) -> p b i t", b=4, i=4)
        sinT = g1[:, 4096:8192].rearrange("p (b i t) -> p b i t", b=4, i=4)
        BT = g1[:, 8192:9216].rearrange("p (r b m s) -> p r b m s", r=2, b=4, m=2)
        gatesT = g1[:, 12288:16384].rearrange("p (n t) -> p n t", n=16)
        bc_raw = g1[:, 12288:13312]
        bt_raw = bc_raw[:, 0:512].rearrange("p (r b s) -> p r b s", r=2, b=4)
        ct_raw = bc_raw[:, 512:1024].rearrange("p (r i c) -> p r i c", r=2, i=ST)
        lamw = g1[:, 13312:13312 + 24 * ST].rearrange("p (n i) -> p n i", i=ST)
        ctw = g1[:, 14336:14336 + 1024].rearrange("p (r i c) -> p r i c", r=4, i=ST)
        dn = dn_ring[:, :, :].rearrange("p k n -> p (k n)")
        QT = dn[:, 0:1024].rearrange("p (j t) -> p j t", j=KA)
        KT = dn[:, 2048:3072].rearrange("p (j t) -> p j t", j=KA)
        PT0 = dn[:, 0:2048].rearrange("p (h t) -> p h t", h=HEADS)
        PT1 = dn[:, 2048:3072].rearrange("p (h t) -> p h t", h=HEADS)
        V = dn[:, 3072:4096].rearrange("p (a n) -> p a n", a=TT)
        relb = dn[:, 4096:6144].rearrange("p (h j) -> p h j", h=HEADS)
        CT = dn[:, 6144:7168].rearrange("p (r i c) -> p r i c", r=2, i=ST)
        uT = dn[:, 7168:8192].rearrange("p (b t) -> p b t", b=4)
        h = sb("h", [P, TT, D])
        hT_mem = sb("hT_mem", [P, 2048])
        hT = hT_mem[:, :].rearrange("p (k t) -> p k t", k=KD)
        mixT = hT
        XT = hT_mem[:, 0:1024].rearrange("p (k c) -> p k c", k=KD)
        wide = sb("wide", [P, 2048])
        s_re = wide[:, 0:1024].rearrange("p (i t) -> p i t", i=4)
        s_im = wide[:, 1024:2048].rearrange("p (i t) -> p i t", i=4)
        ssmT = wide[:, 0:1024].rearrange("p (b t) -> p b t", b=4)
        gel = wide[:, 1024:2048].rearrange("p (b t) -> p b t", b=4)
        h1T = wide[:, :].rearrange("p (k t) -> p k t", k=KD)
        xg, xl, sig = wide[:, 0:512], wide[:, 512:1024], wide[:, 1024:1536]
        Gd = wide[:, 0:TT * P].rearrange("p (a e) -> p a e", a=TT)
        sel4 = [wide[:, 1536:1792].rearrange("p (q c) -> p q c", q=4), wide[:, 1792:2048].rearrange("p (q c) -> p q c", q=4)]
        mid = sb("mid", [P, 3072])
        z_re = mid[:, 0:1024].rearrange("p (i t) -> p i t", i=4)
        z_im = mid[:, 1024:2048].rearrange("p (i t) -> p i t", i=4)
        z_both = mid[:, 0:2048].rearrange("p (r i t) -> p r i t", r=2, i=4)
        tmp = mid[:, 2048:3072].rearrange("p (i t) -> p i t", i=4)
        tmp_both = mid[:, 2048:3072].rearrange("p (i r t) -> p i r t", i=2, r=2)
        S1 = mid[:, 0:2048].rearrange("p (h k) -> p h k", h=HEADS)
        S0 = mid[:, 2048:3072].rearrange("p (h k) -> p h k", h=HEADS)
        rows = mid[:, 0:2048].rearrange("p (r d) -> p r d", r=2)
        actT = mid[:, 0:512].rearrange("p (k c) -> p k c", k=4)
        ysb = mid[:, 512:1024]
        Pm = sb("Pm", [P, TT, P])
        PG = mid[:, 1280:1536].rearrange("p (a s) -> p a s", a=TT)
        bgu = mid[:, 1536:2048]
        bdn = mid[:, 2048:3072]
        ln2_rows = [hT_mem[:, 1024:2048], mid[:, 2048:3072]]
        attnT_m = sb("attnT", [P, 1024])
        attnT = attnT_m[:, :].rearrange("p (j t) -> p j t", j=KA)
        GT = attnT_m[:, 0:512].rearrange("p (a t) -> p a t", a=2)
        consts = sb("consts", [P, O_END])
        ident = consts[:, O_ID:O_ID + 128]
        upper = consts[:, O_UP:O_UP + 128]
        slots = consts[:, O_SLOT:O_SLOT + 128]
        times = consts[:, O_TIME:O_TIME + 256]
        gmask = consts[:, O_MASK:O_MASK + 2]
        alpha_id = consts[:, O_ALPHA:O_ALPHA + 128]
        cols = sb("cols", [P, C_END])
        posx = sb("posx", [P, TT, ROUNDS * E + 2])
        gx = sb("gx", [P, TT, ROUNDS * E])
        decay = sb("decay", [P, ST])
        turn = sb("turn", [P, ST])
        stat = sb("stat", [P, TT, 2, 6])
        mv = sb("mv", [P, TT, 2])
        rstd = sb("rstd", [P, TT])
        half_power = sb("half_power", [P, 1])
        negmax = sb("negmax", [P, 2, HEADS])
        psums = sb("psums", [P, 2, HEADS])
        top = sb("top", [P, TT, 8])
        topi = sb("topi", [P, TT, 8], U32)
        topf = sb("topf", [P, TT, 8])
        ex = sb("ex", [P, TT, 8])
        cmax = ex[:, 0, 7:8]
        rwb = sb("rwb", [P, E])
        cint = sb("cint", [P, 1], I32)
        rw = gx[:, :, :].rearrange("p a e -> p (a e)")[:, 0:KD * E].rearrange("p (k e) -> p k e", k=KD)
        logits = attnT_m[:, 0:64].rearrange("p (a e) -> p a e", a=TT)
        mask = attnT_m[:, 64:128].rearrange("p (a e) -> p a e", a=TT)
        oneh = attnT_m[:, 256:512].rearrange("p (a k e) -> p a k e", a=TT, k=TOPK)
        oneg = attnT_m[:, 512:768].rearrange("p (a k e) -> p a k e", a=TT, k=TOPK)
        GdT = attnT_m[:, 768:1024]
        ones = sb("ones", [P, P])

        ps = [ctx.enter_context(nc.psum_tensor(f"ps{i}", [P, 512], F32)) for i in range(8)]
        psA, psB, psY, psM = ps[4], ps[5], ps[6], ps[7]

        x_in = [sem(f"x_in{i}") for i in range(2 * TT)]
        ident_in = sem("ident_in")
        const_in, cols_in, bc_in, relb_in, rb_in = (sem(n) for n in ("const_in", "cols_in", "bc_in", "relb_in", "rb_in"))
        rw_in, lnin_in, ln1_in, bgu_in, bdn_in, ln2_in = (sem(n) for n in ("rw_in", "lnin_in", "ln1_in", "bgu_in", "bdn_in", "ln2_in"))
        w_first = [sem(f"w_first{a}") for a in range(2)]
        w_loaded = [sem(f"w_loaded{s}") for s in range(4)]
        gu_loaded = [[sem(f"gu_loaded{a}_{k}") for k in range(KD)] for a in range(2)]
        dn_loaded = [sem(f"dn_loaded{j}") for j in range(4)]
        vec_chain, act_chain, pool_chain = sem("vec_chain"), sem("act_chain"), sem("pool_chain")
        xhat_ready, hT_psum, hT_act, hT_vec = sem("xhat_ready"), sem("hT_psum"), sem("hT_act"), sem("hT_vec")
        dt_ready, lam_ready, decay_ready, turn_ready, sin_ready, coef_ready = (
            sem(n) for n in ("dt_ready", "lam_ready", "decay_ready", "turn_ready", "sin_ready", "coef_ready"))
        ang_ready, table_ready = sem("ang_ready"), sem("table_ready")
        bt_ready, ct_ready, h_ready = sem("bt_ready"), sem("ct_ready"), sem("h_ready")
        proj_done, proj_act, proj_vec = sem("proj_done"), sem("proj_act"), sem("proj_vec")
        bu_psum, bu_used, s_ready, y_psum, y_used = (sem(n) for n in ("bu_psum", "bu_used", "s_ready", "y_psum", "y_used"))
        glu_psum, glu_sig, glu_ready = sem("glu_psum"), sem("glu_sig"), sem("glu_ready")
        gelu_arg, gelu_sig, gelu_ready = sem("gelu_arg"), sem("gelu_sig"), sem("gelu_ready")
        score_psum, score_used, max_ready, exp_done, p_norm = (sem(n) for n in ("score_psum", "score_used", "max_ready", "exp_done", "p_norm"))
        pt_psum, pt_act, pt_vec, pv_psum, attn_ready = (sem(n) for n in ("pt_psum", "pt_act", "pt_vec", "pv_psum", "attn_ready"))
        mix_ready, wo_done, h1_ready, h1T_psum, h1T_act, h1T_vec = (sem(n) for n in ("mix_ready", "wo_done", "h1_ready", "h1T_psum", "h1T_act", "h1T_vec"))
        ln1_done, h1_vec = sem("ln1_done"), sem("h1_vec")
        logit_psum, top_ready, topexp, mask_ready, pos_psum, gd_ready, gdT_psum, gdT_ready = (
            sem(n) for n in ("logit_psum", "top_ready", "topexp", "mask_ready", "pos_psum", "gd_ready", "gdT_psum", "gdT_ready"))
        count_psum = sem("count_psum")
        gd_zero, bdn_zero = sem("gd_zero"), sem("bdn_zero")
        gdT_used, var_ready, rstd_ready = sem("gdT_used"), sem("var_ready"), sem("rstd_ready")
        slots_ready, count_ready, pad_ready = sem("slots_ready"), sem("count_ready"), sem("pad_ready")
        p_ready, gather_psum, xt_ready = sem("p_ready"), sem("gather_psum"), sem("xt_ready")
        sel_ready, gu_done, gu_used, dn_used = sem("sel_ready"), sem("gu_done"), sem("gu_used"), sem("dn_used")
        pg_ready, gt_psum, gt_ready = sem("pg_ready"), sem("gt_psum"), sem("gt_ready")
        xg_ready, ab_free, lin_ready, sig_ready, act_ready = (sem(n) for n in ("xg_ready", "ab_free", "lin_ready", "sig_ready", "act_ready"))
        at_psum, at_ready, y_ready = sem("at_psum"), sem("at_ready"), sem("y_ready")
        combined, out_ready, out_done = sem("combined"), sem("out_ready"), sem("out_done")

        G_U, G_Q, G_K, G_V, G_GATE, G_US, G_UA, G_END = 0, 4, 8, 12, 16, 32, 40, 48
        B_GLU, B_US, B_UA, B_WO = 8, 9, 10, 11
        used_up = [(proj_done, g) for g in (4, 8, 12, 16, 20, 24, 28, 32)] + [(glu_psum, 4)]

        def h_half(tt, i):
            return h[:, tt, i * 512:(i + 1) * 512]

        def w_in_block(c0):
            return w_in[:, c0:c0 + 512].rearrange("(k p) n -> p k n", p=P)

        blocks = [w_in_block(c) for c in (1536, 0, 512, 1024, 2048, 2560, 3072, 3584)]
        blocks += [w.rearrange("(k p) n -> p k n", p=P) for w in (w_glu, w_us, w_ua)]
        blocks += [w_o[:, c:c + 512].rearrange("(k p) n -> p k n", p=P) for c in (0, 512)]

        def bank_of(g):
            return ps[g % 2][:, 0:T]

        def read_by_act(g):
            return g < G_US

        def group_read(g):
            mine = [i for i in range(g + 1) if read_by_act(i) == read_by_act(g)]
            return (proj_act if read_by_act(g) else proj_vec), len(mine)

        def gu_src(e, k):
            return w_gu[e, k * P:(k + 1) * P, :]

        def dn_src(e, j):
            return w_dn[e, 2 * j * P:2 * (j + 1) * P, :].rearrange("(k p) n -> p k n", p=P)

        block = ctx.enter_context(nc.Block())

        @block.sync
        def _(sp):
            def load_block(i):
                if i >= 4:
                    sp.wait_ge(*used_up[i - 4])
                src = blocks[i]
                nk = src.shape[1]
                dst = stream[i % 4].rearrange("p (k n) -> p k n", k=nk)
                for a in range(2):
                    ks = slice(a * nk // 2, (a + 1) * nk // 2)
                    sp.dma_start(dst[:, ks, :], src[:, ks, :]).then_inc(w_first[a] if i == 0 else w_loaded[i % 4], 16)

            for tt in range(TT):
                for i in range(2):
                    sp.dma_start(h_half(tt, i), x[tt * P:(tt + 1) * P, i * 512:(i + 1) * 512]).then_inc(x_in[2 * tt + i], 16)
            load_block(0)
            sp.dma_start(consts[:, O_UP:O_END], consts_d[:, O_UP:O_END]).then_inc(const_in, 16)
            sp.dma_start(bc_raw, bc_d).then_inc(bc_in, 16)
            for i in range(1, 4):
                load_block(i)
            for a in range(2):
                sp.dma_start(relb[CHUNK * a:CHUNK * a + CHUNK, :, :],
                             bass.AP(tensor=rel_bias.tensor, offset=0, ap=[[1, CHUNK], [REL, HEADS], [1, 256]])).then_inc(relb_in, 16)
            sp.dma_start(rwb[:, :], router_b.to_broadcast([P, E])).then_inc(rb_in, 16)
            sp.dma_start(rw, router_w.rearrange("(k p) e -> p k e", p=P)).then_inc(rw_in, 16)
            for i in range(4, 11):
                load_block(i)

            def load_gu(e, a, k):
                sp.dma_start(gu_ring[:, a, k, :], gu_src(e, k)).then_inc(gu_loaded[a][k], 16)

            def load_dn(e, j):
                sp.dma_start(dn_ring[:, 2 * j:2 * j + 2, :], dn_src(e, j)).then_inc(dn_loaded[j], 16)

            sp.wait_ge(s_ready, 4)
            for k in K_ORDER[0:4]:
                load_gu(1, 1, k)
            load_block(11)
            load_gu(1, 1, 0)
            load_gu(1, 1, 1)
            load_block(12)
            sp.wait_ge(pv_psum, 2)
            for j in J_ORDER:
                load_dn(0, j)
            sp.wait_ge(h_ready, 1)
            for r in range(2):
                sp.dma_start(rows[:, r, :], lnrows_d[2 + r:3 + r, :].to_broadcast([P, D])).then_inc(ln1_in, 16)
            sp.wait_ge(proj_done, G_UA)
            load_gu(0, 0, 2)
            load_gu(0, 0, 3)
            sp.wait_ge(proj_done, G_END)
            load_gu(0, 0, 4)
            load_gu(0, 0, 5)
            sp.wait_ge(mix_ready, KD)
            load_gu(1, 1, 6)
            load_gu(1, 1, 7)
            sp.wait_ge(wo_done, 3)
            load_gu(0, 0, 6)
            load_gu(0, 0, 7)
            sp.wait_ge(wo_done, 4)
            load_gu(0, 0, 1)
            load_gu(0, 0, 0)

            def gu_loads(n, e, a, chunks_at_once=2):
                for i, k in enumerate(K_ORDER):
                    if i % chunks_at_once == 0:
                        sp.wait_ge(gu_used, n * KD + (i + chunks_at_once - 2 * KD))
                    sp.dma_start(gu_ring[:, a, k, :],
                                 w_gu[bass.ds(e, 1), k * P:(k + 1) * P, :].rearrange("o p n -> (o p) n")).then_inc(gu_loaded[a][k], 16)

            def dn_loads(n, e):
                for i, j in enumerate(J_ORDER):
                    if i % 2 == 0:
                        sp.wait_ge(dn_used, n * 4 + (i + 2 - 4))
                    sp.dma_start(dn_ring[:, 2 * j:2 * j + 2, :],
                                 w_dn[bass.ds(e, 1), 2 * j * P:2 * (j + 1) * P, :].rearrange("o (k p) n -> p (o k) n", p=P)).then_inc(dn_loaded[j], 16)

            swap = PAIRS - 3
            gu_loads(2, 2, 0, 1)
            with sp.Fori(1, swap) as it:
                dn_loads(it * 2 - 1, it * 2 - 1)
                gu_loads(it * 2 + 1, it * 2 + 1, 1)
                dn_loads(it * 2, it * 2)
                gu_loads(it * 2 + 2, it * 2 + 2, 0)
            dn_loads(2 * swap - 1, 2 * swap - 1)
            dn_loads(2 * swap, 2 * swap)
            gu_loads(2 * swap + 1, 2 * swap + 1, 1)
            dn_loads(2 * swap + 1, 2 * swap + 1)
            with sp.Fori(swap + 1, PAIRS) as it:
                for a in range(2):
                    gu_loads(it * 2 + a, it * 2 + a, a)
                    dn_loads(it * 2 + a, it * 2 + a)
            sp.wait_ge(count_ready, 1)
            fullest = sp.value_load(cint[0:1, 0:1], min_val=0, max_val=T)
            with sp.If(fullest > CAP):
                with sp.Fori(1, ROUNDS) as rnd:
                    with sp.Fori(0, PAIRS) as pair:
                        for a in range(2):
                            n, e = rnd * E + pair * 2 + a, pair * 2 + a
                            gu_loads(n, e, a)
                            dn_loads(n, e)
            with sp.Else():
                sp.nop()
            for tt in range(TT):
                for i in range(2):
                    sp.wait_ge(out_ready, 2 * tt + i + 1)
                    sp.dma_start(out[tt * P:(tt + 1) * P, i * 512:(i + 1) * 512], h_half(tt, i)).then_inc(out_done, 16)
            sp.wait_ge(out_done, 2 * 16 * TT)

        @block.scalar
        def _(act):
            chain = [0]

            def link(ins):
                chain[0] += 1
                ins.then_inc(act_chain, 1)
                act.wait_ge(act_chain, chain[0])

            act.dma_start(cols[:, :], cols_d).then_inc(cols_in, 16)
            act.dma_start(ident, consts_d[:, 0:O_UP]).then_inc(ident_in, 16)

            act.wait_ge(cols_in, 16)
            act.activation(lamw[:, 0, :], cols[:, C_DT:C_DT + ST], ACT.Exp).then_inc(dt_ready, 1)
            act.wait_ge(lam_ready, 1)
            act.activation(decay[:, :], lamw[:, 1, :], ACT.Exp).then_inc(decay_ready, 1)

            def tables(b):
                act.wait_ge(ang_ready, b + 1)
                link(act.activation(cosT[:, b], sinT[:, b], ACT.Sin, scale=TWO_PI / 2))
                link(act.activation(sinT[:, b], sinT[:, b], ACT.Sin, scale=TWO_PI))
                link(act.activation(cosT[:, b], cosT[:, b], ACT.Square))
                act.activation(cosT[:, b], cosT[:, b], ACT.Copy, scale=-2.0, bias=1.0).then_inc(table_ready, 1)

            for k in (0, 1, 4, 5):
                act.wait_ge(hT_psum, k // 2 + 1)
                act.activation(hT[:, k, :], ps[4 + k // 2][:, (k % 2) * T:(k % 2) * T + T], ACT.Identity,
                               bias=cols[:, C_B + k:C_B + k + 1], scale=cols[:, C_G + k:C_G + k + 1]).then_inc(hT_act, 1)
            act.wait_ge(turn_ready, 1)
            act.activation(lamw[:, 5, :], turn[:, :], ACT.Sin, scale=TWO_PI).then_inc(sin_ready, 1)
            act.activation(lamw[:, 6, :], turn[:, :], ACT.Sin, scale=TWO_PI / 2).then_inc(sin_ready, 1)

            def evac(g):
                act.wait_ge(proj_done, g + 1)
                src = bank_of(g)
                if g < G_Q:
                    ins = act.activation(uT[:, g - G_U, :], src, ACT.Copy)
                elif g < G_K:
                    ins = act.activation(QT[:, g - G_Q, :], src, ACT.Copy, scale=HD ** -0.5)
                elif g < G_V:
                    ins = act.activation(KT[:, g - G_K, :], src, ACT.Copy)
                elif g < G_GATE:
                    a, c = divmod(g - G_V, 2)
                    ins = act.activation(V[:, a, c * 256:(c + 1) * 256], src, ACT.Copy)
                else:
                    n = g - G_GATE
                    if n == 0:
                        act.wait_ge(ct_ready, 1)
                        act.wait_ge(bt_ready, 2)
                    ins = act.activation(gatesT[:, n, :], src, ACT.Sigmoid, bias=cols[:, C_GATE + n:C_GATE + n + 1])
                ins.then_inc(proj_act, 1)

            evac(G_U)
            tables(0)
            for g in range(G_U + 1, G_Q):
                evac(g)
            tables(1)
            for g in range(G_Q, G_V):
                evac(g)
            tables(2)
            for g in range(G_V, G_GATE + 4):
                evac(g)
            tables(3)
            for g in range(G_GATE + 4, G_GATE + 12):
                evac(g)
            act.wait_ge(gelu_arg, 1)
            act.activation(gel, gel, ACT.Sigmoid, scale=2.0 * GELU_C).then_inc(gelu_sig, 1)
            for g in range(G_GATE + 12, G_US):
                evac(g)

            act.wait_ge(max_ready, 1)
            for i in range(4):
                a, Sx = ((0, S0), (1, S1))[i // 2]
                for hd in range(4 * (i % 2), 4 * (i % 2) + 4):
                    act.activation(Sx[:, hd, :], Sx[:, hd, :], ACT.Exp, bias=negmax[:, a, hd:hd + 1],
                                   accum_out=psums[:, a, hd:hd + 1]).then_inc(exp_done, 1)
            for i in range(2):
                act.wait_ge(glu_psum, i + 1)
                act.activation(gel[:, 2 * i:2 * i + 2, :].rearrange("p b t -> p (b t)"), ps[4 + i][:, :], ACT.Sigmoid).then_inc(glu_sig, 1)
            for i in (1, 3, 5):
                act.wait_ge(pt_psum, i + 1)
                dst = (PT0[:, 2 * i:2 * i + 2, :] if i < 4 else PT1[:, 4 * (i - 4):4 * (i - 4) + 4, :])
                act.activation(dst.rearrange("p h t -> p (h t)"), ps[2 + i][:, :], ACT.Copy).then_inc(pt_act, 1)
            for tt in range(TT):
                act.wait_ge(h1T_psum, 2 * tt + 2)
                for k in range(4, KD):
                    act.activation(h1T[:, k, tt * P:(tt + 1) * P], ps[2 * tt + 1][:, (k - 4) * P:(k - 3) * P], ACT.Identity,
                                   bias=cols[:, C_B1 + k:C_B1 + k + 1], scale=cols[:, C_G1 + k:C_G1 + k + 1]).then_inc(h1T_act, 1)
                act.wait_ge(top_ready, tt + 1)
                act.activation(ex[:, tt, 0:TOPK], top[:, tt, 0:TOPK], ACT.Exp, bias=topf[:, tt, 7:8],
                               accum_out=ex[:, tt, 4:5]).then_inc(topexp, 1)
            for i, bank in ((0, psA), (1, psM)):
                act.wait_ge(gather_psum, i + 1)
                act.activation(XT[:, 4 * i:4 * i + 4, :].rearrange("p k c -> p (k c)"), bank[:, :], ACT.Copy).then_inc(xt_ready, 1)
            act.wait_ge(gdT_psum, TT)
            act.activation(GdT, psY[:, 0:256], ACT.Copy).then_inc(gdT_ready, 1)

            def pair_work(it):
                for a in range(2):
                    n = it * 2 + a
                    act.wait_ge(xg_ready, n + 1)
                    act.activation(sig, xg, ACT.Sigmoid, scale=SWALPHA).then_inc(sig_ready, 1)
                    if a == 1:
                        act.wait_ge(gather_psum, it * 2 + 3)
                        act.activation(XT[:, 0:4, :].rearrange("p k c -> p (k c)"), psM[:, :], ACT.Copy).then_inc(xt_ready, 1)
                    act.wait_ge(gt_psum, n + 2)
                    act.activation(GT[:, a, :], psY[:, 0:256], ACT.Copy).then_inc(gt_ready, 1)
                    act.wait_ge(at_psum, n + 1)
                    act.activation(actT[:, :, :].rearrange("p k c -> p (k c)"), psY[:, :], ACT.Copy).then_inc(at_ready, 1)
                    if a == 1:
                        act.wait_ge(gather_psum, it * 2 + 4)
                        act.activation(XT[:, 4:8, :].rearrange("p k c -> p (k c)"), psA[:, :], ACT.Copy).then_inc(xt_ready, 1)

            with act.Fori(0, PAIRS) as it:
                pair_work(it)
            act.wait_ge(count_ready, 1)
            fullest = act.value_load(cint[0:1, 0:1], min_val=0, max_val=T)
            with act.If(fullest > CAP):
                with act.Fori(1, ROUNDS) as rnd:
                    with act.Fori(0, PAIRS) as pair:
                        pair_work(rnd * PAIRS + pair)
            with act.Else():
                act.nop()

        @block.gpsimd
        def _(pool):
            chain = [0]

            def link(ins):
                chain[0] += 1
                ins.then_inc(pool_chain, 1)
                pool.wait_ge(pool_chain, chain[0])

            norms = [0]

            def inverse_deviation(tt):
                norms[0] += 1
                pool.wait_ge(var_ready, norms[0])
                pool.tensor_tensor(rstd[:, tt:tt + 1], mv[:, tt, 1:2], half_power[:, :], ALU.pow).then_inc(rstd_ready, 1)

            def gain_and_shift(tt, i):
                v = slice(i * 512, (i + 1) * 512)
                link(pool.tensor_tensor(h_half(tt, i), h_half(tt, i), rows[:, 0, v], ALU.mult))
                pool.tensor_tensor(h_half(tt, i), h_half(tt, i), rows[:, 1, v], ALU.add).then_inc(h1_ready, 1)

            pool.memset(ones[:, :], 1.0).then_inc(pad_ready, 1)
            link(pool.memset(CT, 0.0))
            link(pool.memset(half_power[:, :], -0.5))
            for tt in range(TT):
                inverse_deviation(tt)
            pool.wait_ge(const_in, 16)
            pool.wait_ge(bc_in, 16)
            for r in range(2):
                for b in range(4):
                    ins = pool.tensor_tensor(BT[:, r, b], bt_raw[:, r, b].unsqueeze(1).to_broadcast([P, 2, NST]),
                                             gmask.unsqueeze(2).to_broadcast([P, 2, NST]), ALU.mult)
                ins.then_inc(bt_ready, 1)
            pool.wait_ge(coef_ready, 1)
            cr = lamw[:, 12, :].unsqueeze(2).to_broadcast([P, ST, GS])
            ci = lamw[:, 13, :].unsqueeze(2).to_broadcast([P, ST, GS])
            for n, (c, co) in enumerate(((0, cr), (1, ci), (0, ci), (1, cr))):
                link(pool.tensor_tensor(ctw[:, n], ct_raw[:, c], co, ALU.mult))
            link(pool.tensor_tensor(ctw[:, 0], ctw[:, 0], ctw[:, 1], ALU.subtract))
            link(pool.tensor_tensor(ctw[:, 2], ctw[:, 2], ctw[:, 3], ALU.add))
            for hf in range(2):
                q, c = slice(64 * hf, 64 * hf + 64), slice(GS * hf, GS * hf + GS)
                link(pool.tensor_copy(CT[q, 0, :, c], ctw[q, 0]))
                ins = pool.tensor_scalar(CT[q, 1, :, c], ctw[q, 2], -1.0, None, ALU.mult)
                if hf == 0:
                    link(ins)
            ins.then_inc(ct_ready, 1)

            pool.wait_ge(pt_psum, 6)
            for r in range(2):
                pool.dma_start(rows[:, r, :], lnrows_d[r:r + 1, :].to_broadcast([P, D])).then_inc(lnin_in, 16)
            pool.memset(bdn[E:2 * E, :], 0.0).then_inc(bdn_zero, 1)
            pool.memset(bdn[2 * E:P, :], 0.0).then_inc(bdn_zero, 1)
            pool.dma_start(bdn[0:E, :], bdn_d).then_inc(bdn_in, 16)
            pool.wait_ge(bdn_zero, 2)
            pool.wait_ge(lnin_in, 32)
            link(pool.tensor_tensor(h[:, :, :], h[:, :, :], rows[:, 0, :].unsqueeze(1).to_broadcast([P, TT, D]), ALU.mult))
            pool.tensor_tensor(h[:, :, :], h[:, :, :], rows[:, 1, :].unsqueeze(1).to_broadcast([P, TT, D]), ALU.add).then_inc(h_ready, 1)
            pool.wait_ge(ln1_in, 32)
            for tt in range(TT):
                inverse_deviation(tt)
                for i in range(tt, 2):
                    pool.wait_ge(h1T_psum, 2 * tt + i + 1)
                    gain_and_shift(tt, i)
            pool.wait_ge(h1_ready, 3)
            pool.wait_ge(h1_vec, 1)
            pool.wait_ge(logit_psum, TT)
            pool.memset(Gd, 0.0).then_inc(gd_zero, 1)
            pool.dma_start(bgu, bgu_d).then_inc(bgu_in, 16)

            def pair_work(it, pair):
                for a in range(2):
                    n, e = it * 2 + a, pair * 2 + a
                    pool.wait_ge(gu_done, n + 1)
                    picked = ident.rearrange("p (q e) -> p q e", q=4)[:, :, bass.ds(e, 1)].to_broadcast([P, 4, CAP])
                    pool.tensor_tensor(sel4[a], picked, ones[:, 0:CAP].unsqueeze(1).to_broadcast([P, 4, CAP]), ALU.mult).then_inc(sel_ready, 1)

            pair_work(0, 0)
            pool.wait_ge(sel_ready, 2)
            pool.wait_ge(gdT_used, 1)
            for r in range(2):
                pool.dma_start(ln2_rows[r], lnrows_d[4 + r:5 + r, :].to_broadcast([P, D])).then_inc(ln2_in, 16)
            with pool.Fori(1, PAIRS) as it:
                pair_work(it, it)
            pool.wait_ge(count_ready, 1)
            fullest = pool.value_load(cint[0:1, 0:1], min_val=0, max_val=T)
            with pool.If(fullest > CAP):
                with pool.Fori(1, ROUNDS) as rnd:
                    with pool.Fori(0, PAIRS) as pair:
                        pair_work(rnd * PAIRS + pair, pair)
            with pool.Else():
                pool.nop()
            for tt in range(TT):
                inverse_deviation(tt)

        @block.vector
        def _(dve):
            chain = [0]

            def link(ins):
                chain[0] += 1
                ins.then_inc(vec_chain, 1)
                dve.wait_ge(vec_chain, chain[0])

            norms = [0]

            def half_stats(tt, i, v):
                chain[0] += 1
                dve.bn_stats(stat[:, tt, i, :], v).then_inc(vec_chain, 1)

            def variance(tt):
                dve.wait_ge(vec_chain, chain[0])
                norms[0] += 1
                link(dve.bn_aggr(mv[:, tt, :], stat[:, tt, :, :].rearrange("p a b -> p (a b)")))
                dve.tensor_scalar(mv[:, tt, 1:2], mv[:, tt, 1:2], EPS, None, ALU.add).then_inc(var_ready, 1)

            def norm_rows(tt, signal, halves, gain, shift):
                variance(tt)
                for i in range(2):
                    chain[0] += 1
                    dve.scalar_tensor_tensor(out=h_half(tt, i), in0=halves[i], scalar=mv[:, tt, 0:1], in1=gain[:, i * 512:(i + 1) * 512],
                                             op0=ALU.subtract, op1=ALU.mult).then_inc(vec_chain, 1)
                dve.wait_ge(vec_chain, chain[0])
                dve.wait_ge(rstd_ready, norms[0])
                for i in range(2):
                    dve.scalar_tensor_tensor(out=h_half(tt, i), in0=h_half(tt, i), scalar=rstd[:, tt:tt + 1], in1=shift[:, i * 512:(i + 1) * 512],
                                             op0=ALU.mult, op1=ALU.add).then_inc(signal, 1)

            def center(tt, norm, signal):
                dve.wait_ge(rstd_ready, norm)
                for i in range(2):
                    dve.tensor_scalar(h_half(tt, i), h_half(tt, i), mv[:, tt, 0:1], rstd[:, tt:tt + 1], ALU.subtract, ALU.mult).then_inc(signal, 1)

            for i in range(2):
                dve.wait_ge(x_in[i], 16)
                half_stats(0, i, h_half(0, i))
            variance(0)
            for i in range(2):
                dve.wait_ge(x_in[2 + i], 16)
                half_stats(1, i, h_half(1, i))
            center(0, 1, xhat_ready)
            variance(1)
            center(1, 2, xhat_ready)

            L = lambda i: lamw[:, i, :]
            lre, lim = cols[:, C_RE:C_RE + ST], cols[:, C_IM:C_IM + ST]
            dve.wait_ge(cols_in, 16)
            dve.wait_ge(dt_ready, 1)
            dve.tensor_tensor(L(1), lre, L(0), ALU.mult).then_inc(lam_ready, 1)
            link(dve.tensor_tensor(L(2), lim, L(0), ALU.mult))
            link(dve.tensor_scalar(L(3), L(2), INV_2PI, None, ALU.mult))
            link(dve.tensor_scalar(L(4), L(3), MAGIC, -MAGIC, ALU.add, ALU.add))
            dve.tensor_tensor(turn[:, :], L(3), L(4), ALU.subtract).then_inc(turn_ready, 1)
            dve.wait_ge(turn_ready, 1)

            for k in (2, 3, 6, 7):
                dve.wait_ge(hT_psum, k // 2 + 1)
                dve.tensor_scalar(hT[:, k, :], ps[4 + k // 2][:, (k % 2) * T:(k % 2) * T + T], cols[:, C_G + k:C_G + k + 1],
                                  cols[:, C_B + k:C_B + k + 1], ALU.mult, ALU.add).then_inc(hT_vec, 1)

            def phases(b):
                ang = sinT[:, b]
                if b == 0:
                    dve.wait_ge(const_in, 16)
                link(dve.tensor_tensor(ang, times.unsqueeze(1).to_broadcast([P, 4, T]),
                                       turn[:, 4 * b:4 * b + 4].unsqueeze(2).to_broadcast([P, 4, T]), ALU.mult))
                link(dve.tensor_scalar(tmp, ang, MAGIC, -MAGIC, ALU.add, ALU.add))
                dve.tensor_tensor(ang, ang, tmp, ALU.subtract).then_inc(ang_ready, 1)
                dve.wait_ge(ang_ready, b + 1)

            phases(0)
            phases(1)
            dve.wait_ge(sin_ready, 2)
            dve.wait_ge(decay_ready, 1)
            link(dve.tensor_tensor(L(7), L(6), L(6), ALU.mult))
            link(dve.tensor_scalar(L(7), L(7), -2.0, 1.0, ALU.mult, ALU.add))
            link(dve.tensor_tensor(L(8), decay[:, :], L(7), ALU.mult))
            link(dve.tensor_scalar(L(8), L(8), 1.0, None, ALU.subtract))
            link(dve.tensor_tensor(L(9), decay[:, :], L(5), ALU.mult))
            link(dve.tensor_tensor(L(10), lre, lre, ALU.mult))
            link(dve.tensor_tensor(L(11), lim, lim, ALU.mult))
            link(dve.tensor_tensor(L(10), L(10), L(11), ALU.add))
            link(dve.reciprocal(L(10), L(10)))
            for o, (a1, b1, a2, b2, op) in ((12, (8, lre, 9, lim, ALU.add)), (13, (9, lre, 8, lim, ALU.subtract))):
                link(dve.tensor_tensor(L(14), L(a1), b1, ALU.mult))
                link(dve.tensor_tensor(L(15), L(a2), b2, ALU.mult))
                link(dve.tensor_tensor(L(14), L(14), L(15), op))
                ins = dve.tensor_tensor(L(o), L(14), L(10), ALU.mult)
                if o == 12:
                    link(ins)
            ins.then_inc(coef_ready, 1)

            def ssm_block(b):
                dve.wait_ge(table_ready, b + 1)
                dve.wait_ge(bu_psum, b + 1)
                cs, sn = cosT[:, b], sinT[:, b]
                for j in range(2):
                    v = slice(2 * j, 2 * j + 2)
                    for i in (2 * j, 2 * j + 1):
                        bu = ps[2 + i][:, :].rearrange("p (r t) -> p r t", r=2)
                        dve.tensor_tensor(z_both[:, :, i], bu, cs[:, i].unsqueeze(1).to_broadcast([P, 2, T]), ALU.mult).then_inc(bu_used, 1)
                        dve.tensor_tensor(tmp_both[:, i % 2], bu, sn[:, i].unsqueeze(1).to_broadcast([P, 2, T]), ALU.mult).then_inc(bu_used, 1)
                    dve.wait_ge(bu_used, 8 * b + 4 * j + 4)
                    chain[0] += 2
                    dve.tensor_tensor(z_re[:, v], z_re[:, v], tmp_both[:, :, 1], ALU.add).then_inc(vec_chain, 1)
                    dve.tensor_tensor(z_im[:, v], z_im[:, v], tmp_both[:, :, 0], ALU.subtract).then_inc(vec_chain, 1)
                    dve.wait_ge(vec_chain, chain[0])
                for zz in (z_re, z_im):
                    for i in range(4):
                        n = 4 * b + i
                        dve.tensor_tensor_scan(zz[:, i], decay[:, n:n + 1].to_broadcast([P, T]), zz[:, i], 0.0,
                                               ALU.mult, ALU.add).then_inc(vec_chain, 1)
                        chain[0] += 1
                dve.wait_ge(vec_chain, chain[0])
                if b >= 1:
                    dve.wait_ge(y_psum, b)
                chain[0] += 2
                dve.tensor_tensor(s_re, z_re, cs, ALU.mult).then_inc(vec_chain, 1)
                dve.tensor_tensor(tmp, z_im, sn, ALU.mult).then_inc(vec_chain, 1)
                dve.wait_ge(vec_chain, chain[0])
                link(dve.tensor_tensor(s_re, s_re, tmp, ALU.subtract))
                chain[0] += 2
                dve.tensor_tensor(s_im, z_re, sn, ALU.mult).then_inc(vec_chain, 1)
                dve.tensor_tensor(tmp, z_im, cs, ALU.mult).then_inc(vec_chain, 1)
                dve.wait_ge(vec_chain, chain[0])
                dve.tensor_tensor(s_im, s_im, tmp, ALU.add).then_inc(s_ready, 1)
                dve.wait_ge(s_ready, b + 1)

            def y_block(b):
                dve.wait_ge(y_psum, b + 1)
                dve.scalar_tensor_tensor(out=uT[:, b, :], in0=uT[:, b, :], scalar=cols[:, C_D + b:C_D + b + 1],
                                         in1=ps[6 + b // 2][:, (b % 2) * 256:(b % 2) * 256 + 256], op0=ALU.mult, op1=ALU.add).then_inc(y_used, 1)

            ssm_block(0)
            phases(2)
            ssm_block(1)
            y_block(0)
            phases(3)
            ssm_block(2)
            y_block(1)
            ssm_block(3)
            y_block(2)
            y_block(3)
            dve.wait_ge(y_used, 4)
            link(dve.tensor_tensor(gel, uT, uT, ALU.mult))
            link(dve.tensor_scalar(gel, gel, GELU_A, 1.0, ALU.mult, ALU.add))
            dve.tensor_tensor(gel, gel, uT, ALU.mult).then_inc(gelu_arg, 1)

            dve.wait_ge(relb_in, 32)
            link(dve.memset(S1[0:64, :, 192:256], -1e30))
            link(dve.memset(S0[0:64, :, 64:128], -1e30))
            for a, Sx in ((1, S1), (0, S0)):
                for c in range(2):
                    nk = CHUNK * (2 * a + c + 1)
                    q = slice(64 * c, 64 * c + 64)
                    rev = slice(nk - 1, None, -1)
                    for half in range(2 * (a + 1)):
                        dve.wait_ge(score_psum, half // 2 + 1 if a else 3)
                        hs = 2 if a else 4
                        hh = slice(4 * (half // 2) + half % 2, 4 * (half // 2) + half % 2 + 2 * hs - 1, 2)
                        src = ps[2 + half] if a else ps[6 + half]
                        src = src[q, :].rearrange("p (h k) -> p h k", h=hs)[:, :, 0:nk]
                        dve.tensor_tensor(Sx[q, hh, 0:nk], src, relb[q, hh, rev], ALU.add).then_inc(score_used, 1)
            dve.wait_ge(score_used, 12)
            for a, Sx in ((0, S0), (1, S1)):
                link(dve.tensor_reduce(negmax[:, a, :], Sx, AX_X, ALU.max))
            dve.tensor_scalar(negmax[:, :, :], negmax[:, :, :], -1.0, None, ALU.mult).then_inc(max_ready, 1)
            dve.wait_ge(gelu_sig, 1)
            dve.tensor_tensor(uT, uT, gel, ALU.mult).then_inc(gelu_ready, 1)
            def normalize(a, Sx):
                dve.tensor_tensor(Sx, Sx, psums[:, a, :].unsqueeze(2).to_broadcast([P, HEADS, P * (a + 1)]), ALU.mult).then_inc(p_norm, 1)

            dve.wait_ge(exp_done, 2 * HEADS)
            link(dve.reciprocal(psums[:, :, :], psums[:, :, :]))
            normalize(0, S0)
            for i in range(2):
                dve.wait_ge(glu_sig, i + 1)
                dve.wait_ge(glu_psum, 2 + i + 1)
                dve.tensor_tensor(ssmT[:, 2 * i:2 * i + 2, :].rearrange("p b t -> p (b t)"), ps[2 + i][:, :],
                                  gel[:, 2 * i:2 * i + 2, :].rearrange("p b t -> p (b t)"), ALU.mult).then_inc(glu_ready, 1)
            normalize(1, S1)

            dve.wait_ge(proj_act, G_US)

            def gated_ssm(n):
                dve.wait_ge(proj_done, G_US + n + 1)
                dve.tensor_tensor(mixT[:, n, :], bank_of(G_US + n), gatesT[:, 8 + n, :], ALU.mult).then_inc(proj_vec, 1)

            for n in range(4):
                gated_ssm(n)
            for i in (0, 2, 4):
                dve.wait_ge(pt_psum, i + 1)
                dst = (PT0[:, 2 * i:2 * i + 2, :] if i < 4 else PT1[:, 4 * (i - 4):4 * (i - 4) + 4, :])
                dve.tensor_copy(dst.rearrange("p h t -> p (h t)"), ps[2 + i][:, :]).then_inc(pt_vec, 1)
            gated_ssm(4)
            gated_ssm(5)
            for i in range(2):
                dve.wait_ge(pv_psum, i + 1)
                dve.tensor_copy(attnT[:, 2 * i:2 * i + 2, :].rearrange("p j t -> p (j t)"), ps[2 + i][:, :]).then_inc(attn_ready, 1)
            gated_ssm(6)
            gated_ssm(7)
            for n in range(8):
                dve.wait_ge(proj_done, G_UA + n + 1)
                if n >= 2:
                    dve.wait_ge(mix_ready, n - 1)
                dve.tensor_tensor(gel[:, n % 2, :], bank_of(G_UA + n), gatesT[:, n, :], ALU.mult).then_inc(proj_vec, 1)
                dve.wait_ge(proj_vec, 8 + n + 1)
                dve.tensor_tensor(mixT[:, n, :], mixT[:, n, :], gel[:, n % 2, :], ALU.add).then_inc(mix_ready, 1)

            dve.wait_ge(h_ready, 1)

            def residual(tt, i):
                dve.wait_ge(wo_done, 2 * tt + i + 1)
                link(dve.scalar_tensor_tensor(out=h_half(tt, i), in0=h_half(tt, i), scalar=ALPHA, in1=ps[4 + 2 * tt + i][:, :],
                                              op0=ALU.mult, op1=ALU.add))
                half_stats(tt, i, h_half(tt, i))

            def new_h(tt):
                variance(tt)
                center(tt, TT + tt + 1, ln1_done)
                dve.wait_ge(h1T_psum, 2 * tt + 1)
                for k in range(4):
                    dve.tensor_scalar(h1T[:, k, tt * P:(tt + 1) * P], ps[2 * tt][:, k * P:(k + 1) * P], cols[:, C_G1 + k:C_G1 + k + 1],
                                      cols[:, C_B1 + k:C_B1 + k + 1], ALU.mult, ALU.add).then_inc(h1T_vec, 1)

            iota_e = times[:, 0:E].unsqueeze(1).to_broadcast([P, TOPK, E])

            def choose(a):
                dve.wait_ge(logit_psum, a + 1)
                link(dve.tensor_tensor(logits[:, a, :], ps[4 + a][:, 0:E], rwb[:, :], ALU.add))
                link(dve.max(top[:, a, :], logits[:, a, :]))
                link(dve.max_index(topi[:, a, :], top[:, a, :], logits[:, a, :]))
                chain[0] += 1
                dve.tensor_copy(topf[:, a, 0:7], topi[:, a, 0:7]).then_inc(vec_chain, 1)
                dve.tensor_scalar(topf[:, a, 7:8], top[:, a, 0:1], -1.0, None, ALU.mult).then_inc(top_ready, 1)
                dve.wait_ge(vec_chain, chain[0])
                link(dve.tensor_tensor(oneh[:, a], iota_e, topf[:, a, 0:TOPK].unsqueeze(2).to_broadcast([P, TOPK, E]), ALU.is_equal))
                dve.tensor_reduce(mask[:, a, :], oneh[:, a].rearrange("p k e -> p e k"), AX_X, ALU.add).then_inc(mask_ready, 1)

            def gates(a):
                dve.wait_ge(topexp, a + 1)
                link(dve.reciprocal(ex[:, a, 5:6], ex[:, a, 4:5]))
                link(dve.tensor_scalar(ex[:, a, 0:TOPK], ex[:, a, 0:TOPK], ex[:, a, 5:6], None, ALU.mult))
                link(dve.tensor_tensor(oneg[:, a], oneh[:, a], ex[:, a, 0:TOPK].unsqueeze(2).to_broadcast([P, TOPK, E]), ALU.mult))

            def first_slots(tt):
                dve.wait_ge(mask_ready, tt + 1)
                dve.wait_ge(pos_psum, tt + 1)
                link(dve.scalar_tensor_tensor(out=logits[:, tt, :], in0=mask[:, tt, :], scalar=FAR,
                                              in1=ps[6][:, tt * E:(tt + 1) * E], op0=ALU.mult, op1=ALU.add))
                link(dve.tensor_scalar(posx[:, tt, 0:E], logits[:, tt, :], -FAR, None, ALU.add))
                for a in range(2):
                    dve.tensor_scalar(Pm[:, tt, CAP * a:CAP * a + CAP], slots[:, 0:CAP], posx[:, tt, a:a + 1], None, ALU.is_equal).then_inc(p_ready, 1)

            residual(0, 0)
            residual(0, 1)
            new_h(0)
            residual(1, 0)
            dve.wait_ge(rb_in, 16)
            choose(0)
            gates(0)
            first_slots(0)
            residual(1, 1)
            new_h(1)
            dve.wait_ge(ln1_in, 32)
            link(dve.tensor_tensor(h_half(1, 0), h_half(1, 0), rows[:, 0, 0:512], ALU.mult))
            dve.tensor_tensor(h_half(1, 0), h_half(1, 0), rows[:, 1, 0:512], ALU.add).then_inc(h1_vec, 1)
            choose(1)
            first_slots(1)
            dve.wait_ge(count_psum, 1)
            link(dve.tensor_reduce(cmax, ps[5][:, 2 * E:3 * E], AX_X, ALU.max))
            dve.tensor_copy(cint[:, :], cmax).then_inc(count_ready, 1)
            gates(1)
            dve.wait_ge(gd_zero, 1)
            for a in range(TT):
                dve.tensor_reduce(Gd[:, a, 0:E], oneg[:, a].rearrange("p k e -> p e k"), AX_X, ALU.add).then_inc(gd_ready, 1)

            def next_rows(it_next):
                for tt in range(TT):
                    for a in range(2):
                        where = posx[:, tt, bass.ds(it_next * 2 + a, 1)]
                        dve.tensor_scalar(Pm[:, tt, CAP * a:CAP * a + CAP], slots[:, 0:CAP], where, None, ALU.is_equal).then_inc(p_ready, 1)

            for r in range(1, ROUNDS):
                dve.tensor_scalar(posx[:, :, r * E:(r + 1) * E], logits[:, :, :], -FAR - CAP * r, None, ALU.add).then_inc(slots_ready, 1)
            dve.wait_ge(gd_ready, TT)
            for r in range(ROUNDS):
                dve.tensor_copy(gx[:, :, r * E:(r + 1) * E], Gd[:, :, 0:E]).then_inc(slots_ready, 1)
            dve.memset(posx[:, :, ROUNDS * E:], -FAR).then_inc(slots_ready, 1)
            dve.wait_ge(slots_ready, 2 * ROUNDS)
            dve.wait_ge(count_ready, 1)
            dve.memset(cmax, 0.0).then_inc(ab_free, 1)

            def pair_work(it):
                for a in range(2):
                    n = it * 2 + a
                    dve.wait_ge(gt_psum, n + 1)
                    for tt in range(TT):
                        dve.tensor_scalar(PG[:, tt, :], slots, posx[:, tt, bass.ds(n, 1)], gx[:, tt, bass.ds(n, 1)],
                                          ALU.is_equal, ALU.mult).then_inc(pg_ready, 1)
                    if a == 0:
                        dve.wait_ge(gather_psum, it * 2 + 2)
                        next_rows(it + 1)
                    dve.wait_ge(gu_done, n + 3)
                    dve.tensor_scalar(xg, psA[:, :], LIMIT, None, ALU.min).then_inc(xg_ready, 1)
                    dve.tensor_scalar(xl, psB[:, :], LIMIT, -LIMIT, ALU.min, ALU.max).then_inc(ab_free, 1)
                    dve.wait_ge(xg_ready, n + 1)
                    dve.wait_ge(ab_free, n + 2)
                    dve.scalar_tensor_tensor(out=xl, in0=xl, scalar=1.0, in1=xg, op0=ALU.add, op1=ALU.mult).then_inc(lin_ready, 1)
                    dve.wait_ge(lin_ready, n + 1)
                    dve.wait_ge(sig_ready, n + 1)
                    dve.tensor_tensor(xl, xl, sig, ALU.mult).then_inc(act_ready, 1)
                    dve.wait_ge(dn_used, n * 4 + 4)
                    dve.tensor_copy(ysb, psY[:, :]).then_inc(y_ready, 1)

            with dve.Fori(0, PAIRS) as it:
                pair_work(it)
            fullest = dve.value_load(cint[0:1, 0:1], min_val=0, max_val=T)
            with dve.If(fullest > CAP):
                with dve.Fori(1, ROUNDS) as rnd:
                    with dve.Fori(0, PAIRS) as pair:
                        pair_work(rnd * PAIRS + pair)
                dve.wait_ge(combined, 4 * E * ROUNDS)
            with dve.Else():
                dve.nop()

            dve.wait_ge(ln2_in, 32)
            for tt in range(TT):
                sums = [ps[2 * tt + i][:, :] for i in range(2)]
                for i in range(2):
                    dve.wait_ge(combined, 4 * (E - 1) + 2 * tt + i + 1)
                    half_stats(tt, i, sums[i])
                norm_rows(tt, out_ready, sums, ln2_rows[0], ln2_rows[1])

        @block.tensor
        def _(pe):
            pe.wait_ge(ident_in, 16)
            for tt in range(TT):
                for k in range(KD):
                    if k % 4 == 0:
                        pe.wait_ge(xhat_ready, 2 * tt + k // 4 + 1)
                    c = (k % 2) * 256 + tt * P
                    ins = pe.transpose(ps[4 + k // 2][:, c:c + P], h[:, tt, k * P:(k + 1) * P], ident)
                    if tt == TT - 1 and k % 2:
                        ins.then_inc(hT_psum, 1)

            def w_there(blk):
                return w_loaded[blk % 4], 32 * (blk // 4 + (blk % 4 > 0))

            def project(g, blk, nk, lhs, rhs):
                if g in (G_Q, G_K, G_V, G_GATE, G_GATE + 4, G_GATE + 8, G_GATE + 12, G_US, G_UA):
                    pe.wait_ge(*w_there(blk))
                if g >= 2:
                    pe.wait_ge(*group_read(g - 2))
                for k in range(nk):
                    if g == 0:
                        if k % 4 == 0:
                            pe.wait_ge(w_first[k // 4], 16)
                        pe.wait_ge(*((hT_act, hT_vec)[k // 2 % 2], 2 * (k // 4) + k % 2 + 1))
                    if g == G_US and k % 2 == 0:
                        pe.wait_ge(glu_ready, k // 2 + 1)
                    ins = pe.matmul(bank_of(g), lhs(k), rhs(k), start=(k == 0), stop=(k == nk - 1))
                ins.then_inc(proj_done, 1)

            def from_h(g0, blk, js=range(4)):
                wv = stream[blk % 4].rearrange("p (k n) -> p k n", k=KD)
                for j in js:
                    if g0 == G_V:
                        a, c = divmod(j, 2)
                        project(g0 + j, blk, KD, lambda k: hT[:, k, a * P:(a + 1) * P], lambda k: wv[:, k, c * 256:(c + 1) * 256])
                    else:
                        project(g0 + j, blk, KD, lambda k: wv[:, k, j * P:(j + 1) * P], lambda k: hT[:, k, :])

            def inputs_of_states(b, r):
                if r == 1:
                    pass
                elif b == 0:
                    pe.wait_ge(bt_ready, 2)
                    pe.wait_ge(proj_act, 4)
                else:
                    pe.wait_ge(bu_used, 8 * b)
                for i in range(4):
                    q = slice(32 * i, 32 * i + 32)
                    ins = pe.matmul(ps[2 + i][:, r * 256:r * 256 + 256],
                                    BT[q, r, b].rearrange("p m s -> p (m s)"), uT[q, b, :], start=True, stop=True)
                if r == 1:
                    ins.then_inc(bu_psum, 1)

            def outputs_of_states(b):
                pe.wait_ge(s_ready, b + 1)
                if b % 2:
                    pe.wait_ge(y_used, b)
                if b == 0:
                    pe.wait_ge(ct_ready, 1)
                for r, s in ((0, s_re), (1, s_im)):
                    for i in range(4):
                        ins = pe.matmul(ps[6 + b // 2][32 * i:32 * i + 32, (b % 2) * 256:(b % 2) * 256 + 256],
                                        CT[:, r, 4 * b + i, :], s[:, i, :], start=(r == 0), stop=(r == 1), skip_group_check=True)
                ins.then_inc(y_psum, 1)

            from_h(G_U, 0, [0, 1, 2, 3])
            from_h(G_Q, 1, [0])
            inputs_of_states(0, 0)
            from_h(G_Q, 1, [1])
            inputs_of_states(0, 1)
            from_h(G_Q, 1, [2, 3])
            inputs_of_states(1, 0)
            from_h(G_K, 2, [0])
            inputs_of_states(1, 1)
            from_h(G_K, 2, [1, 2, 3])
            outputs_of_states(0)
            from_h(G_V, 3, [0, 1, 2, 3])
            inputs_of_states(2, 0)
            from_h(G_GATE, 4, [0])
            inputs_of_states(2, 1)
            from_h(G_GATE, 4, [1, 2, 3])
            outputs_of_states(1)
            inputs_of_states(3, 0)
            from_h(G_GATE + 4, 5, [0])
            inputs_of_states(3, 1)
            from_h(G_GATE + 4, 5, [1, 2, 3])
            outputs_of_states(2)
            from_h(G_GATE + 8, 6, [0, 1, 2, 3])
            outputs_of_states(3)

            pe.wait_ge(bu_used, 32)
            def score(hd, q, nk, dst):
                c = slice(64 * (hd % 2), 64 * (hd % 2) + 64)
                return pe.matmul(dst, QT[c, hd // 2, q], KT[c, hd // 2, 0:nk], start=True, stop=True)

            for two in range(2):
                for hd in range(4 * two, 4 * two + 4):
                    c = hd // 2 % 2 * 256
                    ins = score(hd, slice(P, 2 * P), 256, ps[2 + 2 * two + hd % 2][:, c:c + 256])
                ins.then_inc(score_psum, 1)
            pe.wait_ge(y_used, 4)
            for hd in range(HEADS):
                ins = score(hd, slice(0, P), P, ps[6 + hd % 2][:, hd // 2 * P:hd // 2 * P + P])
            ins.then_inc(score_psum, 1)
            from_h(G_GATE + 12, 7)

            wg = stream[B_GLU % 4].rearrange("p (k n) -> p k n", k=KA)
            pe.wait_ge(*w_there(B_GLU))
            pe.wait_ge(gelu_ready, 1)
            for bank, c0 in ((4, AW), (2, 0)):
                for i in range(4):
                    for k in range(KA):
                        ins = pe.matmul(ps[bank + i // 2][:, (i % 2) * 256:(i % 2) * 256 + 256], wg[:, k, c0 + i * P:c0 + (i + 1) * P], uT[:, k, :],
                                        start=(k == 0), stop=(k == KA - 1), skip_group_check=True)
                    if i % 2:
                        ins.then_inc(glu_psum, 1)

            wu = stream[B_US % 4].rearrange("p (k n) -> p k n", k=KA)

            def up_ssm(n):
                project(G_US + n, B_US, KA, lambda k: wu[:, k, n * P:(n + 1) * P], lambda k: ssmT[:, k, :])

            for n in range(4):
                up_ssm(n)
            pe.wait_ge(p_norm, 2)
            for i in range(4):
                for hd in (2 * i, 2 * i + 1):
                    c = (hd % 2) * 256
                    pe.transpose(ps[2 + i][:, c:c + P], S0[:, hd, :], ident)
                    ins = pe.transpose(ps[2 + i][:, c + P:c + 2 * P], S1[:, hd, 0:P], ident)
                ins.then_inc(pt_psum, 1)
            for i in range(2):
                for hd in range(4 * i, 4 * i + 4):
                    ins = pe.transpose(ps[6 + i][:, (hd % 4) * P:(hd % 4) * P + P], S1[:, hd, P:2 * P], ident)
                ins.then_inc(pt_psum, 1)
            up_ssm(4)
            up_ssm(5)
            pe.wait_ge(pt_act, 3)
            pe.wait_ge(pt_vec, 3)
            for j in range(4):
                for hd in (2 * j, 2 * j + 1):
                    q = slice(64 * (hd % 2), 64 * (hd % 2) + 64)
                    o = ps[2 + j // 2][q, (j % 2) * 256:(j % 2) * 256 + 256]
                    pe.matmul(o, V[:, 0, hd * HD:(hd + 1) * HD], PT0[:, hd, :], start=True, stop=False, skip_group_check=True)
                    ins = pe.matmul(o[:, P:2 * P], V[:, 1, hd * HD:(hd + 1) * HD], PT1[:, hd, :], start=False, stop=True, skip_group_check=True)
                if j % 2:
                    ins.then_inc(pv_psum, 1)
            up_ssm(6)
            up_ssm(7)
            pe.wait_ge(attn_ready, 2)
            wa = stream[B_UA % 4].rearrange("p (k n) -> p k n", k=KA)
            for n in range(8):
                project(G_UA + n, B_UA, KA, lambda k: wa[:, k, n * P:(n + 1) * P], lambda k: attnT[:, k, :])

            def out_projection(tt, hf, ks=range(KD)):
                blk = B_WO + hf
                pe.wait_ge(*w_there(blk))
                wo = stream[blk % 4].rearrange("p (k n) -> p k n", k=KD)
                for k in ks:
                    if tt == 0 and hf == 0:
                        pe.wait_ge(mix_ready, k + 1)
                    ins = pe.matmul(ps[4 + 2 * tt + hf][:, :], mixT[:, k, tt * P:(tt + 1) * P], wo[:, k, :], start=(k == 0), stop=(k == KD - 1))
                if k == KD - 1:
                    ins.then_inc(wo_done, 1)

            def transpose_h1(tt):
                for k in range(KD):
                    if k % 4 == 0:
                        pe.wait_ge(ln1_done, 2 * tt + k // 4 + 1)
                    ins = pe.transpose(ps[2 * tt + k // 4][:, (k % 4) * P:(k % 4) * P + P], h[:, tt, k * P:(k + 1) * P], ident)
                    if k % 4 == 3:
                        ins.then_inc(h1T_psum, 1)

            def route(tt):
                for k in range(KD):
                    pe.wait_ge((h1T_vec, h1T_act)[k // 4], 4 * tt + k % 4 + 1)
                    ins = pe.matmul(ps[4 + tt][:, 0:E], h1T[:, k, tt * P:(tt + 1) * P], rw[:, k, :], start=(k == 0), stop=(k == KD - 1))
                ins.then_inc(logit_psum, 1)

            def start_sums(tt, halves=range(2)):
                pe.wait_ge(h1_ready, 2 + tt)
                if tt == 1:
                    pe.wait_ge(h1_vec, 1)
                for hf in halves:
                    pe.matmul(ps[2 * tt + hf][:, :], alpha_id, h[:, tt, hf * 512:(hf + 1) * 512], start=True, stop=False, skip_group_check=True)

            out_projection(0, 0)
            out_projection(0, 1)
            out_projection(1, 0)
            transpose_h1(0)
            out_projection(1, 1, range(4))
            pe.wait_ge(rw_in, 16)
            route(0)
            out_projection(1, 1, range(4, 6))
            pe.wait_ge(mask_ready, 1)
            pe.wait_ge(pad_ready, 1)
            pe.matmul(ps[6][:, 0:E], upper, mask[:, 0, :], start=True, stop=True, skip_group_check=True)
            pe.matmul(ps[6][:, E:2 * E], ones[:, :], mask[:, 0, :], start=True, stop=False, skip_group_check=True).then_inc(pos_psum, 1)
            out_projection(1, 1, range(6, KD))
            start_sums(0, [0])

            def gather(i, bank, tiles=range(TT)):
                for tt in tiles:
                    for k in range(4 * i, 4 * i + 4):
                        ins = pe.matmul(bank[:, (k % 4) * P:(k % 4) * P + P], h[:, tt, k * P:(k + 1) * P], Pm[:, tt, :],
                                        start=(tt == 0 and k % 4 == 0), stop=(tt == TT - 1), skip_group_check=True)
                if TT - 1 in tiles:
                    ins.then_inc(gather_psum, 1)

            pe.wait_ge(p_ready, 2)
            gather(0, psA, [0])
            transpose_h1(1)
            start_sums(0, [1])
            route(1)
            gather(1, psM, [0])
            pe.wait_ge(mask_ready, 2)
            pe.matmul(ps[6][:, E:2 * E], upper, mask[:, 1, :], start=False, stop=True, skip_group_check=True).then_inc(pos_psum, 1)
            start_sums(1, [0])
            for tt in range(TT):
                ins = pe.matmul(ps[5][:, 2 * E:3 * E], ones[:, :], mask[:, tt, :], start=(tt == 0), stop=(tt == TT - 1))
            ins.then_inc(count_psum, 1)
            pe.wait_ge(p_ready, 4)
            pe.wait_ge(h1_vec, 1)
            gather(0, psA, [1])
            pe.wait_ge(h1_ready, 3)
            gather(1, psM, [1])

            def transpose_gates():
                pe.wait_ge(gd_ready, TT)
                for tt in range(TT):
                    pe.transpose(psY[:, tt * P:(tt + 1) * P], Gd[:, tt, :], ident).then_inc(gdT_psum, 1)

            def bias_sums():
                pe.wait_ge(gdT_ready, 1)
                pe.wait_ge(bdn_in, 16)
                pe.wait_ge(bdn_zero, 2)
                for tt in range(TT):
                    for hf in range(2):
                        ins = pe.matmul(ps[2 * tt + hf][:, :], GdT[:, tt * P:(tt + 1) * P], bdn[:, hf * 512:(hf + 1) * 512],
                                        start=False, stop=False, skip_group_check=True)
                ins.then_inc(gdT_used, 1)

            pe.sem_inc(gu_done, 2)
            pe.sem_inc(gt_psum, 1)

            def combine(a, n):
                pe.wait_ge(y_ready, n + 1)
                pe.wait_ge(gt_ready, n + 1)
                for tt in range(TT):
                    for hf in range(2):
                        q = slice(64 * hf, 64 * hf + 64)
                        pe.matmul(ps[2 * tt + hf][:, :], GT[q, a, tt * P:(tt + 1) * P], ysb[q, :], start=False, stop=False, skip_group_check=True).then_inc(combined, 1)

            def pair_work(it, first=False):
                for a in range(2):
                    n = it * 2 + a
                    if a == 0:
                        pe.wait_ge(xt_ready, 1 if first else it * 2 + 2)
                    pe.wait_ge(ab_free, n + 1)
                    for i, k in enumerate(K_ORDER):
                        if first and a == 0 and i == 2:
                            pe.wait_ge(xt_ready, 2)
                        pe.wait_ge(gu_loaded[a][k], it * 16 + 16)
                        for q in range(4):
                            bank, hf = (psA, psB)[q // 2], q % 2
                            ins = pe.matmul(bank[64 * hf:64 * hf + 64, :], XT[:, k, CAP * a:CAP * a + CAP], gu_ring[:, a, k, q * 512:(q + 1) * 512],
                                            start=(i == 0), stop=False, skip_group_check=True)
                        ins.then_inc(gu_used, 1)
                    if first and a == 0:
                        transpose_gates()
                        pe.wait_ge(bgu_in, 16)
                    pe.wait_ge(sel_ready, n + 1)
                    for q in range(4):
                        bank, hf = (psA, psB)[q // 2], q % 2
                        ins = pe.matmul(bank[64 * hf:64 * hf + 64, :], sel4[a][:, q, :], bgu, start=False, stop=True, skip_group_check=True)
                    ins.then_inc(gu_done, 1)
                    if first and a == 0:
                        start_sums(1, [1])
                        bias_sums()
                    if a == 1:
                        pe.wait_ge(y_ready, n)
                    pe.wait_ge(pg_ready, n * 2 + 2)
                    for tt in range(TT):
                        ins = pe.transpose(psY[:, tt * P:(tt + 1) * P], PG[:, tt, :], ident)
                    ins.then_inc(gt_psum, 1)
                    if a == 1:
                        combine(0, n - 1)
                    if a == 0:
                        pe.wait_ge(p_ready, it * 4 + 8)
                        pe.wait_ge(xt_ready, it * 2 + 2)
                        gather(0, psM)
                    pe.wait_ge(act_ready, n + 1)
                    pe.wait_ge(gt_ready, n + 1)
                    for j in range(4):
                        ins = pe.transpose(psY[:, j * P:(j + 1) * P], xl[:, j * P:(j + 1) * P], ident)
                    ins.then_inc(at_psum, 1)
                    pe.wait_ge(at_ready, n + 1)
                    for i, j in enumerate(J_ORDER):
                        pe.wait_ge(dn_loaded[j], n * 16 + 16)
                        for k in (2 * j, 2 * j + 1):
                            for hf in range(2):
                                ins = pe.matmul(psY[64 * hf:64 * hf + 64, :], actT[:, k % 4, CAP * (k // 4):CAP * (k // 4) + CAP],
                                                dn_ring[:, k, hf * 512:(hf + 1) * 512], start=(i == 0 and k % 2 == 0), stop=(i == 3 and k % 2 == 1), skip_group_check=True)
                        ins.then_inc(dn_used, 1)
                    if a == 1:
                        gather(1, psA)
                        combine(1, n)

            pair_work(0, first=True)
            with pe.Fori(1, PAIRS) as it:
                pair_work(it)
            fullest = pe.value_load(cint[0:1, 0:1], min_val=0, max_val=T)
            with pe.If(fullest > CAP):
                with pe.Fori(1, ROUNDS) as rnd:
                    with pe.Fori(0, PAIRS) as pair:
                        pair_work(rnd * PAIRS + pair)
            with pe.Else():
                pe.nop()


def _consts():
    c = np.zeros((P, O_END), np.float32)
    c[:, O_ID:O_ID + 128] = np.eye(P)
    c[:, O_ALPHA:O_ALPHA + 128] = np.eye(P) * ALPHA
    c[:, O_UP:O_UP + 128] = np.triu(np.ones((P, P)), 1)
    c[:, O_SLOT:O_SLOT + 128] = np.tile(np.arange(CAP), 2)[None]
    c[:, O_TIME:O_TIME + 256] = np.arange(T)[None]
    c[np.arange(P), O_MASK + np.arange(P) // GS % 2] = 1
    return c


def kernel(**inputs):
    import concourse.bacc as bacc
    from concourse.bass_utils import run_bass_kernel_spmd

    a = {k: np.asarray(v) for k, v in inputs.items()}

    def by_partition(v):
        return v.reshape(-1, P).T

    def by_state(v):
        return v.reshape(ST, 2 * NST).T

    cols = np.concatenate([
        by_partition(a["ln_in_g"]), by_partition(a["ln_in_b"]), by_partition(a["b_gate"][0]), by_partition(a["ssm_d"][0]),
        by_state(a["lam_re"][0]), by_state(a["lam_im"][0]), by_state(np.repeat(a["log_dt"][0][:, None], NST, axis=1)),
        by_partition(a["ln1_g"][0]), by_partition(a["ln1_b"][0])], axis=1)
    b_l = [a[n][0].reshape(4, 8, NST, GS).transpose(1, 3, 0, 2).reshape(P, -1) for n in ("ssm_b_re", "ssm_b_im")]
    c_l = [a[n][0].reshape(ST, 2, GS, NST).transpose(1, 3, 0, 2).reshape(P, -1) for n in ("ssm_c_re", "ssm_c_im")]
    arrays = {
        "x": a["x"][0], "w_in": a["w_in"][0], "w_glu": a["w_glu"][0], "w_ua": a["w_up_attn"][0], "w_us": a["w_up_ssm"][0],
        "w_o": a["w_o"][0], "w_gu": a["w_gate_up"][0], "w_dn": a["w_down"][0], "rel_bias": a["rel_bias"][0],
        "router_w": a["router_w"][0], "router_b": a["router_b"],
        "cols": cols, "bc": np.concatenate(b_l + c_l, axis=1), "consts": _consts(),
        "lnrows": np.stack([a["ln_in_g"], a["ln_in_b"], a["ln1_g"][0], a["ln1_b"][0], a["ln2_g"][0], a["ln2_b"][0]]),
        "bgu": a["b_gate_up"][0].reshape(E, 4, 512).transpose(1, 0, 2).reshape(P, 512), "bdn": a["b_down"][0],
    }
    nc = bacc.Bacc("TRN2", target_bir_lowering=False, num_devices=1)
    ins, aps = {}, []
    for name, v in arrays.items():
        v = np.ascontiguousarray(v)
        ins[f"in_{name}_dram"] = v
        aps.append(nc.dram_tensor(f"in_{name}_dram", v.shape, mybir.dt.from_np(v.dtype), kind="ExternalInput").ap())
    aps.append(nc.dram_tensor("out_0_dram", (T, D), F32, kind="ExternalOutput").ap())
    trunk_and_moe(nc, *aps)
    r = run_bass_kernel_spmd(nc, [ins], core_ids=[0])
    return r.results[0]["out_0_dram"].reshape(1, T, D)
```
